# Optimizing a Trainium2 kernel written in Bass

```python
import jax, jax.numpy as jnp
from jax import lax
import numpy as np

D_MODEL = 2048
BATCH = 1
SEQ = 256
DEPTH = 2

GRID_W = 64
CTX_LEN = 256

D_A = 1024
RWKV_HEAD = 64
H_A = D_A // RWKV_HEAD
W_LORA = 64
A_LORA = 64
G_LORA = 128
LNX_EPS = 64e-5
D_B = 1024
HEAD_DIM = 128
H_Q = D_B // HEAD_DIM
H_KV = 2
Q_PER_KV = H_Q // H_KV
ROPE_AXIS_DIM = HEAD_DIM // 2
ROPE_THETA = 10000.0
Q_BLOCK = 128
RWKV_SPLITS = [D_A, 2 * D_A, 3 * D_A, 3 * D_A + W_LORA, 3 * D_A + W_LORA + A_LORA]
A_COLS = 3 * D_A + W_LORA + A_LORA + G_LORA
B_COLS = D_B + 2 * H_KV * HEAD_DIM
IN_COLS = A_COLS + B_COLS
D_MIX = D_A + D_B
FOURIER_GROUPS = 8
FOURIER_GROUP_DIM = D_MODEL // FOURIER_GROUPS
N_EXPERTS = 16
N_EXPERT_GROUPS = 4
EXPERTS_PER_GROUP = N_EXPERTS // N_EXPERT_GROUPS
TOP_K = 2
D_EXPERT = 512
N_EVEN = (DEPTH + 1) // 2
N_ODD = DEPTH // 2
NORM_EPS = 1e-6

kernel_name = 'hybrid_rwkv7_gqa_fnet_moe_dit'

def rms_norm(x, gain, eps=NORM_EPS):
    xf = x.astype(jnp.float32)
    y = xf * lax.rsqrt(jnp.mean(xf * xf, axis=-1, keepdims=True) + eps)
    return (y * gain.astype(jnp.float32)).astype(x.dtype)

def centred_shift(p, mu_prev, mu_next):
    zero = jnp.zeros_like(p[:, :1])
    prev = jnp.concatenate([zero, p[:, :-1]], axis=1)
    nxt = jnp.concatenate([p[:, 1:], zero], axis=1)
    return p + mu_prev * (prev - p) + mu_next * (nxt - p)

def axial_rope(n):
    rows = n // GRID_W
    row = jnp.repeat(jnp.arange(rows), GRID_W).astype(jnp.float32)
    col = jnp.tile(jnp.arange(GRID_W), rows).astype(jnp.float32)
    inv = ROPE_THETA ** (-jnp.arange(0, ROPE_AXIS_DIM, 2, dtype=jnp.float32) / ROPE_AXIS_DIM)
    ang = jnp.concatenate([row[:, None] * inv, col[:, None] * inv], axis=-1)
    return jnp.cos(ang), jnp.sin(ang)

def apply_rope(x, cos, sin):
    xf = x.astype(jnp.float32).reshape(x.shape[:-1] + (HEAD_DIM // 2, 2))
    x0, x1 = xf[..., 0], xf[..., 1]
    bshape = cos.shape[:1] + (1,) * (x.ndim - 3) + cos.shape[1:]
    c, s = cos.reshape(bshape), sin.reshape(bshape)
    out = jnp.stack([x0 * c - x1 * s, x0 * s + x1 * c], axis=-1)
    return out.reshape(x.shape).astype(x.dtype)

def wkv7_scan(s0, r, w, k, v, a, b, reverse):
    def step(s, inp):
        r_t, w_t, k_t, v_t, a_t, b_t = inp
        sa = jnp.einsum('bhij,bhj->bhi', s, a_t)
        s = s * w_t[:, :, None, :] + sa[..., None] * b_t[:, :, None, :] + v_t[..., None] * k_t[:, :, None, :]
        return s, jnp.einsum('bhij,bhj->bhi', s, r_t)
    xs = tuple(jnp.moveaxis(t, 1, 0) for t in (r, w, k, v, a, b))
    s_fin, ys = lax.scan(step, s0, xs, reverse=reverse)
    return s_fin, jnp.moveaxis(ys, 0, 1)

def rwkv7_streams(pa, w0, w2, a0, a2, g2, k_k, k_a):
    bsz, t = pa.shape[:2]
    heads = lambda z: z.astype(jnp.float32).reshape(bsz, t, H_A, RWKV_HEAD)
    r, k, v, xw, xa, xg = jnp.split(pa, RWKV_SPLITS, axis=-1)
    g = jax.nn.sigmoid(xg) @ g2
    kk = heads(k * k_k)
    kk = kk * lax.rsqrt(jnp.sum(kk * kk, axis=-1, keepdims=True) + 1e-12)
    dirs = []
    for d in range(2):
        w_log = -jax.nn.softplus(-(w0[d] + jnp.tanh(xw) @ w2[d])) - 0.5
        decay = jnp.exp(-jnp.exp(w_log.astype(jnp.float32)))
        a = jax.nn.sigmoid(a0[d] + xa @ a2[d])
        k_d = k * (1 + (a - 1) * k_a)
        dirs.append((heads(decay), heads(k_d), heads(a)))
    return heads(r), heads(v), kk, g, dirs

def rwkv7_finish(y, r, v, k_dirs, g, ln_g, ln_b, r_k):
    bsz, t = y.shape[:2]
    mu = jnp.mean(y, axis=-1, keepdims=True)
    var = jnp.mean(jnp.square(y - mu), axis=-1, keepdims=True)
    yn = ((y - mu) * lax.rsqrt(var + LNX_EPS)).reshape(bsz, t, D_A) * ln_g + ln_b
    kb = k_dirs[0] + k_dirs[1]
    bonus = (jnp.sum(r * kb * r_k, axis=-1, keepdims=True) * v).reshape(bsz, t, D_A)
    return ((yn + bonus) * g).astype(g.dtype)

def even_mixer(h_ctx, h_lat, w_in, mu_prev, mu_next, w0, w2, a0, a2, g2, k_k, k_a, r_k, ln_g, ln_b,
               q_gain, k_gain, w_out, cos, sin, ctx_out):
    p_ctx = h_ctx @ w_in
    p_lat = h_lat @ w_in
    pa_c = centred_shift(p_ctx[..., :A_COLS], mu_prev, mu_next)
    pa_l = centred_shift(p_lat[..., :A_COLS], mu_prev, mu_next)
    pb_c, pb_l = p_ctx[..., A_COLS:], p_lat[..., A_COLS:]

    rc, vc, kkc, gc, dc = rwkv7_streams(pa_c, w0, w2, a0, a2, g2, k_k, k_a)
    rl, vl, kkl, gl, dl = rwkv7_streams(pa_l, w0, w2, a0, a2, g2, k_k, k_a)
    s0 = jnp.zeros((h_lat.shape[0], H_A, RWKV_HEAD, RWKV_HEAD), jnp.float32)
    ys_c, ys_l = [], []
    for d, rev in enumerate((False, True)):
        dec_c, k_c, a_c = dc[d]
        dec_l, k_l, a_l = dl[d]
        s_c, y_c = wkv7_scan(s0, rc, dec_c, k_c, vc, -kkc, kkc * a_c, rev)
        _, y_l = wkv7_scan(s_c, rl, dec_l, k_l, vl, -kkl, kkl * a_l, rev)
        ys_c.append(y_c)
        ys_l.append(y_l)
    ya_l = rwkv7_finish(ys_l[0] + ys_l[1], rl, vl, [dl[0][1], dl[1][1]], gl, ln_g, ln_b, r_k)

    def qkv(pb):
        bsz, t = pb.shape[:2]
        q, k, v = jnp.split(pb, [D_B, D_B + H_KV * HEAD_DIM], axis=-1)
        q = rms_norm(q.reshape(bsz, t, H_KV, Q_PER_KV, HEAD_DIM), q_gain)
        k = rms_norm(k.reshape(bsz, t, H_KV, HEAD_DIM), k_gain)
        return q, k, v.reshape(bsz, t, H_KV, HEAD_DIM)
    qc, kc, vc_b = qkv(pb_c)
    ql, kl, vl_b = qkv(pb_l)
    ql = apply_rope(ql, cos, sin)
    kl = apply_rope(kl, cos, sin)
    k_all = jnp.concatenate([kc, kl], axis=1)
    v_all = jnp.concatenate([vc_b, vl_b], axis=1)
    scale = HEAD_DIM ** -0.5

    def attend(qb, keys, vals):
        s = jnp.einsum('bqkgd,bskd->bkgqs', qb, keys, preferred_element_type=jnp.float32) * scale
        p = jax.nn.softmax(s, axis=-1)
        return jnp.einsum('bkgqs,bskd->bqkgd', p.astype(vals.dtype), vals)

    bsz, seq = ql.shape[:2]
    nb = seq // Q_BLOCK
    qblocks = jnp.moveaxis(ql.reshape(bsz, nb, Q_BLOCK, H_KV, Q_PER_KV, HEAD_DIM), 1, 0)
    o_l = lax.map(lambda qb: attend(qb, k_all, v_all), qblocks)
    yb_l = jnp.moveaxis(o_l, 0, 1).reshape(bsz, seq, D_B)

    out_lat = jnp.concatenate([ya_l, yb_l.astype(ya_l.dtype)], axis=-1) @ w_out
    out_ctx = None
    if ctx_out:
        ya_c = rwkv7_finish(ys_c[0] + ys_c[1], rc, vc, [dc[0][1], dc[1][1]], gc, ln_g, ln_b, r_k)
        yb_c = attend(qc, kc, vc_b).reshape(bsz, qc.shape[1], D_B)
        out_ctx = jnp.concatenate([ya_c, yb_c.astype(ya_c.dtype)], axis=-1) @ w_out
    return out_lat, out_ctx

def fourier_mixer(h, w_out):
    bsz, t, _ = h.shape
    hg = h.astype(jnp.float32).reshape(bsz, t, FOURIER_GROUPS, FOURIER_GROUP_DIM)
    f = jnp.fft.fftn(hg, axes=(1, 3), norm='ortho').real
    return f.reshape(bsz, t, D_MODEL).astype(h.dtype) @ w_out

def route_grouped_top2(h, router_w, router_b):
    s = jax.nn.sigmoid((h @ router_w).astype(jnp.float32))
    sel = s + router_b.astype(jnp.float32)
    grp = sel.reshape(-1, N_EXPERT_GROUPS, EXPERTS_PER_GROUP)
    grp_score = jnp.sum(lax.top_k(grp, TOP_K)[0], axis=-1)
    best = jnp.argmax(grp_score, axis=-1)
    in_grp = jnp.repeat(best[:, None] == jnp.arange(N_EXPERT_GROUPS), EXPERTS_PER_GROUP, axis=-1)
    _, idx = lax.top_k(jnp.where(in_grp, sel, -jnp.inf), TOP_K)
    w = jnp.take_along_axis(s, idx, axis=-1)
    w = w / jnp.sum(w, axis=-1, keepdims=True)
    return jnp.sum(jax.nn.one_hot(idx, N_EXPERTS, dtype=jnp.float32) * w[..., None], axis=1)

def moe_ffn(h, router_w, router_b, w_gate, w_up, w_down):
    gates = route_grouped_top2(h, router_w, router_b).astype(h.dtype)
    out = jnp.zeros_like(h)
    for e in range(N_EXPERTS):
        u = jax.nn.silu(h @ w_gate[e]) * (h @ w_up[e])
        out = out + gates[:, e:e + 1] * (u @ w_down[e])
    return out

def setup_inputs(seed: int = 0) -> dict:
    key = jax.random.key(seed)
    ks = iter(list(jax.random.split(key, 40)))
    f32 = jnp.float32
    nrm = lambda shape, s: jax.random.normal(next(ks), shape, f32) * s
    uni = lambda shape: jax.random.uniform(next(ks), shape, f32, 0.0, 0.5)
    return {
        'x': nrm((BATCH, SEQ, D_MODEL), 1.0),
        'c': nrm((BATCH, D_MODEL), 1.0),
        'ctx': nrm((BATCH, CTX_LEN, D_MODEL), 1.0),
        'c_ctx': nrm((D_MODEL,), 1.0),
        'mod_w': nrm((DEPTH, D_MODEL, 6 * D_MODEL), 0.5 * D_MODEL ** -0.5),
        'mod_b': nrm((DEPTH, 6 * D_MODEL), 0.01),
        'norm_mix': 1.0 + nrm((DEPTH, D_MODEL), 0.02),
        'norm_ffn': 1.0 + nrm((DEPTH, D_MODEL), 0.02),
        'ab_w_in': nrm((N_EVEN, D_MODEL, IN_COLS), D_MODEL ** -0.5),
        'ab_mu_prev': uni((N_EVEN, A_COLS)),
        'ab_mu_next': uni((N_EVEN, A_COLS)),
        'rwkv_w0': nrm((N_EVEN, 2, D_A), 0.5),
        'rwkv_w2': nrm((N_EVEN, 2, W_LORA, D_A), 0.1),
        'rwkv_a0': nrm((N_EVEN, 2, D_A), 0.5),
        'rwkv_a2': nrm((N_EVEN, 2, A_LORA, D_A), A_LORA ** -0.5),
        'rwkv_g2': nrm((N_EVEN, G_LORA, D_A), G_LORA ** -0.5),
        'rwkv_k_k': 0.85 + nrm((N_EVEN, D_A), 0.02),
        'rwkv_k_a': 1.0 + nrm((N_EVEN, D_A), 0.02),
        'rwkv_r_k': nrm((N_EVEN, H_A, RWKV_HEAD), 0.1),
        'rwkv_ln_g': 1.0 + nrm((N_EVEN, D_A), 0.02),
        'rwkv_ln_b': nrm((N_EVEN, D_A), 0.01),
        'attn_q_norm': 1.0 + nrm((N_EVEN, HEAD_DIM), 0.02),
        'attn_k_norm': 1.0 + nrm((N_EVEN, HEAD_DIM), 0.02),
        'ab_w_out': nrm((N_EVEN, D_MIX, D_MODEL), D_MIX ** -0.5),
        'fourier_w_out': nrm((N_ODD, D_MODEL, D_MODEL), D_MODEL ** -0.5),
        'router_w': nrm((D_MODEL, N_EXPERTS), D_MODEL ** -0.5),
        'router_b': nrm((N_EXPERTS,), 0.01),
        'exp_w_gate': nrm((DEPTH, N_EXPERTS, D_MODEL, D_EXPERT), D_MODEL ** -0.5),
        'exp_w_up': nrm((DEPTH, N_EXPERTS, D_MODEL, D_EXPERT), D_MODEL ** -0.5),
        'exp_w_down': nrm((DEPTH, N_EXPERTS, D_EXPERT, D_MODEL), D_EXPERT ** -0.5),
    }

def reference(x, c, ctx, c_ctx, mod_w, mod_b, norm_mix, norm_ffn, ab_w_in, ab_mu_prev, ab_mu_next,
              rwkv_w0, rwkv_w2, rwkv_a0, rwkv_a2, rwkv_g2, rwkv_k_k, rwkv_k_a, rwkv_r_k, rwkv_ln_g, rwkv_ln_b,
              attn_q_norm, attn_k_norm, ab_w_out, fourier_w_out, router_w, router_b,
              exp_w_gate, exp_w_up, exp_w_down):
    seq = x.shape[1]
    cos, sin = axial_rope(seq)
    s_lat = jax.nn.silu(c)
    s_ctx = jax.nn.silu(c_ctx)
    for l in range(DEPTH):
        ctx_out = any(j % 2 == 0 for j in range(l + 1, DEPTH))
        uses_ctx = (l % 2 == 0) or ctx_out
        m_lat = (s_lat @ mod_w[l] + mod_b[l])[:, None, :]
        sh1, sc1, gt1, sh2, sc2, gt2 = jnp.split(m_lat, 6, axis=-1)
        h_lat = rms_norm(x, norm_mix[l]) * (1 + sc1) + sh1
        if uses_ctx:
            m_ctx = s_ctx @ mod_w[l] + mod_b[l]
            csh1, csc1, cgt1, csh2, csc2, cgt2 = jnp.split(m_ctx, 6)
            h_ctx = rms_norm(ctx, norm_mix[l]) * (1 + csc1) + csh1
        if l % 2 == 0:
            e = l // 2
            y_lat, y_ctx = even_mixer(h_ctx, h_lat, ab_w_in[e], ab_mu_prev[e], ab_mu_next[e],
                                      rwkv_w0[e], rwkv_w2[e], rwkv_a0[e], rwkv_a2[e], rwkv_g2[e],
                                      rwkv_k_k[e], rwkv_k_a[e], rwkv_r_k[e], rwkv_ln_g[e], rwkv_ln_b[e],
                                      attn_q_norm[e], attn_k_norm[e], ab_w_out[e], cos, sin, ctx_out)
        else:
            o = l // 2
            y_lat = fourier_mixer(h_lat, fourier_w_out[o])
            y_ctx = fourier_mixer(h_ctx, fourier_w_out[o]) if ctx_out else None
        x = x + gt1 * y_lat
        tokens = (rms_norm(x, norm_ffn[l]) * (1 + sc2) + sh2).reshape(-1, D_MODEL)
        if ctx_out:
            ctx = ctx + cgt1 * y_ctx
            h2c = rms_norm(ctx, norm_ffn[l]) * (1 + csc2) + csh2
            tokens = jnp.concatenate([tokens, h2c.reshape(-1, D_MODEL)], axis=0)
        f = moe_ffn(tokens, router_w, router_b, exp_w_gate[l], exp_w_up[l], exp_w_down[l])
        n_lat = x.shape[0] * seq
        x = x + gt2 * f[:n_lat].reshape(x.shape)
        if ctx_out:
            ctx = ctx + cgt2 * f[n_lat:].reshape(ctx.shape)
    return x


_drawn_inputs = setup_inputs


def setup_inputs(seed=0):
    import zlib

    import numpy as np

    out = dict(_drawn_inputs(seed))
    spreads = {}
    factors = {'norm_mix': 2.799,
     'rwkv_k_k': 47.536,
     'rwkv_k_a': 3.404,
     'rwkv_ln_g': 32.627,
     'rwkv_ln_b': 49.408,
     'attn_q_norm': 8.0,
     'attn_k_norm': 8.0,
     'norm_ffn': 3.694,
     'router_b': 2.954}
    for name, (base, spread) in spreads.items():
        noise = np.random.default_rng([zlib.crc32(name.encode()), seed]).standard_normal(out[name].shape)
        drawn = base * np.exp(spread * noise) if base else spread * noise
        out[name] = __import__('jax').numpy.asarray(drawn.astype(out[name].dtype))
    for name, factor in factors.items():
        out[name] = (out[name] * factor).astype(out[name].dtype)
    return out
```

```python
from contextlib import ExitStack

import numpy as np

import concourse.bass as bass
from concourse import mybir

F32 = mybir.dt.float32
ALU = mybir.AluOpType
ACT = mybir.ActivationFunctionType
AX = mybir.AxisListType

P = 128
D = 2048
KT = D // P
T = 256
T2 = 2 * T
NB = 512
MOD_BLOCKS = 6 * D // NB
MOD_FIRST = 2 * D // NB
HP = 1024 // P
C = 64
A_TILES = 26
NH = 8
HD = 128
NCH = T2 // C
SLOT = KT * P
W_RING = 3
SLOTS = 8
LAYERS = 2
E = 16
CAP = 64
FF = 512
M_RING = 4
NORM_EPS = 1e-6
LNX_EPS = 64e-5
CREDIT = 1
DECAY = float(np.exp(-0.5))

TILE_ORDER = ([24, 25] + [t for hp in range(HP) for t in (hp, 8 + hp, 16 + hp)]
              + [34, 35, 36, 37] + list(range(26, 34)))
W0, A0, K_K, K_A, R_K, LN_G, LN_B = 0, 2, 4, 5, 6, 7, 8
N_PAR = 9

G_LEN = 2 * (4 * C + 4 * 2 * C)
BK_LEN = NCH * P
AR_LEN = NCH * 2 * C
DIR_LEN = G_LEN + BK_LEN + AR_LEN + NCH
V_AT = 2 * DIR_LEN
BONUS_AT = V_AT + 4 * P
GATE_AT = BONUS_AT + T
REC_LEN = GATE_AT + T


def g_at(head, c):
    base = head * (G_LEN // 2)
    return (base + c * C, C) if c < 4 else (base + 4 * C + (c - 4) * 2 * C, 2 * C)


class Count:

    def __init__(self, eng, sem):
        self.eng, self.sem, self.n, self.i, self.k, self.first = eng, sem, 0, None, 0, 0

    def loop(self, i, k, first=0):
        self.i, self.k, self.first, self.start = i, k, first, self.n

    def end(self, iterations):
        assert self.n - self.start == self.k, (self.n - self.start, self.k)
        self.n, self.i = self.start + self.k * iterations, None

    def inc(self, ins):
        ins.then_inc(self.sem, 1)
        self.n += 1

    def wait(self, back=0):
        v = self.n - back
        wait(self.eng, self.sem, v if self.i is None else self.i * self.k + (v - self.first * self.k))


def wait(eng, sem, value):
    if not (isinstance(value, int) and value <= 0):
        eng.wait_ge(sem, value)


class Builder:
    def __init__(self, nc, dram):
        self.nc, self.d = nc, dram
        self.keep = ExitStack()
        self.staged = []

    def sem(self, name):
        return self.nc.alloc_semaphore(name)

    def stage_sem(self, name):
        self.staged.append(self.nc.alloc_semaphore(name))
        return self.staged[-1]

    def end_stage(self):
        self.nc.clear_and_free_semaphores(self.staged)
        self.staged = []
        self.nc.all_engine_barrier()

    def sb(self, name, shape, stack=None):
        return (stack or self.keep).enter_context(self.nc.sbuf_tensor(name, shape, F32))

    def ps(self, name, shape, stack):
        return stack.enter_context(self.nc.psum_tensor(name, shape, F32))


def build_mix_in(b):
    nc, d = b.nc, b.d
    st = ExitStack()
    S = b.stage_sem
    ident, blk, hT, par = b.ident, b.blk, b.hT, b.par
    wring, mring, stage = b.sb("wring", [P, W_RING, SLOT], st), b.mring, b.stage
    sq = b.sb("sq_mix", [P, 2, T2], st)
    mload = b.sb("mload", [32, 2, 5, P], st)
    shc = b.sb("shc", [P, 2, KT], st)
    scc = b.sb("scc", [P, 2, KT], st)
    lora = b.sb("lora", [P, 2, T2], st)
    rkv = b.sb("rkv", [P, 3, T2], st)
    mu = b.sb("mu", [P, 3, 26], st)
    cur = b.sb("cur_cols", [P, 8], st)
    lw = b.sb("lora_w", [P, 3, P], st)
    mask = b.sb("mask", [P, 2, 2 * C], st)
    restart = b.sb("restart", [P, T2], st)
    tw = b.sb("tw", [P, 2, T2], st)
    ta = b.sb("ta", [P, 2, T2], st)
    cum = b.sb("cum", [P, T2], st)
    ep = b.sb("ep", [P, T2], st)
    en = b.sb("en", [P, T2], st)
    ex = b.sb("ex", [P, T2], st)
    kkr = b.sb("kkr", [P, T2], st)
    kk = b.sb("kk", [P, T2], st)
    kd = b.sb("kd", [P, 2, T2], st)
    rkb = b.sb("rkb", [P, T], st)
    both = b.mixT[:].rearrange("p k t -> p (k t)").rearrange("p (w d c n) -> p w d c n", w=2, d=2, n=2 * C)
    kb, kbp = both[:, 0], both[:, 1]
    rec = b.sb("rec", [P, REC_LEN], st)
    p_in = b.ps("p_in", [P, 2, NB], st)
    p_mod = b.ps("p_mod", [P, 2, NB], st)
    p_lo = b.ps("p_lo", [P, 2, NB], st)
    p_g = b.ps("p_g", [P, 2, NB], st)

    cond_in, x_in, small_in = S("cond_in"), S("x_in"), S("small_in")
    consts_ready, silu_ready, par_ready = S("consts_ready"), S("silu_ready"), S("par_ready")
    mod_full, mod_used, mod_evac, mod_stored = b.mod_full, b.mod_used, b.mod_evac, b.mod_stored
    w_full = [S(f"w_full{i}") for i in range(W_RING)]
    sq_ready, sq_used, rms_ready, rstd_ready, hr_ready = (
        S("sq_ready"), S("sq_used"), S("rms_ready"), S("rstd_ready"), S("hr_ready"))
    mload_in, mcol_ready, mcol_evac = S("mload_in"), S("mcol_ready"), S("mcol_evac")
    h_ctx, h_lat = S("h_ctx_ready"), S("h_lat_ready")
    in_ready, in_scaled, in_evac = S("in_ready"), S("in_scaled"), S("in_evac")
    cur_ready = S("cur_ready")
    lora_ready, lw_in = S("lora_ready"), S("lora_w_in")
    z_ready, z_used = S("z_ready"), S("z_used")
    kks_ready, rkb_ready = S("kks_ready"), S("rkb_ready")
    cum_ready, x_ready, e_ready = S("cum_ready"), S("x_ready"), S("e_ready")
    kb_ready, kbp_ready = S("kb_ready"), S("kbp_ready")
    g_ready, g_evac, t_ready, t_evac = S("g_ready"), S("g_evac"), S("t_ready"), S("t_evac")
    pair_read = S("pair_read")
    rec_stored, tri_stored = S("rec_stored"), S("tri_stored")
    own_dve, own_pool = S("own_dve_in"), S("own_pool_in")

    def chunks(ap):
        return ap.rearrange("p (c t) -> p c t", t=C)

    with nc.Block() as block:
        @block.sync
        def _(sp):
            def mod_load(m):
                for q in range(4):
                    wait(sp, mod_used, m * 4 + q - 3)
                    sp.dma_start(mring[:, q, :], d["mod_w"][bass.ds(m, 1), q][0]).then_inc(mod_full[q], 16)

            def w_load(t, slot):
                wait(sp, in_ready, t - 2)
                sp.dma_start(wring[:, slot, :], d["w_in"][bass.ds(t, 1)][0]).then_inc(w_full[slot], 16)

            mod_load(0)
            with sp.Fori(1, MOD_FIRST) as m:
                mod_load(m)
            for t in range(5):
                w_load(t, t % 3)

            def pair(hp, last):
                for j in range(3):
                    mod_load(hp * 4 + (MOD_FIRST + j))
                    if not last:
                        w_load(hp * 3 + (5 + j), (2 + j) % 3)
                mod_load(hp * 4 + (MOD_FIRST + 3))

            with sp.Fori(0, HP - 1) as hp:
                pair(hp, False)
            pair(HP - 1, True)

        @block.gpsimd
        def _(pool):
            own = Count(pool, own_pool)

            def link(ins):
                own.inc(ins)
                own.wait()

            link(pool.memset(ident[:], 0.0))
            link(pool.memset(blk[:], 0.0))
            link(pool.memset(restart[:], 1.0))
            link(pool.memset(mask[:], 1.0))
            link(pool.memset(b.ones[:], 1.0))
            link(pool.memset(b.eps[:, 0:1], NORM_EPS))
            link(pool.memset(b.eps[:, 1:2], 1e-12))
            link(pool.memset(b.eps[:, 2:3], LNX_EPS))
            link(pool.memset(blk[0:C, 0:C], 1.0))
            link(pool.memset(blk[C:P, C:P], 1.0))
            link(pool.memset(chunks(restart[:])[:, :, 0:1], 0.0))
            for half in range(2):
                rows = slice(half * C, half * C + C)
                for dr in range(2):
                    sign = 1 if dr == 0 else -1
                    for incl in range(2):
                        part = mask[rows, dr, incl * C:incl * C + C]
                        link(pool.affine_select(out=part, in_=part, compare_op=ALU.is_ge, fill=0.0,
                                                   base=incl - 1, pattern=[[sign, C]],
                                                   channel_multiplier=-sign))
            link(pool.affine_select(out=ident[:], in_=ident[:], compare_op=ALU.not_equal, fill=1.0,
                                       base=0, pattern=[[-1, P]], channel_multiplier=1))
            pool.sem_inc(consts_ready, 1)

            def mod_store(m, buf):
                pool.wait_ge(mod_evac, m + 1)
                for row in range(2):
                    pool.dma_start(d["modp"][row, :, bass.ds(m * NB, NB)], stage[row:P:32, buf, :]
                                   ).then_inc(mod_stored[buf], 16)

            with pool.Fori(0, MOD_FIRST, 2) as m:
                mod_store(m, 0)
                mod_store(m + 1, 1)
            for q in range(2):
                pool.wait_ge(mod_stored[q], 16 * MOD_FIRST)
            for row in range(2):
                pool.dma_start(mload[:, row, 0:4, :],
                               d["modp"][row, :, 0:32 * P].rearrange("g (j p) -> j g p", p=P)
                               ).then_inc(mload_in, 16)
                pool.dma_start(mload[:, row, 4, :], d["mod_b"][0, 0:32, :]).then_inc(mload_in, 16)

            def lora_weights(hp):
                wait(pool, z_ready, hp * 6 - 1)
                pool.dma_start(lw[:], d["lora_w"][bass.ds(hp, 1)][0]).then_inc(lw_in, 16)

            def record_out(hp):
                pool.wait_ge(g_evac, hp * 5 + 5)
                pool.wait_ge(t_evac, hp * 3 + 3)
                pool.wait_ge(z_used, hp * 6 + 5)
                for dr in range(2):
                    for head in range(2):
                        for lat in range(2):
                            base, n = g_at(head, 4 * lat)
                            for odd in range(2):
                                rows = slice(0, C) if odd else slice(C, P)
                                src = rec[rows, dr * DIR_LEN + base:dr * DIR_LEN + base + 4 * n]
                                src = src.rearrange("p (c e t) -> p e c t", e=2, t=n)[:, odd, :, 0:C]
                                dst = d["tri"][dr, bass.ds(hp, 1), head, 2 * lat:2 * lat + 2, odd]
                                pool.dma_start(dst.rearrange("o c s t -> s (o c) t"), src
                                               ).then_inc(tri_stored, 16)
                pool.dma_start(d["rec"][bass.ds(hp, 1)][0], rec[:]).then_inc(rec_stored, 16)

            def pair(hp, first=False):
                lora_weights(hp)
                mod_store(hp * 4 + MOD_FIRST, 0)
                mod_store(hp * 4 + (MOD_FIRST + 1), 1)
                if not first:
                    record_out(hp - 1)
                    pool.wait_ge(rec_stored, hp * 16)
                    pool.wait_ge(tri_stored, hp * 256)
                mod_store(hp * 4 + (MOD_FIRST + 2), 0)
                for dr in range(2):
                    pool.wait_ge(kb_ready, hp * 2 + (dr + 1))
                    last = C - 1 if dr == 0 else 0
                    total = chunks(ep[:])[:, :, last:last + 1]
                    pool.tensor_tensor(kbp[:, dr], kb[:, dr], total.broadcast_to([P, NCH, 2 * C]), ALU.mult)
                    pool.tensor_copy(rec[:, dr * DIR_LEN + DIR_LEN - NCH:dr * DIR_LEN + DIR_LEN],
                                     total.rearrange("p c o -> p (c o)")).then_inc(kbp_ready, 1)
                mod_store(hp * 4 + (MOD_FIRST + 3), 1)

            pair(0, True)
            with pool.Fori(1, HP) as hp:
                pair(hp)
            record_out(HP - 1)
            pool.wait_ge(rec_stored, 16 * HP)
            pool.wait_ge(tri_stored, 256 * HP)
            for q in range(2):
                pool.wait_ge(mod_stored[q], 16 * (MOD_FIRST + 4 * HP))

        @block.tensor
        def _(pe):
            def mod_block(m, q4):
                wait(pe, mod_evac, m - 1)
                for q in range(4):
                    pe.wait_ge(mod_full[q], m * 16 + 16)
                    for g in range(4):
                        mm = pe.matmul(p_mod[32 * g:32 * g + 32, q4, :], b.scol[:, 4 * q + g, :],
                                       mring[:, q, g * NB:(g + 1) * NB], start=q == 0, stop=q == 3)
                    mm.then_inc(mod_used, 1)

            pe.wait_ge(consts_ready, 1)
            for k in range(KT):
                pe.wait_ge(sq_ready, k + 1)
                pe.matmul(p_in[:, 0, :], b.ones[:], sq[:, k % 2, :], start=k == 0, stop=k == KT - 1
                          ).then_inc(sq_used, 1)
            pe.wait_ge(silu_ready, 1)
            mod_block(0, 0)
            mod_block(1, 1)
            with pe.Fori(2, MOD_FIRST, 2) as m:
                mod_block(m, 0)
                mod_block(m + 1, 1)
            pe.wait_ge(mload_in, 64)
            for row in range(2):
                for part in range(5):
                    mm = pe.matmul(p_lo[:, 0, row * 32:row * 32 + 32], mload[:, row, part, :],
                                   ident[0:32, 0:32], start=part == 0, stop=part == 4)
            mm.then_inc(mcol_ready, 1)

            def tile(slot, full, bank, first=False):
                pe.wait_ge(w_full[slot], full)
                for k in range(KT):
                    if first:
                        pe.wait_ge(h_ctx, k + 1)
                        pe.wait_ge(h_lat, k + 1)
                    mm = pe.matmul(p_in[:, bank, :], wring[:, slot, k * P:(k + 1) * P], hT[:, k, :],
                                   start=k == 0, stop=k == KT - 1)
                mm.then_inc(in_ready, 1)

            tile(0, 16, 0, first=True)
            tile(1, 16, 1)

            def low_rank(hp):
                n = 6
                pe.wait_ge(lw_in, hp * 16 + 16)
                pe.wait_ge(lora_ready, 2)
                for dr in range(2):
                    wait(pe, z_used, hp * n + (dr - 1))
                    pe.matmul(p_lo[:, dr, :], lw[0:C, dr, :], lora[0:C, 0, :], start=True, stop=True
                              ).then_inc(z_ready, 1)
                for dr in range(2):
                    wait(pe, z_used, hp * n + (dr + 1))
                    pe.matmul(p_lo[:, dr, :], lw[C:P, dr, :], lora[C:P, 0, :], start=True, stop=True
                              ).then_inc(z_ready, 1)
                pe.wait_ge(z_used, hp * n + 3)
                pe.matmul(p_lo[:, 0, 0:T], lw[:, 2, :], lora[:, 1, T:T2], start=True, stop=True
                          ).then_inc(z_ready, 1)
                pe.wait_ge(z_used, hp * n + 4)
                pe.wait_ge(kks_ready, hp + 1)
                pe.matmul(p_lo[:, 1, :], blk[:], sq[:, 0, :], start=True, stop=True).then_inc(z_ready, 1)

            def chunk_matrices(hp):
                def flip(dr):
                    pe.wait_ge(kbp_ready, hp * 2 + (dr + 1))
                    for c in range(NCH):
                        mm = pe.transpose(p_g[:, c // 4, (c % 4) * P:(c % 4 + 1) * P], kbp[:, dr, c, :], ident[:])
                    mm.then_inc(t_ready, 1)

                def products(dr, lat):
                    ar = rec[:, dr * DIR_LEN + G_LEN + BK_LEN:dr * DIR_LEN + DIR_LEN - NCH]
                    ar = ar.rearrange("p (c n) -> p c n", n=2 * C)
                    n = 2 * C if lat else C
                    for c in range(4):
                        for head in range(2):
                            rows = slice(head * C, head * C + C)
                            mm = pe.matmul(p_g[:, head, c * n:(c + 1) * n], kb[rows, dr, 4 * lat + c, :],
                                           ar[rows, 4 * lat + c, 0:n], start=True, stop=True)
                    mm.then_inc(g_ready, 1)

                wait(pe, g_evac, hp * 5)
                wait(pe, t_evac, hp * 3)
                for dr in range(2):
                    if dr:
                        pe.wait_ge(g_evac, hp * 5 + 2)
                    flip(dr)
                    pe.wait_ge(t_evac, hp * 3 + (dr + 1))
                    products(dr, 0)
                    pe.wait_ge(g_evac, hp * 5 + (2 * dr + 1))
                    products(dr, 1)
                pe.wait_ge(g_evac, hp * 5 + 4)
                for i in range(4):
                    mm = pe.transpose(p_g[:, 0, i * P:(i + 1) * P], rkv[:, 2, i * P:(i + 1) * P], ident[:])
                mm.then_inc(t_ready, 1)
                pe.wait_ge(rkb_ready, hp + 1)
                pe.matmul(p_g[:, 1, 0:T], blk[:], rkb[:], start=True, stop=True).then_inc(g_ready, 1)

            def pair(hp, first=False):
                pe.wait_ge(in_evac, hp * 3 + 2)
                tile(2, hp * 16 + 16, 0)
                mod_block(hp * 4 + MOD_FIRST, 0)
                tile(0, hp * 16 + 32, 1)
                mod_block(hp * 4 + (MOD_FIRST + 1), 1)
                if not first:
                    chunk_matrices(hp - 1)
                pe.wait_ge(in_evac, hp * 3 + 3)
                tile(1, hp * 16 + 32, 0)
                mod_block(hp * 4 + (MOD_FIRST + 2), 0)
                low_rank(hp)
                mod_block(hp * 4 + (MOD_FIRST + 3), 1)

            pair(0, True)
            with pe.Fori(1, HP) as hp:
                pair(hp)
            chunk_matrices(HP - 1)

        @block.scalar
        def _(act):
            act.dma_start(b.cond[:], d["cond"]).then_inc(cond_in, 16)
            for g in range(4):
                kt = slice(4 * g, 4 * g + 4)
                act.dma_start(hT[:, kt, 0:T], d["ctxT"][:, kt, :]).then_inc(x_in, 16)
                act.dma_start(hT[:, kt, T:T2], d["xT"][:, kt, :]).then_inc(x_in, 16)
            act.dma_start(mu[:, 0:2, :], d["mu"]).then_inc(small_in, 16)
            act.dma_start(par[:, 0:N_PAR, :], d["par"]).then_inc(small_in, 16)
            act.dma_start(b.gain[:], d["gain"]).then_inc(small_in, 16)
            act.wait_ge(cond_in, 16)
            act.wait_ge(par_ready, 1)
            act.activation(b.scol[:, :, 0:2], b.cond[:], ACT.Silu).then_inc(silu_ready, 1)
            act.wait_ge(x_in, 16 * 8)
            for k in range(KT):
                wait(act, sq_used, k - 1)
                act.activation(sq[:, k % 2, :], hT[:, k, :], ACT.Square).then_inc(sq_ready, 1)
            act.wait_ge(sq_used, KT)
            act.activation(sq[:, 0, :], p_in[:, 0, :], ACT.Sqrt, scale=1.0 / D, bias=b.eps[:, 0:1]
                           ).then_inc(rms_ready, 1)

            def mod_evacuate(m, buf):
                act.wait_ge(mod_used, m * 4 + 4)
                wait(act, mod_stored[buf], (m - buf) * 16)
                act.activation(stage[:, buf, :], p_mod[:, buf, :], ACT.Copy).then_inc(mod_evac, 1)

            mod_evacuate(0, 0)
            mod_evacuate(1, 1)
            with act.Fori(2, MOD_FIRST, 2) as m:
                mod_evacuate(m, 0)
                mod_evacuate(m + 1, 1)
            act.wait_ge(mcol_evac, 1)
            for k in range(KT):
                act.wait_ge(hr_ready, k + 1)
                act.activation(hT[:, k, 0:T], hT[:, k, 0:T], ACT.Identity, bias=shc[:, 1, k:k + 1],
                               scale=scc[:, 1, k:k + 1]).then_inc(h_ctx, 1)

            def scaled(bank, ready, mu_col, out):
                act.wait_ge(in_ready, ready)
                act.activation(out, p_in[:, bank, :], ACT.Copy, scale=mu_col).then_inc(in_scaled, 1)

            scaled(0, 1, mu[:, 2, 0:1], lora[:, 0, :])
            scaled(1, 2, mu[:, 2, 1:2], lora[:, 1, :])
            act.wait_ge(in_evac, 2)
            act.activation(lora[0:C, 0, :], lora[0:C, 0, :], ACT.Tanh).then_inc(lora_ready, 1)
            act.activation(lora[:, 1, T:T2], lora[:, 1, T:T2], ACT.Sigmoid).then_inc(lora_ready, 1)

            def flipped(hp, dr):
                act.wait_ge(t_ready, hp * 3 + (dr + 1))
                at = dr * DIR_LEN + G_LEN
                act.activation(rec[:, at:at + NB], p_g[:, 0, :], ACT.Copy)
                act.activation(rec[:, at + NB:at + 2 * NB], p_g[:, 1, :], ACT.Copy).then_inc(t_evac, 1)

            def tail(hp):
                flipped(hp, 0)
                flipped(hp, 1)
                act.wait_ge(t_ready, hp * 3 + 3)
                act.activation(rec[:, V_AT:V_AT + 4 * P], p_g[:, 0, :], ACT.Copy).then_inc(t_evac, 1)

            def pair(hp, first=False):
                mod_evacuate(hp * 4 + MOD_FIRST, 0)
                mod_evacuate(hp * 4 + (MOD_FIRST + 1), 1)
                if not first:
                    tail(hp - 1)
                    act.wait_ge(pair_read, hp)
                act.wait_ge(cur_ready, hp + 1)
                for j in range(3):
                    scaled([0, 1, 0][j], hp * 3 + (3 + j), cur[:, j:j + 1], rkv[:, j, :])
                    if j == 1:
                        act.wait_ge(in_evac, hp * 3 + 4)
                        kcol = cur[:, 7:8]
                        act.activation(kkr[:], rkv[:, 1, :], ACT.Copy, scale=kcol)
                        wait(act, z_ready, hp * 6)
                        act.activation(sq[:, 0, :], rkv[:, 1, :], ACT.Square, scale=kcol).then_inc(kks_ready, 1)
                mod_evacuate(hp * 4 + (MOD_FIRST + 2), 0)
                for dr in range(2):
                    act.wait_ge(z_ready, hp * 6 + (dr + 1))
                    act.activation(tw[:, dr, :], p_lo[:, dr, :], ACT.Tanh, scale=0.5,
                                   bias=cur[:, 3 + dr:4 + dr]).then_inc(z_used, 1)
                for dr in range(2):
                    act.wait_ge(z_ready, hp * 6 + (dr + 3))
                    act.activation(ta[:, dr, :], p_lo[:, dr, :], ACT.Tanh, scale=0.5,
                                   bias=cur[:, 5 + dr:6 + dr]).then_inc(z_used, 1)
                act.wait_ge(z_ready, hp * 6 + 5)
                if not first:
                    act.wait_ge(rec_stored, hp * 16)
                act.activation(rec[:, GATE_AT:GATE_AT + T], p_lo[:, 0, 0:T], ACT.Copy).then_inc(z_used, 1)
                act.wait_ge(z_ready, hp * 6 + 6)
                act.activation(ex[:], p_lo[:, 1, :], ACT.Sqrt, bias=b.eps[:, 1:2]).then_inc(z_used, 1)
                for dr in range(2):
                    act.wait_ge(cum_ready, hp * 2 + (dr + 1))
                    wait(act, kbp_ready, hp * 2 + dr)
                    act.activation(ep[:], cum[:], ACT.Exp)
                    act.activation(en[:], cum[:], ACT.Exp, scale=-1.0)
                    act.wait_ge(x_ready, hp * 2 + (dr + 1))
                    act.activation(ex[:], ex[:], ACT.Exp).then_inc(e_ready, 1)
                mod_evacuate(hp * 4 + (MOD_FIRST + 3), 1)

            pair(0, True)
            with act.Fori(1, HP) as hp:
                pair(hp)
            tail(HP - 1)

        @block.vector
        def _(dve):
            own = Count(dve, own_dve)

            def link(ins):
                own.inc(ins)
                own.wait()

            link(dve.memset(b.scol[:], 0.0))
            dve.sem_inc(par_ready, 1)
            dve.wait_ge(small_in, 48)
            link(dve.tensor_tensor(mu[:, 2, :], mu[:, 0, :], mu[:, 1, :], ALU.add))
            link(dve.tensor_scalar(mu[:, 2, :], mu[:, 2, :], -1.0, 1.0, ALU.mult, ALU.add))
            link(dve.tensor_scalar(par[:, N_PAR:N_PAR + 4, :], par[:, 0:4, :], 0.5, None, ALU.mult))
            link(dve.tensor_scalar(par[:, N_PAR + 4, :], par[:, K_A, :], 0.5, None, ALU.mult))
            link(dve.tensor_scalar(par[:, N_PAR + 5, :], par[:, K_A, :], -0.5, 1.0, ALU.mult, ALU.add))
            dve.wait_ge(rms_ready, 1)
            dve.reciprocal(sq[:, 1, :], sq[:, 0, :]).then_inc(rstd_ready, 1)
            dve.wait_ge(rstd_ready, 1)
            for k in range(KT):
                dve.tensor_tensor(hT[:, k, :], hT[:, k, :], sq[:, 1, :], ALU.mult).then_inc(hr_ready, 1)
            dve.wait_ge(mcol_ready, 1)
            mod = p_lo[:, 0, 0:64].rearrange("p (r n) -> p r n", n=32)
            dve.tensor_copy(shc[:], mod[:, :, 0:KT])
            for row in range(2):
                own.inc(dve.scalar_tensor_tensor(scc[:, row, :], mod[:, row, KT:2 * KT], 1.0, b.gain[:, 0, :],
                                                 ALU.add, ALU.mult))
            own.wait()
            dve.sem_inc(mcol_evac, 1)
            dve.wait_ge(hr_ready, KT)
            for k in range(KT):
                dve.tensor_scalar(hT[:, k, T:T2], hT[:, k, T:T2], scc[:, 0, k:k + 1], shc[:, 0, k:k + 1],
                                  ALU.mult, ALU.add).then_inc(h_lat, 1)

            def shift(bank, scaled, prev, nxt, out):
                dve.wait_ge(in_scaled, scaled)
                o = out.rearrange("p (s t) -> p s t", t=T)
                p = p_in[:, bank, :].rearrange("p (s t) -> p s t", t=T)
                link(dve.scalar_tensor_tensor(o[:, :, 1:T], p[:, :, 0:T - 1], prev, o[:, :, 1:T],
                                              ALU.mult, ALU.add))
                dve.scalar_tensor_tensor(o[:, :, 0:T - 1], p[:, :, 1:T], nxt, o[:, :, 0:T - 1],
                                         ALU.mult, ALU.add).then_inc(in_evac, 1)

            for j in range(2):
                shift(j, j + 1, mu[:, 0, j:j + 1], mu[:, 1, j:j + 1], lora[:, j, :])

            def tail(hp):
                for dr in range(2):
                    for lat in range(2):
                        dve.wait_ge(g_ready, hp * 5 + (2 * dr + lat + 1))
                        for head in range(2):
                            base, n = g_at(head, 4 * lat)
                            out = rec[:, dr * DIR_LEN + base:dr * DIR_LEN + base + 4 * n]
                            m = mask[:, dr:dr + 1, 0:n].broadcast_to([P, 4, n])
                            ins = dve.tensor_tensor(out.rearrange("p (c n) -> p c n", n=n),
                                                    p_g[:, head, 0:4 * n].rearrange("p (c n) -> p c n", n=n),
                                                    m, ALU.mult)
                        ins.then_inc(g_evac, 1)
                dve.wait_ge(g_ready, hp * 5 + 5)
                ins = dve.tensor_tensor(rec[:, BONUS_AT:BONUS_AT + T], p_g[:, 1, 0:T], rkv[:, 2, T:T2], ALU.mult)
                own.inc(ins)
                own.wait()
                dve.sem_inc(g_evac, 1)
                dve.sem_inc(pair_read, 1)

            def pair(hp, first=False):
                dve.tensor_copy(cur[:, 0:3], mu[:, 2, bass.ds(hp * 3 + 2, 3)])
                dve.tensor_copy(cur[:, 3:7], par[:, N_PAR:N_PAR + 4, bass.ds(hp, 1)].rearrange("p n o -> p (n o)"))
                dve.tensor_copy(cur[:, 7:8], par[:, K_K, bass.ds(hp, 1)]).then_inc(cur_ready, 1)
                if not first:
                    tail(hp - 1)
                for j in range(3):
                    cols = bass.ds(hp * 3 + (2 + j), 1)
                    shift([0, 1, 0][j], hp * 3 + (3 + j), mu[:, 0, cols], mu[:, 1, cols], rkv[:, j, :])
                dve.wait_ge(in_evac, hp * 3 + 5)
                r, k, v = rkv[:, 0, :], rkv[:, 1, :], rkv[:, 2, :]
                for dr in range(2):
                    dve.wait_ge(z_used, hp * 6 + (dr + 3))
                    own.inc(dve.tensor_scalar(tw[:, dr, :], tw[:, dr, :], -DECAY / 2, -DECAY / 2, ALU.mult, ALU.add))
                    own.inc(dve.tensor_scalar(kd[:, dr, :], ta[:, dr, :], par[:, N_PAR + 4, bass.ds(hp, 1)],
                                              par[:, N_PAR + 5, bass.ds(hp, 1)], ALU.mult, ALU.add))
                    own.wait()
                    own.inc(dve.tensor_tensor(kd[:, dr, :], kd[:, dr, :], k, ALU.mult))
                    own.inc(dve.tensor_scalar(ta[:, dr, :], ta[:, dr, :], 0.5, 0.5, ALU.mult, ALU.add))
                dve.wait_ge(z_used, hp * 6 + 6)
                link(dve.reciprocal(ex[:], ex[:]))
                link(dve.tensor_tensor(kk[:], kkr[:], ex[:], ALU.mult))
                for dr in range(2):
                    fwd = slice(None) if dr == 0 else slice(None, None, -1)
                    if dr:
                        dve.wait_ge(e_ready, hp * 2 + 1)
                    own.inc(dve.tensor_tensor_scan(cum[:, fwd], restart[:], tw[:, dr, fwd], 0.0, ALU.mult, ALU.add))
                    own.wait()
                    dve.sem_inc(cum_ready, 1)
                    own.inc(dve.tensor_tensor(ex[:], cum[:], tw[:, dr, :], ALU.subtract))
                    own.wait()
                    dve.sem_inc(x_ready, 1)
                    link(dve.tensor_tensor(ta[:, dr, :], kk[:], ta[:, dr, :], ALU.mult))
                    dve.wait_ge(e_ready, hp * 2 + (dr + 1))
                    wait(dve, t_ready, hp * 3)
                    quads = kb[:, dr].rearrange("p (c e) (h t) -> p c (e h) t", e=2, h=2)
                    en4 = en[:].rearrange("p (c e t) -> p c e t", e=2, t=C)
                    kd4 = kd[:, dr, :].rearrange("p (c e t) -> p c e t", e=2, t=C)
                    b4 = ta[:, dr, :].rearrange("p (c e t) -> p c e t", e=2, t=C)
                    own.inc(dve.tensor_tensor(quads[:, :, 0:4:3, :], kd4, en4, ALU.mult))
                    own.inc(dve.tensor_tensor(quads[:, :, 1:3, :], b4, en4, ALU.mult))
                    if dr == 0 and not first:
                        dve.wait_ge(rec_stored, hp * 16)
                        dve.wait_ge(tri_stored, hp * 256)
                    ar = rec[:, dr * DIR_LEN + G_LEN + BK_LEN:dr * DIR_LEN + DIR_LEN - NCH]
                    ar = ar.rearrange("p (c n) -> p c n", n=2 * C)
                    own.inc(dve.scalar_tensor_tensor(ar[:, :, 0:C], chunks(kk[:]), -1.0, chunks(ex[:]),
                                                     ALU.mult, ALU.mult))
                    own.inc(dve.tensor_tensor(ar[:, 0:4, C:2 * C], chunks(r)[:, 0:4, :], chunks(ep[:])[:, 0:4, :], ALU.mult))
                    own.inc(dve.tensor_tensor(ar[:, 4:8, C:2 * C], chunks(r)[:, 4:8, :], chunks(ep[:])[:, 4:8, :], ALU.mult))
                    own.wait()
                    dve.sem_inc(kb_ready, 1)
                link(dve.tensor_tensor(rkb[:], kd[:, 0, T:T2], kd[:, 1, T:T2], ALU.add))
                own.inc(dve.scalar_tensor_tensor(rkb[:], rkb[:], par[:, R_K, bass.ds(hp, 1)], r[:, T:T2],
                                                 ALU.mult, ALU.mult))
                own.wait()
                dve.sem_inc(rkb_ready, 1)

            before = own.n
            pair(0, True)
            k_first = own.n - before
            with dve.Fori(1, HP) as hp:
                own.loop(hp, k_first + 1, 1)
                pair(hp)
            own.end(HP - 1)
            tail(HP - 1)
    st.close()
    b.end_stage()


def build_attend(b):
    nc, d = b.nc, b.d
    st = ExitStack()
    S = b.stage_sem
    ident, hT, mring, stage = b.ident, b.hT, b.mring, b.stage
    mixT = b.mixT
    wring = b.sb("wring_at", [P, W_RING, SLOT], st)
    kv = b.sb("kv", [P, 4, T2], st)
    q = b.sb("q", [P, NH, T], st)
    qsq = b.sb("qsq", [P, NH, T], st)
    rsq = b.sb("rsq", [P, 2, T2], st)
    rope = b.sb("rope", [P, 2, T], st)
    rot = b.sb("rot", [P, P], st)
    hgain = b.sb("hgain", [P, 2], st)
    part = b.sb("rope_part", [P, 2, T], st)
    vt = b.sb("vt", [P, 2, 4, P], st)
    prob = b.sb("prob", [P, 2, T2], st)
    probT = b.sb("probT", [P, 2, 4, T], st)
    smax = b.sb("smax", [P, 16], st)
    ssum = b.sb("ssum", [P, 16], st)
    tri = [b.sb(f"tri{dr}", [P, C, C], st) for dr in range(2)]
    outer = [b.sb(f"outer{dr}", [P, C * C // 4], st) for dr in range(2)]
    p_in = b.ps("p_in_at", [P, 2, NB], st)
    p_mod = b.ps("p_mod_at", [P, 2, NB], st)
    p_b = b.ps("p_b", [P, 2, NB], st)

    small_in = S("at_small_in")
    w_full = [S(f"at_w_full{i}") for i in range(W_RING)]
    tile_ready, tile_evac = S("at_tile_ready"), S("at_tile_evac")
    mod_full, mod_used, mod_evac = b.mod_full, b.mod_used, b.mod_evac
    mod_stored = [S(f"at_mod_stored{i}") for i in range(2)]
    ssq_ready, rms_ready, normed = S("at_ssq_ready"), S("at_rms_ready"), S("at_normed")
    rot_ready, roped = S("rot_ready"), S("roped")
    vt_ready, vt_evac = S("vt_ready"), S("vt_evac")
    sc_ready, max_ready, exp_ready, prob_ready = (
        S("scores_ready"), S("max_ready"), S("exp_ready"), S("prob_ready"))
    pt_ready, pt_evac, av_ready, av_evac = S("pt_ready"), S("pt_evac"), S("av_ready"), S("av_evac")
    tri_in, inv_fwd, inv_bwd, inv_stored = S("tri_in"), S("inv_fwd"), S("inv_bwd"), S("inv_stored")
    own_dve, own_pool = S("own_dve_at"), S("own_pool_at")
    FIRST = MOD_FIRST + 4 * HP
    LEFT = 2 * MOD_BLOCKS - FIRST
    SCALE = float(HD) ** -0.5

    def invert(eng, dr, sem):
        y = tri[dr]
        n = 0
        for s in range(1, C - 1):
            s = s if dr == 0 else C - 1 - s
            js = slice(0, s) if dr == 0 else slice(s + 1, C)
            ts = slice(s + 1, C) if dr == 0 else slice(0, s)
            nj, nt = js.stop - js.start, ts.stop - ts.start
            o = outer[dr][:, 0:nj * nt].rearrange("p (j t) -> p j t", t=nt)
            eng.tensor_tensor(o, y[:, js, s:s + 1].broadcast_to([P, nj, nt]),
                              y[:, s:s + 1, ts].broadcast_to([P, nj, nt]), ALU.mult).then_inc(sem, 1)
            eng.wait_ge(sem, n + 1)
            eng.tensor_tensor(y[:, js, ts], y[:, js, ts], o, ALU.add).then_inc(sem, 1)
            eng.wait_ge(sem, n + 2)
            n += 2
        eng.memset(y[:].rearrange("p s t -> p (s t)")[:, 0:C * C:C + 1], 1.0).then_inc(sem, 1)
        return n + 1

    INV = 2 * (C - 2) + 1

    with nc.Block() as block:
        @block.sync
        def _(sp):
            def w_load(n):
                wait(sp, tile_ready, n - 2)
                sp.dma_start(wring[:, n % 3, :], d["w_in"][A_TILES + n]).then_inc(w_full[n % 3], 16)

            for n in range(3):
                w_load(n)
            for dr in range(2):
                sp.dma_start(tri[dr][:].rearrange("p s t -> p (s t)"),
                             d["tri"][dr].rearrange("hp h k e s t -> (hp h k e) (s t)")).then_inc(tri_in, 16)
            for n in range(LEFT):
                m = FIRST + n
                for q4 in range(4):
                    sp.wait_ge(mod_used, 4 * m + q4 - 3)
                    sp.dma_start(mring[:, q4, :], d["mod_w"][m, q4]).then_inc(mod_full[q4], 16)
                if n + 3 < 12:
                    w_load(n + 3)
            for n in range(LEFT + 3, 12):
                w_load(n)
            for dr, sem in ((0, inv_fwd), (1, inv_bwd)):
                sp.wait_ge(sem, INV)
                sp.dma_start(d["inv"][dr].rearrange("hp h k e s t -> (hp h k e) (s t)"),
                             tri[dr][:].rearrange("p s t -> p (s t)")).then_inc(inv_stored, 16)
            sp.wait_ge(inv_stored, 32)

        @block.gpsimd
        def _(pool):
            pool.dma_start(rope[:], d["rope"]).then_inc(small_in, 16)
            pool.dma_start(rot[:], d["rot"]).then_inc(small_in, 16)
            pool.dma_start(hgain[:], d["hgain"]).then_inc(small_in, 16)
            pool.wait_ge(tri_in, 32)
            y = invert(pool, 1, inv_bwd)
            assert y == INV

        @block.tensor
        def _(pe):
            def mod_block(n):
                m = FIRST + n
                pe.wait_ge(mod_evac, m - 1)
                for q4 in range(4):
                    pe.wait_ge(mod_full[q4], 16 * (m + 1))
                    for g in range(4):
                        mm = pe.matmul(p_mod[32 * g:32 * g + 32, n % 2, :], b.scol[:, 4 * q4 + g, :],
                                       mring[:, q4, g * NB:(g + 1) * NB], start=q4 == 0, stop=q4 == 3)
                    mm.then_inc(mod_used, 1)

            for n in range(12):
                pe.wait_ge(w_full[n % 3], 16 * (n // 3 + 1))
                wait(pe, tile_evac, n - 1)
                cols = slice(0, T2) if n < 4 else slice(T, T2)
                for k in range(KT):
                    mm = pe.matmul(p_in[:, n % 2, 0:cols.stop - cols.start], wring[:, n % 3, k * P:(k + 1) * P],
                                   hT[:, k, cols], start=k == 0, stop=k == KT - 1)
                mm.then_inc(tile_ready, 1)
                if n < LEFT:
                    mod_block(n)
                if n in (4, 5):
                    g = n - 4
                    for i in range(4):
                        mm = pe.transpose(p_b[:, g, i * P:(i + 1) * P], kv[:, 2 + g, i * P:(i + 1) * P], ident[:])
                    mm.then_inc(vt_ready, 1)
            for n in range(6):
                if n < 2:
                    pe.wait_ge(vt_evac, n + 1)
                else:
                    pe.wait_ge(rms_ready, n - 1)
                if n == 0:
                    pe.wait_ge(tile_evac, 12)
                rhs = qsq[:, 2 * n:2 * n + 2, :] if n < 4 else b.ksq[:, n - 4, :]
                pe.matmul(p_b[:, n % 2, :], b.ones[:], rhs, start=True, stop=True).then_inc(ssq_ready, 1)
            pe.wait_ge(small_in, 48)
            for n in range(5):
                pe.wait_ge(rms_ready, 6)
                pe.wait_ge(normed, n + 1 if n < 4 else 6)
                wait(pe, roped, n - 1)
                rhs = q[:, 2 * n:2 * n + 2, :] if n < 4 else kv[:, 0:2, T:T2]
                pe.matmul(p_b[:, n % 2, :], rot[:], rhs, start=True, stop=True).then_inc(rot_ready, 1)
            pe.wait_ge(roped, 5)

            def scores(i):
                head, qt = i // 2, i % 2
                wait(pe, exp_ready, i - 1)
                pe.matmul(p_in[:, i % 2, :], q[:, head, qt * P:(qt + 1) * P], kv[:, head // 4, :],
                          start=True, stop=True).then_inc(sc_ready, 1)

            scores(0)
            for i in range(16):
                head, qt = i // 2, i % 2
                if i + 1 < 16:
                    scores(i + 1)
                pe.wait_ge(prob_ready, i + 1)
                wait(pe, pt_evac, i - 1)
                if i < 2:
                    pe.wait_ge(mod_evac, 2 * MOD_BLOCKS)
                for kc in range(4):
                    mm = pe.transpose(p_mod[:, i % 2, kc * P:(kc + 1) * P], prob[:, i % 2, kc * P:(kc + 1) * P], ident[:])
                mm.then_inc(pt_ready, 1)
                if qt:
                    pe.wait_ge(pt_evac, i + 1)
                    wait(pe, av_evac, head - 1)
                    for kc in range(4):
                        mm = pe.matmul(p_b[:, head % 2, 0:T], vt[:, head // 4, kc, :], probT[:, head % 2, kc, :],
                                       start=kc == 0, stop=kc == 3)
                    mm.then_inc(av_ready, 1)

        @block.scalar
        def _(act):
            for n in range(12):
                act.wait_ge(tile_ready, n + 1)
                if n < 4:
                    ins = act.activation(kv[:, n, :], p_in[:, n % 2, :], ACT.Copy)
                    if n < 2:
                        ins = act.activation(b.ksq[:, n, :], p_in[:, n % 2, :], ACT.Square)
                else:
                    act.activation(q[:, n - 4, :], p_in[:, n % 2, 0:T], ACT.Copy)
                    ins = act.activation(qsq[:, n - 4, :], p_in[:, n % 2, 0:T], ACT.Square)
                ins.then_inc(tile_evac, 1)
                if n < LEFT:
                    m = FIRST + n
                    act.wait_ge(mod_used, 4 * m + 4)
                    wait(act, mod_stored[n % 2], 32 * (n // 2))
                    act.activation(stage[:, n % 2, :], p_mod[:, n % 2, :], ACT.Copy).then_inc(mod_evac, 1)
                    act.wait_ge(mod_evac, m + 1)
                    for row in range(2):
                        act.dma_start(d["modp"][row, :, m * NB:(m + 1) * NB], stage[row:P:32, n % 2, :]
                                      ).then_inc(mod_stored[n % 2], 16)
                if n in (5, 6):
                    g = n - 5
                    act.wait_ge(vt_ready, g + 1)
                    act.activation(vt[:, g, :, :].rearrange("p k n -> p (k n)"), p_b[:, g, :], ACT.Copy
                                   ).then_inc(vt_evac, 1)
            for n in range(6):
                act.wait_ge(ssq_ready, n + 1)
                wait(act, normed, n - 1)
                act.activation(rsq[:, n % 2, :], p_b[:, n % 2, :], ACT.Sqrt, scale=1.0 / HD, bias=b.eps[:, 0:1]
                               ).then_inc(rms_ready, 1)
            for q2 in range(2):
                act.wait_ge(mod_stored[q2], 16 * LEFT)
            for i in range(16):
                head, qt = i // 2, i % 2
                act.wait_ge(max_ready, i + 1)
                wait(act, pt_ready, i - 1)
                act.activation(prob[:, i % 2, :], p_in[:, i % 2, :], ACT.Exp, scale=SCALE, bias=smax[:, i:i + 1],
                               accum_out=ssum[:, i:i + 1]).then_inc(exp_ready, 1)
                if qt:
                    for j in (i - 1, i):
                        act.wait_ge(pt_ready, j + 1)
                        wait(act, av_ready, head - 1)
                        act.activation(probT[:, head % 2, :, (j % 2) * P:(j % 2 + 1) * P],
                                       p_mod[:, j % 2, :].rearrange("p (k t) -> p k t", t=P), ACT.Copy
                                       ).then_inc(pt_evac, 1)
                    act.wait_ge(av_ready, head + 1)
                    act.activation(mixT[:, HP + head, :], p_b[:, head % 2, 0:T], ACT.Copy).then_inc(av_evac, 1)

        @block.vector
        def _(dve):
            own = Count(dve, own_dve)

            def link(ins):
                own.inc(ins)
                own.wait()

            dve.wait_ge(tri_in, 32)
            invert(dve, 0, inv_fwd)
            dve.wait_ge(small_in, 48)
            for n in range(6):
                dve.wait_ge(rms_ready, n + 1)
                link(dve.reciprocal(rsq[:, n % 2, :], rsq[:, n % 2, :]))
                x = q[:, 2 * n:2 * n + 2, :].rearrange("p h t -> p (h t)") if n < 4 else kv[:, n - 4, :]
                dve.scalar_tensor_tensor(x, x, hgain[:, n // 4:n // 4 + 1], rsq[:, n % 2, :],
                                         ALU.mult, ALU.mult).then_inc(normed, 1)
            dve.wait_ge(normed, 6)
            cos = rope[:, 0:1, :].broadcast_to([P, 2, T])
            sin = rope[:, 1:2, :].broadcast_to([P, 2, T])
            for n in range(5):
                x = q[:, 2 * n:2 * n + 2, :] if n < 4 else kv[:, 0:2, T:T2]
                dve.wait_ge(rot_ready, n + 1)
                own.inc(dve.tensor_tensor(part[:], p_b[:, n % 2, :].rearrange("p (h t) -> p h t", t=T), sin, ALU.mult))
                own.inc(dve.tensor_tensor(x, x, cos, ALU.mult))
                own.wait()
                own.inc(dve.tensor_tensor(x, x, part[:], ALU.add))
                own.wait()
                dve.sem_inc(roped, 1)
            for i in range(16 + 1):
                if i < 16:
                    dve.wait_ge(sc_ready, i + 1)
                    link(dve.tensor_reduce(smax[:, i:i + 1], p_in[:, i % 2, :], AX.X, ALU.max))
                    own.inc(dve.tensor_scalar(smax[:, i:i + 1], smax[:, i:i + 1], -SCALE, None, ALU.mult))
                    own.wait()
                    dve.sem_inc(max_ready, 1)
                if i:
                    j = i - 1
                    dve.wait_ge(exp_ready, j + 1)
                    link(dve.reciprocal(ssum[:, j:j + 1], ssum[:, j:j + 1]))
                    dve.tensor_scalar(prob[:, j % 2, :], prob[:, j % 2, :], ssum[:, j:j + 1], None, ALU.mult
                                      ).then_inc(prob_ready, 1)
    st.close()
    b.end_stage()


def build_recur(b):
    nc, d = b.nc, b.d
    st = ExitStack()
    S = b.stage_sem
    y = b.y
    CUT = BONUS_AT
    rec = b.sb("rec_rc", [P, 2, 2, CUT], st)
    inv = b.sb("inv_rc", [P, 2, 2, 2, 2, 4, C], st)
    akv = b.sb("akv", [P, 2, 2, 2, 4, C], st)
    H = b.sb("state", [P, 2, 2, 2, C], st)
    W = b.sb("w_rc", [P, 2, 2, C], st)
    UV = b.sb("uv", [P, 2, 2, 2, 2 * C], st)
    p_c = [b.ps(f"p_chain{g}", [P, 2, NB], st) for g in range(2)]
    p_y = [b.ps(f"p_y{g}", [P, 2, NB], st) for g in range(2)]

    rec_in = [[S(f"rec_in{s}{g}") for g in range(2)] for s in range(2)]
    ak_ready, ak_evac = ([S(f"{n}{g}") for g in range(2)] for n in ("ak_ready", "ak_evac"))
    w_ready, w_evac = ([S(f"{n}{g}") for g in range(2)] for n in ("rc_w_ready", "rc_w_evac"))
    u_ready, u_evac = ([S(f"{n}{g}") for g in range(2)] for n in ("rc_u_ready", "rc_u_evac"))
    v_placed = [S(f"v_placed{g}") for g in range(2)]
    hy_ready = [S(f"hy_ready{g}") for g in range(2)]
    h_done = [S(f"h_done{g}") for g in range(2)]
    y_evac = [S(f"y_evac{g}") for g in range(2)]

    def chunk(i, dr):
        return i if dr == 0 else (3 - i if i < 4 else 11 - i)

    def half(c, u=True):
        return slice(C, P) if (c % 2 == 0) == u else slice(0, C)

    def g_cols(s, g, dr, head, c, lat_part):
        base, n = g_at(head, c)
        base += dr * DIR_LEN + (C if lat_part else 0)
        return rec[:, s, g, base:base + C]

    def ar_cols(s, g, dr, c, lat_part):
        base = dr * DIR_LEN + G_LEN + BK_LEN + c * 2 * C + (C if lat_part else 0)
        return rec[:, s, g, base:base + C]

    with nc.Block() as block:
        @block.sync
        def _(sp):
            def load(n, s, g):
                hp = n * 4 + (2 * s + g)
                wait(sp, h_done[g], (n * 2 + s - 1) * 9)
                wait(sp, hy_ready[g], (n * 2 + s - 1) * 8)
                sp.dma_start(rec[:, s, g, :], d["rec"][bass.ds(hp, 1)][0][:, 0:CUT]).then_inc(rec_in[s][g], 16)
                for dr in range(2):
                    for odd in range(2):
                        rows = half(odd)
                        sp.dma_start(inv[rows, s, g, dr].rearrange("s h k t -> s (h k) t"),
                                     d["inv"][dr, bass.ds(hp, 1), :, :, odd].rearrange("o h k s t -> s (o h k) t")
                                     ).then_inc(rec_in[s][g], 16)

            for s in range(2):
                for g in range(2):
                    load(0, s, g)
            for s in range(2):
                for g in range(2):
                    sp.wait_ge(h_done[g], (s + 1) * 9)
                    load(1, s, g)

        @block.gpsimd
        def _(pool):
            def place(n, s, i, g):
                cnt = n * 16 + (8 * s + i)
                pool.wait_ge(rec_in[s][g], n * 80 + 80)
                wait(pool, hy_ready[g], cnt - 1)
                for dr in range(2):
                    c = chunk(i, dr)
                    rows = half(c, u=False)
                    v = rec[rows, s, g, V_AT + (c // 2) * P:V_AT + (c // 2 + 1) * P]
                    ins = pool.tensor_copy(UV[rows, g, i % 2, dr, :], v)
                ins.then_inc(v_placed[g], 1)

            def steps(n):
                for s in range(2):
                    for i in range(8):
                        for g in range(2):
                            place(n, s, i, g)

            for n in range(2):
                steps(n)

        @block.tensor
        def _(pe):
            def outer_values(n, s, g):
                pe.wait_ge(rec_in[s][g], n * 80 + 80)
                for dr in range(2):
                    wait(pe, y_evac[g], (n * 2 + s) * 4)
                    wait(pe, ak_evac[g], (n * 2 + s) * 2 + dr)
                    for head in range(2):
                        for k in range(4):
                            for odd in range(2):
                                c = 2 * k + odd
                                vr, ur = half(c, False), half(c)
                                mm = pe.matmul(p_y[g][ur, odd, (head * 4 + k) * C:(head * 4 + k + 1) * C],
                                               g_cols(s, g, dr, head, c, False)[vr],
                                               rec[vr, s, g, V_AT + k * P + head * C:V_AT + k * P + (head + 1) * C],
                                               start=True, stop=True)
                    mm.then_inc(ak_ready[g], 1)

            def form_w(n, s, i, g):
                pe.wait_ge(h_done[g], (n * 2 + s) * 9 + (i + 1))
                for dr in range(2):
                    c = chunk(i, dr)
                    for head in range(2):
                        rows = slice(head * C, head * C + C)
                        mm = pe.matmul(p_c[g][half(c), head, 0:C], ar_cols(s, g, dr, c, False)[rows],
                                       H[rows, g, i % 2, dr, :], start=True, stop=True)
                mm.then_inc(w_ready[g], 1)

            def form_u(n, s, i, g):
                pe.wait_ge(w_evac[g], n * 16 + (8 * s + i + 1))
                for dr in range(2):
                    c = chunk(i, dr)
                    rows = half(c)
                    for head in range(2):
                        mm = pe.matmul(p_c[g][rows, rows.start // C, head * C:(head + 1) * C],
                                       inv[rows, s, g, dr, head, c // 2, :], W[rows, g, head, :],
                                       start=True, stop=True)
                mm.then_inc(u_ready[g], 1)

            def form_state(n, s, i, g):
                pe.wait_ge(u_evac[g], n * 16 + (8 * s + i + 1))
                pe.wait_ge(v_placed[g], n * 16 + (8 * s + i + 1))
                if i > 4:
                    pe.wait_ge(y_evac[g], (n * 2 + s) * 4 + (i - 4))
                for dr in range(2):
                    c = chunk(i, dr)
                    for head in range(2):
                        rows = slice(head * C, head * C + C)
                        bk = dr * DIR_LEN + G_LEN + c * P + head * C
                        mm = pe.matmul(p_c[g][rows, 0, dr * C:(dr + 1) * C], rec[:, s, g, bk:bk + C],
                                       UV[:, g, i % 2, dr, rows], start=True, stop=True)
                if i >= 4:
                    for dr in range(2):
                        c = chunk(i, dr)
                        for head in range(2):
                            rows = slice(head * C, head * C + C)
                            out = p_y[g][rows, head, dr * C:(dr + 1) * C]
                            pe.matmul(out, UV[:, g, i % 2, dr, rows], g_cols(s, g, dr, head, c, True),
                                      start=True, stop=False)
                            mm = pe.matmul(out, H[rows, g, i % 2, dr, :], ar_cols(s, g, dr, c, True)[rows],
                                           start=False, stop=True)
                mm.then_inc(hy_ready[g], 1)

            for n in range(2):
                for s in range(2):
                    for g in range(2):
                        outer_values(n, s, g)
                    for i in range(8):
                        for f in (form_w, form_u, form_state):
                            for g in range(2):
                                f(n, s, i, g)

        @block.scalar
        def _(act):
            for n in range(2):
                for s in range(2):
                    for g in range(2):
                        for dr in range(2):
                            act.wait_ge(ak_ready[g], (n * 2 + s) * 2 + dr + 1)
                            for odd in range(2):
                                rows = half(odd)
                                ins = act.activation(akv[rows, g, dr].rearrange("p h k t -> p (h k t)"),
                                                     p_y[g][rows, odd, :], ACT.Copy)
                            ins.then_inc(ak_evac[g], 1)
                    for i in range(8):
                        for g in range(2):
                            act.wait_ge(u_ready[g], n * 16 + (8 * s + i + 1))
                            for dr in range(2):
                                rows = half(chunk(i, dr))
                                ins = act.activation(UV[rows, g, i % 2, dr, :],
                                                     p_c[g][rows, rows.start // C, 0:2 * C], ACT.Copy)
                            ins.then_inc(u_evac[g], 1)

        @block.vector
        def _(dve):
            for n in range(2):
                for s in range(2):
                    for g in range(2):
                        wait(dve, h_done[g], (n * 2 + s) * 9)
                        dve.memset(H[:, g, 0], 0.0).then_inc(h_done[g], 1)
                        dve.wait_ge(ak_evac[g], (n * 2 + s) * 2 + 2)
                    for i in range(8):
                        cnt = n * 16 + (8 * s + i)
                        for g in range(2):
                            dve.wait_ge(w_ready[g], cnt + 1)
                            for dr in range(2):
                                c = chunk(i, dr)
                                rows = half(c)
                                ins = dve.tensor_tensor(W[rows, g], p_c[g][rows, :, 0:C],
                                                        akv[rows, g, dr, :, c // 2, :], ALU.add)
                            ins.then_inc(w_evac[g], 1)
                        for g in range(2):
                            dve.wait_ge(hy_ready[g], cnt + 1)
                            dve.wait_ge(h_done[g], (n * 2 + s) * 9 + (i + 1))
                            for dr in range(2):
                                tot = dr * DIR_LEN + DIR_LEN - NCH + chunk(i, dr)
                                ins = dve.scalar_tensor_tensor(
                                    H[:, g, (i + 1) % 2, dr, :], H[:, g, i % 2, dr, :], rec[:, s, g, tot:tot + 1],
                                    p_c[g][:, 0, dr * C:(dr + 1) * C], ALU.mult, ALU.add)
                            ins.then_inc(h_done[g], 1)
                            if i >= 4:
                                hp = n * 4 + 2 * s + g
                                if i > 5:
                                    dve.wait_ge(y_evac[g], (n * 2 + s) * 4 + 2)
                                for head in range(2):
                                    rows = slice(head * C, head * C + C)
                                    cf, cb = chunk(i, 0) - 4, chunk(i, 1) - 4
                                    lo, hi = min(cf, cb), max(cf, cb)
                                    out = y[rows, hp, lo:hi + 1:hi - lo, :]
                                    new = p_y[g][rows, head, 0:2 * C].rearrange("p (d t) -> p d t", t=C)
                                    if cf > cb:
                                        new = new[:, ::-1, :]
                                    if i < 6:
                                        ins = dve.tensor_copy(out, new)
                                    else:
                                        ins = dve.tensor_tensor(out, new, out, ALU.add)
                                ins.then_inc(y_evac[g], 1)
    st.close()
    b.end_stage()


class Ring:

    def __init__(self, b, tile, full, used):
        self.tile, self.full, self.used = tile, full, used
        self.loads = self.uses = 0

    def load(self, sp, src, i=0, k=0, ahead=0):
        n = self.loads + ahead
        slot = n % SLOTS
        if isinstance(i, int):
            wait(sp, self.used, n + i * k - (SLOTS - 1))
        else:
            sp.wait_ge(self.used, i * k + (n - (SLOTS - 1)))
        sp.dma_start(self.tile[:, slot, :], src).then_inc(self.full[slot], 16)

    def use(self, pe, ahead=0, i=0, k=0):
        n = self.uses + ahead
        slot = n % SLOTS
        pe.wait_ge(self.full[slot], i * (k // SLOTS * 16) + 16 * (n // SLOTS + 1))
        return self.tile[:, slot, :]


def build_mix_out(b):
    nc, d = b.nc, b.d
    st = ExitStack()
    S = b.stage_sem
    y, x, mixT, mcol, ring = b.y, b.x, b.mixT, b.mcol, b.ring
    ml = b.sb("mload2", [96, 2, 5, P], st)
    bg = b.sb("bonus_gate", [P, HP, 2, T], st)
    sd = b.sb("sd_gn", [P, HP, T], st)
    p_n = b.ps("p_n", [P, 4, NB], st)
    p_m = b.ps("p_mcol", [P, 2, NB], st)
    p_o = b.ps("p_out", [P, 2, NB], st)
    ml_in, bg_in, x_in = S("mload2_in"), S("bonus_gate_in"), S("x_again_in")
    mc_ready, mc_evac = S("mcol2_ready"), S("mcol2_evac")
    mean_ready, cent, sq_ready, var_ready, sd_ready, mix_ready = (
        S("gn_mean_ready"), S("gn_centred"), S("gn_sq_ready"), S("gn_var_ready"), S("gn_sd_ready"), S("mix_ready"))
    o_ready, o_evac = S("wout_ready"), S("wout_evac")
    own_dve, own_pool, router_in = S("own_dve_mo"), S("own_pool_mo"), S("router_in")
    slot_i = st.enter_context(nc.sbuf_tensor("slot_i", [P, CAP], mybir.dt.int32))
    y2 = y[:].rearrange("p h c t -> p (h c t)")
    sd2 = sd[:].rearrange("p h t -> p (h t)")

    with nc.Block() as block:
        @block.sync
        def _(sp):
            for l in range(LAYERS):
                sp.dma_start(ml[:, l, 0:4, :], d["modp"][0, :, l * 96 * P:(l + 1) * 96 * P]
                             .rearrange("g (j p) -> j g p", p=P)).then_inc(ml_in, 16)
                sp.dma_start(ml[:, l, 4, :], d["mod_b"][l]).then_inc(ml_in, 16)
            for ot in range(SLOTS):
                ring.load(sp, d["w_out"][ot], ahead=ot)
            sp.dma_start(x[:], d["xT"]).then_inc(x_in, 16)
            for ot in range(SLOTS, KT):
                ring.load(sp, d["w_out"][ot], ahead=ot)

        @block.gpsimd
        def _(pool):
            own = Count(pool, own_pool)

            def link(ins):
                own.inc(ins)
                own.wait()

            link(pool.memset(b.before[:], 1.0))
            link(pool.affine_select(out=b.before[:], in_=b.before[:], compare_op=ALU.is_ge, fill=0.0, base=-1,
                                    pattern=[[1, P]], channel_multiplier=-1))
            link(pool.memset(b.lower[:], 0.0))
            for mine in range(1, 4):
                link(pool.memset(b.lower[:, 4 * mine:4 * mine + mine], 1.0))
            link(pool.iota(slot_i[:], pattern=[[1, CAP]], base=0, channel_multiplier=0))
            link(pool.tensor_copy(b.slot_no[:], slot_i[:]))
            pool.dma_start(b.router[:], d["router_w"]).then_inc(router_in, 16)
            pool.dma_start(b.router_b[:], d["router_b"].broadcast_to([P, E])).then_inc(router_in, 16)
            pool.wait_ge(router_in, 32)

        @block.scalar
        def _(act):
            act.dma_start(bg[:].rearrange("p h two t -> p h (two t)"),
                          d["rec"][:, :, BONUS_AT:REC_LEN].rearrange("h p n -> p h n")).then_inc(bg_in, 16)
            act.wait_ge(cent, 1)
            act.activation(sd2, y2, ACT.Square).then_inc(sq_ready, 1)
            act.wait_ge(var_ready, 1)
            act.activation(sd2, p_n[:].rearrange("p b n -> p (b n)"), ACT.Sqrt, scale=1.0 / C, bias=b.eps[:, 2:3]
                           ).then_inc(sd_ready, 1)

        @block.tensor
        def _(pe):
            for q in range(4):
                mm = pe.matmul(p_n[:, q, :], b.blk[:], y2[:, q * NB:(q + 1) * NB], start=True, stop=True)
            mm.then_inc(mean_ready, 1)
            pe.wait_ge(ml_in, 64)
            for l in range(LAYERS):
                for part in range(5):
                    mm = pe.matmul(p_m[:, l, 0:96], ml[:, l, part, :], b.ident[0:96, 0:96],
                                   start=part == 0, stop=part == 4)
            mm.then_inc(mc_ready, 1)
            pe.wait_ge(sq_ready, 1)
            for q in range(4):
                mm = pe.matmul(p_n[:, q, :], b.blk[:], sd2[:, q * NB:(q + 1) * NB], start=True, stop=True)
            mm.then_inc(var_ready, 1)
            pe.wait_ge(mix_ready, 1)

            def out_tiles(i):
                for j in range(SLOTS):
                    w = ring.use(pe, ahead=j, i=i, k=SLOTS)
                    wait(pe, o_evac, i * SLOTS + (j - 1))
                    for k in range(KT):
                        mm = pe.matmul(p_o[:, j % 2, 0:T], w[:, k * P:(k + 1) * P], mixT[:, k, :],
                                       start=k == 0, stop=k == KT - 1)
                    mm.then_inc(ring.used, 1)

            for i in range(KT // SLOTS):
                out_tiles(i)

        @block.vector
        def _(dve):
            own = Count(dve, own_dve)

            def link(ins):
                own.inc(ins)
                own.wait()

            dve.wait_ge(mean_ready, 1)
            dve.scalar_tensor_tensor(y2, p_n[:].rearrange("p b n -> p (b n)"), -1.0 / C, y2, ALU.mult, ALU.add
                                     ).then_inc(cent, 1)
            dve.wait_ge(mc_ready, 1)
            own.inc(dve.tensor_copy(mcol[:], p_m[:, :, 0:96]))
            own.wait()
            for l in range(LAYERS):
                own.inc(dve.scalar_tensor_tensor(mcol[:, l, 4 * KT:5 * KT], mcol[:, l, 4 * KT:5 * KT], 1.0,
                                                 b.gain[:, 2 + l, :], ALU.add, ALU.mult))
            own.inc(dve.scalar_tensor_tensor(mcol[:, 1, KT:2 * KT], mcol[:, 1, KT:2 * KT], 1.0,
                                             b.gain[:, 1, :], ALU.add, ALU.mult))
            dve.wait_ge(sd_ready, 1)
            link(dve.reciprocal(sd2, sd2))
            link(dve.tensor_tensor(sd2, sd2, y2, ALU.mult))
            dve.wait_ge(bg_in, 16)
            lng = b.par[:, LN_G, :].rearrange("p (h o) -> p h o", o=1).broadcast_to([P, HP, T])
            lnb = b.par[:, LN_B, :].rearrange("p (h o) -> p h o", o=1).broadcast_to([P, HP, T])
            link(dve.tensor_tensor(sd[:], sd[:], lng, ALU.mult))
            link(dve.tensor_tensor(sd[:], sd[:], lnb, ALU.add))
            link(dve.tensor_tensor(sd[:], sd[:], bg[:, :, 0, :], ALU.add))
            dve.tensor_tensor(mixT[:, 0:HP, :], sd[:], bg[:, :, 1, :], ALU.mult).then_inc(mix_ready, 1)
            dve.wait_ge(x_in, 16)
            base = ring.uses
            for t in range(KT):
                dve.wait_ge(ring.used, base + t + 1)
                dve.scalar_tensor_tensor(x[:, t, :], p_o[:, t % 2, 0:T], mcol[:, 0, 2 * KT + t:2 * KT + t + 1],
                                         x[:, t, :], ALU.mult, ALU.add).then_inc(o_evac, 1)
    ring.loads += KT
    ring.uses += KT
    st.close()
    b.end_stage()


class Norm:

    def __init__(self, b, name, hT, htok, p_sum, p_flip, gain, shift):
        self.b, self.hT, self.htok, self.p_sum, self.p_flip = b, hT, htok, p_sum, p_flip
        self.gain, self.shift = gain, shift
        S = lambda n: b.stage_sem(f"{name}_{n}")
        self.squared, self.summed, self.rooted = S("squared"), S("summed"), S("rooted")
        self.inverted, self.scaled = S("inverted"), S("scaled")
        self.done_act, self.done_dve = S("normed_act"), S("normed_dve")
        self.flipped, self.out_act, self.out_dve = S("flipped"), S("flip_out_act"), S("flip_out_dve")

    def ready(self, eng, k):
        eng.wait_ge(self.done_dve if k % 2 else self.done_act, k // 2 + 1)

    def act(self, act):
        x, h = self.b.x, self.hT
        for q in range(4):
            act.activation(h[:, 4 * q:4 * q + 4, :], x[:, 4 * q:4 * q + 4, :], ACT.Square).then_inc(self.squared, 1)
        act.wait_ge(self.summed, 1)
        act.activation(self.b.rms[:], self.p_sum, ACT.Sqrt, scale=1.0 / D, bias=self.b.eps[:, 0:1]
                       ).then_inc(self.rooted, 1)
        for k in range(0, KT, 2):
            act.wait_ge(self.scaled, k // 4 + 1)
            act.activation(h[:, k, :], h[:, k, :], ACT.Identity, bias=self.shift[:, k:k + 1],
                           scale=self.gain[:, k:k + 1]).then_inc(self.done_act, 1)
        for r in range(0, 8, 2):
            act.wait_ge(self.flipped, r + 1)
            act.activation(self.flip_out(r), self.p_flip[:, 0, :], ACT.Copy).then_inc(self.out_act, 1)

    def dve(self, dve):
        x, h, rms = self.b.x, self.hT, self.b.rms
        dve.wait_ge(self.rooted, 1)
        dve.reciprocal(rms[:], rms[:]).then_inc(self.inverted, 1)
        dve.wait_ge(self.inverted, 1)
        r4 = rms[:].rearrange("p (o t) -> p o t", o=1).broadcast_to([P, 4, T])
        for q in range(4):
            dve.tensor_tensor(h[:, 4 * q:4 * q + 4, :], x[:, 4 * q:4 * q + 4, :], r4, ALU.mult).then_inc(self.scaled, 1)
        for k in range(1, KT, 2):
            dve.wait_ge(self.scaled, k // 4 + 1)
            dve.tensor_scalar(h[:, k, :], h[:, k, :], self.gain[:, k:k + 1], self.shift[:, k:k + 1],
                              ALU.mult, ALU.add).then_inc(self.done_dve, 1)
        for r in range(1, 8, 2):
            dve.wait_ge(self.flipped, r + 1)
            dve.tensor_copy(self.flip_out(r), self.p_flip[:, 1, :]).then_inc(self.out_dve, 1)

    def flip_out(self, r):
        return self.htok[:, r % 2, (r // 2) * NB:(r // 2 + 1) * NB]

    def pe_sum(self, pe):
        for k in range(KT):
            pe.wait_ge(self.squared, k // 4 + 1)
            mm = pe.matmul(self.p_sum, self.b.ones[:], self.hT[:, k, :], start=k == 0, stop=k == KT - 1)
        mm.then_inc(self.summed, 1)

    def pe_flip(self, pe):
        for r in range(8):
            wait(pe, self.out_dve if r % 2 else self.out_act, r // 2)
            for j in range(4):
                k = 4 * (r // 2) + j
                self.ready(pe, k)
                mm = pe.transpose(self.p_flip[:, r % 2, j * P:(j + 1) * P],
                                  self.hT[:, k, (r % 2) * P:(r % 2 + 1) * P], self.b.ident[:])
            mm.then_inc(self.flipped, 1)

    def flips_out(self, eng):
        eng.wait_ge(self.out_act, 4)
        eng.wait_ge(self.out_dve, 4)


class Route:

    def __init__(self, placed, gates, over_i):
        self.placed, self.gates, self.over_i = placed, gates, over_i


def build_moe(b, l):
    nc, d = b.nc, b.d
    st = ExitStack()
    S = lambda n: b.stage_sem(f"moe{l}_{n}")
    x, mcol, ring, htok = b.x, b.mcol, b.ring, b.htok
    chosen = b.sb(f"chosen{l}", [P, 2, E], st)
    placed = b.sb(f"placed{l}", [P, 2, E], st)
    gates = b.sb(f"gates{l}", [P, 2, E], st)
    over = b.sb(f"over{l}", [P, 2, E], st)
    over_n = b.sb(f"over_n{l}", [P, 1], st)
    over_i = st.enter_context(nc.sbuf_tensor(f"over_i{l}", [P, 1], mybir.dt.int32))
    inner = ExitStack()
    hT = b.sb(f"h_moe{l}", [P, KT, T], inner)
    hot = b.sb(f"hot{l}", [P, 2, E, CAP], inner)
    hotq = b.sb(f"hotq{l}", [P, 2, 4, CAP], inner)
    s = b.sb(f"score{l}", [P, 2, E], inner)
    sel = b.sb(f"sel{l}", [P, 2, E], inner)
    beat = b.sb(f"beat{l}", [P, 8, 4, 4], inner)
    beat2 = b.sb(f"beat2{l}", [P, 8, 4, 4], inner)
    gsum = b.sb(f"gsum{l}", [P, 2, 4], inner)
    gwin = b.sb(f"gwin{l}", [P, 2, 4], inner)
    tot = b.sb(f"tot{l}", [P, 2], inner)
    hg = b.sb(f"hg{l}", [P, 2, KT, 4 * CAP], inner)
    comb = b.sb(f"comb{l}", [P, 2, 2, T], inner)
    act_g = b.sb(f"act_g{l}", [P, 2, FF], inner)
    uT = b.sb(f"uT{l}", [P, 2, 4, CAP], inner)
    f = b.sb(f"f{l}", [P, D], inner)
    p_x = b.ps(f"p_x{l}", [P, 2, NB], inner)
    p_gu = b.ps(f"p_gu{l}", [P, 2, NB], inner)
    p_t = b.ps(f"p_t{l}", [P, 4, P], inner)
    p_d = b.ps(f"p_d{l}", [P, 2, NB], inner)
    norm = Norm(b, f"moe{l}", hT, htok, p_x[:, 0, 0:T], p_gu, mcol[:, l, 4 * KT:5 * KT], mcol[:, l, 3 * KT:4 * KT])
    logits, scored, chosen_ready, counted, hot_ready = (
        S("logits"), S("scored"), S("chosen"), S("counted"), S("hot_ready"))
    over_summed, over_counted, over_done = S("over_summed"), S("over_counted"), S("over_done")
    b.route = Route(placed, gates, over_i)
    hotq_ready, g_ready, g_evac, c_ready, c_evac = (
        S("hotq_ready"), S("gather_ready"), S("gather_evac"), S("comb_ready"), S("comb_evac"))
    silu, u_ready, t_ready, t_evac = S("silu"), S("u_ready"), S("ut_ready"), S("ut_evac")
    d_act, d_dve = S("down_evac_act"), S("down_evac_dve")
    own_dve, act_clear = S("own_dve"), S("act_clear")
    N_EX = 8
    HALVES = E // N_EX
    base_use = ring.uses

    with nc.Block() as block:
        @block.sync
        def _(sp):
            with sp.Fori(0, HALVES) as i:
                for j in range(N_EX):
                    for q in range(12):
                        ring.load(sp, d["experts"][l, bass.ds(i * N_EX + j, 1), q][0], i=i, k=N_EX * 12,
                                  ahead=12 * j + q)

        @block.tensor
        def _(pe):
            norm.pe_sum(pe)
            norm.pe_flip(pe)
            for tt in range(2):
                for k in range(KT):
                    mm = pe.matmul(p_x[:, 1, tt * E:(tt + 1) * E], hT[:, k, tt * P:(tt + 1) * P],
                                   b.router[:, k, :], start=k == 0, stop=k == KT - 1)
            mm.then_inc(logits, 1)
            pe.wait_ge(chosen_ready, 1)
            pe.matmul(p_t[:, 0, 0:E], b.before[:], chosen[:, 0, :], start=True, stop=True)
            pe.matmul(p_t[:, 0, E:2 * E], b.before[:], chosen[:, 1, :], start=True, stop=False)
            pe.matmul(p_t[:, 0, E:2 * E], b.ones[:], chosen[:, 0, :], start=False, stop=True).then_inc(counted, 1)
            pe.wait_ge(hot_ready, 1)
            pe.wait_ge(act_clear, 1)
            norm.flips_out(pe)

            def gather(i, quad, r0, r1):
                base = i * 18 + 9 * quad
                if r0 == 0:
                    pe.wait_ge(c_evac, i * 32 + CREDIT)
                pe.wait_ge(g_evac, base + r0 + CREDIT)
                for r in range(r0, r1):
                    if r >= r0 + 2:
                        pe.wait_ge(g_evac, base + (r - 1 + CREDIT))
                    if r < 8:
                        for j in range(2):
                            k = 2 * r + j
                            for tt in range(2):
                                mm = pe.matmul(p_x[:, r % 2, j * 4 * CAP:(j + 1) * 4 * CAP],
                                               htok[:, tt, k * P:(k + 1) * P],
                                               hot[:, tt, bass.ds(i * N_EX + 4 * quad, 4), :], start=tt == 0, stop=tt == 1)
                    else:
                        pe.wait_ge(hotq_ready, i * 2 + (quad + 1))
                        for pair in range(2):
                            for tt in range(2):
                                mm = pe.matmul(p_x[:, 0, (pair * 2 + tt) * P:(pair * 2 + tt + 1) * P],
                                               hotq[:, tt, 2 * pair:2 * pair + 2, :], b.ident[:], start=True, stop=True)
                    mm.then_inc(g_ready, 1)

            def gate_up(i, j):
                pe.wait_ge(u_ready, i * N_EX + (max(j - 1, 0) + CREDIT))
                pe.wait_ge(g_evac, i * 18 + (9 * (j // 4 + 1) + CREDIT))
                for q in range(8):
                    w = ring.use(pe, ahead=12 * j + q, i=i, k=12 * N_EX)
                    for kk in range(4):
                        k = 4 * (q // 2) + kk
                        rows = slice((q % 2) * C, (q % 2) * C + C)
                        mm = pe.matmul(p_gu[rows, j % 2, :], hg[:, j // 4, k, (j % 4) * CAP:(j % 4 + 1) * CAP],
                                       w[:, kk * NB:(kk + 1) * NB], start=q < 2 and kk == 0,
                                       stop=q >= 6 and kk == 3)
                    mm.then_inc(ring.used, 1)

            def down(i, j):
                n = i * N_EX + j
                pe.wait_ge(u_ready, n + (1 + CREDIT))
                pe.wait_ge(t_evac, n + CREDIT)
                for q in range(4):
                    mm = pe.transpose(p_t[:, q, :], act_g[:, j % 2, q * P:(q + 1) * P], b.ident[:])
                mm.then_inc(t_ready, 1)
                pe.wait_ge(t_evac, n + (1 + CREDIT))
                pe.wait_ge(d_act, n + CREDIT)
                pe.wait_ge(d_dve, n + CREDIT)
                for q in range(4):
                    w = ring.use(pe, ahead=12 * j + 8 + q, i=i, k=12 * N_EX)
                    for cb in (0, 2, 1, 3):
                        rows = slice((cb // 2) * C, (cb // 2) * C + C)
                        mm = pe.matmul(p_d[rows, cb % 2, :], uT[:, j % 2, q, :], w[:, cb * NB:(cb + 1) * NB],
                                       start=q == 0, stop=q == 3)
                    mm.then_inc(ring.used, 1)

            def combine(i, pair):
                pe.wait_ge(d_act, i * N_EX + (2 * pair + 2 + CREDIT))
                pe.wait_ge(d_dve, i * N_EX + (2 * pair + 2 + CREDIT))
                pe.wait_ge(g_evac, i * 18 + (18 + CREDIT))
                pe.wait_ge(c_evac, (i * 4 + pair) * 8 + CREDIT)
                for r in range(8):
                    if r >= 2:
                        pe.wait_ge(c_evac, (i * 4 + pair) * 8 + (r - 1 + CREDIT))
                    for jj in range(2):
                        k = 2 * r + jj
                        mm = pe.matmul(p_x[:, r % 2, jj * T:(jj + 1) * T], f[:, k * P:(k + 1) * P],
                                       comb[:, pair // 2, pair % 2, :], start=True, stop=True)
                    mm.then_inc(c_ready, 1)

            pe.sem_inc(g_ready, CREDIT)
            with pe.Fori(0, HALVES) as i:
                gather(i, 0, 0, 9)
                for j in range(N_EX):
                    gate_up(i, j)
                    if j == 0:
                        gather(i, 1, 0, 5)
                    elif j == 1:
                        gather(i, 1, 5, 9)
                    elif j % 2 == 0:
                        combine(i, j // 2 - 1)
                    down(i, j)
                combine(i, 3)
            pe.wait_ge(over_summed, 1)
            pe.matmul(p_t[:, 0, 0:1], b.ones[:], over_n[:], start=True, stop=True).then_inc(over_counted, 1)

        @block.scalar
        def _(act):
            norm.act(act)
            act.wait_ge(logits, 1)
            act.activation(s[:], p_x[:, 1, 0:2 * E].rearrange("p (a e) -> p a e", e=E), ACT.Sigmoid
                           ).then_inc(scored, 1)

            def gathered(i, quad, r0, r1):
                for r in range(r0, r1):
                    act.wait_ge(g_ready, i * 18 + (9 * quad + r + 1 + CREDIT))
                    if r < 8:
                        out = hg[:, quad, 2 * r:2 * r + 2, :].rearrange("p k n -> p (k n)")
                    else:
                        out = comb[:, quad].rearrange("p a t -> p (a t)")
                    act.activation(out, p_x[:, r % 2, :], ACT.Copy).then_inc(g_evac, 1)

            for sem in (g_evac, t_evac, d_act):
                act.sem_inc(sem, CREDIT)
            with act.Fori(0, HALVES) as i:
                gathered(i, 0, 0, 9)
                for j in range(N_EX):
                    n = i * N_EX + j
                    act.wait_ge(ring.used, (n * 12) + (base_use + 8))
                    act.activation(act_g[C:P, j % 2, :], p_gu[0:C, j % 2, :], ACT.Silu).then_inc(silu, 1)
                    if j == 0:
                        gathered(i, 1, 0, 5)
                    elif j == 1:
                        gathered(i, 1, 5, 9)
                    act.wait_ge(t_ready, n + 1)
                    act.activation(uT[:, j % 2], p_t[:, :, C:P], ACT.Copy).then_inc(t_evac, 1)
                    act.wait_ge(ring.used, (n * 12) + (base_use + 12))
                    rows = slice((j % 2) * C, (j % 2) * C + C)
                    act.activation(f[rows, 0:D // 2].rearrange("p (b n) -> p b n", n=NB), p_d[0:C, :, :], ACT.Copy
                                   ).then_inc(d_act, 1)

        @block.gpsimd
        def _(pool):
            pool.memset(act_g[0:C], 0.0).then_inc(act_clear, 1)
            pool.wait_ge(hot_ready, 1)

            def gated(i, quad):
                e4 = bass.ds(i * N_EX + 4 * quad, 4)
                pool.wait_ge(g_ready, i * 18 + (9 * quad + CREDIT))
                for tt in range(2):
                    g = gates[:, tt, e4].rearrange("p (e o) -> p e o", o=1).broadcast_to([P, 4, CAP])
                    ins = pool.tensor_tensor(hotq[:, tt], hot[:, tt, e4, :], g, ALU.mult)
                ins.then_inc(hotq_ready, 1)

            with pool.Fori(0, HALVES) as i:
                gated(i, 0)
                gated(i, 1)

        @block.vector
        def _(dve):
            own = Count(dve, own_dve)

            def link(ins):
                own.inc(ins)
                own.wait()

            norm.dve(dve)
            dve.wait_ge(scored, 1)
            rb = b.router_b[:].rearrange("p (o e) -> p o e", o=1).broadcast_to([P, 2, E])
            link(dve.tensor_tensor(sel[:], s[:], rb, ALU.add))
            low = b.lower[:].rearrange("p (o a c) -> p o a c", o=1, a=4)

            def ranks(values, n):
                v = values.rearrange("p (g e) -> p g e", e=4)
                mine = v.rearrange("p g (e o) -> p g e o", o=1).broadcast_to([P, n, 4, 4])
                other = v.rearrange("p g (o e) -> p g o e", o=1).broadcast_to([P, n, 4, 4])
                own.inc(dve.tensor_tensor(beat[:, 0:n], other, mine, ALU.is_ge))
                own.inc(dve.tensor_tensor(beat2[:, 0:n], other, mine, ALU.is_gt))
                own.wait()
                link(dve.tensor_tensor(beat[:, 0:n], beat[:, 0:n], low.broadcast_to([P, n, 4, 4]), ALU.mult))
                link(dve.tensor_tensor(beat[:, 0:n], beat[:, 0:n], beat2[:, 0:n], ALU.max))

            flat = lambda t: t.rearrange("p a e -> p (a e)")
            ranks(flat(sel[:]), 8)
            link(dve.tensor_reduce(flat(chosen[:]).rearrange("p (g e) -> p g e", e=4), beat[:], AX.X, ALU.add))
            link(dve.tensor_scalar(chosen[:], chosen[:], 2.0, None, ALU.is_lt))
            link(dve.tensor_tensor(placed[:], chosen[:], sel[:], ALU.mult))
            link(dve.tensor_reduce(flat(gsum[:]), flat(placed[:]).rearrange("p (g e) -> p g e", e=4), AX.X, ALU.add))
            ranks(flat(gsum[:]), 2)
            link(dve.tensor_reduce(gwin[:], beat[:, 0:2], AX.X, ALU.add))
            link(dve.tensor_scalar(gwin[:], gwin[:], 1.0, None, ALU.is_lt))
            c4 = flat(chosen[:]).rearrange("p (g e) -> p g e", e=4)
            own.inc(dve.tensor_tensor(c4, c4, flat(gwin[:]).rearrange("p (g o) -> p g o", o=1).broadcast_to([P, 8, 4]), ALU.mult))
            own.wait()
            dve.sem_inc(chosen_ready, 1)
            link(dve.tensor_tensor(gates[:], s[:], chosen[:], ALU.mult))
            link(dve.tensor_reduce(tot[:], gates[:], AX.X, ALU.add))
            link(dve.reciprocal(tot[:], tot[:]))
            link(dve.tensor_tensor(gates[:], gates[:], tot[:].rearrange("p (a o) -> p a o", o=1).broadcast_to([P, 2, E]), ALU.mult))
            dve.wait_ge(counted, 1)
            link(dve.scalar_tensor_tensor(flat(placed[:]), p_t[:, 0, 0:2 * E], 1.0, flat(chosen[:]), ALU.add, ALU.mult))
            link(dve.tensor_scalar(placed[:], placed[:], -1.0, None, ALU.add))
            iota = b.slot_no[:].rearrange("p (o n) -> p o n", o=1).broadcast_to([P, 2 * E, CAP])
            at = flat(placed[:]).rearrange("p (n o) -> p n o", o=1).broadcast_to([P, 2 * E, CAP])
            dve.tensor_tensor(hot[:].rearrange("p a e n -> p (a e) n"), iota, at, ALU.is_equal).then_inc(hot_ready, 1)
            link(dve.tensor_scalar(over[:], placed[:], float(CAP), None, ALU.is_ge))
            dve.tensor_reduce(over_n[:], flat(over[:]), AX.X, ALU.add).then_inc(over_summed, 1)

            def combined(i, pair):
                for r in range(8):
                    dve.wait_ge(c_ready, (i * 4 + pair) * 8 + (r + 1))
                    for jj in range(2):
                        k = 2 * r + jj
                        ins = dve.scalar_tensor_tensor(x[:, k, :], p_x[:, r % 2, jj * T:(jj + 1) * T],
                                                       mcol[:, l, 5 * KT + k:5 * KT + k + 1], x[:, k, :],
                                                       ALU.mult, ALU.add)
                    ins.then_inc(c_evac, 1)

            for sem in (u_ready, c_evac, d_dve):
                dve.sem_inc(sem, CREDIT)
            with dve.Fori(0, HALVES) as i:
                for j in range(N_EX):
                    n = i * N_EX + j
                    dve.wait_ge(silu, n + 1)
                    dve.tensor_tensor(act_g[C:P, j % 2, :], act_g[C:P, j % 2, :], p_gu[C:P, j % 2, :], ALU.mult
                                      ).then_inc(u_ready, 1)
                    if j and j % 2 == 0:
                        combined(i, j // 2 - 1)
                    dve.wait_ge(ring.used, (n * 12) + (base_use + 12))
                    rows = slice((j % 2) * C, (j % 2) * C + C)
                    dve.tensor_copy(f[rows, D // 2:D].rearrange("p (b n) -> p b n", n=NB), p_d[C:P, :, :]
                                    ).then_inc(d_dve, 1)
                combined(i, 3)
            dve.wait_ge(over_counted, 1)
            dve.tensor_copy(over_i[:], p_t[:, 0, 0:1]).then_inc(over_done, 1)
            dve.wait_ge(over_done, 1)
    ring.loads += 12 * E
    ring.uses += 12 * E
    inner.close()
    b.end_stage()
    build_moe_rest(b, l, b.route)
    st.close()


def build_moe_rest(b, l, r):
    nc, d = b.nc, b.d
    st = ExitStack()
    S = lambda n: b.stage_sem(f"rest{l}_{n}")
    x, mcol, htok = b.x, b.mcol, b.htok
    PASSES = T // CAP - 1
    RS = 4
    w = b.sb(f"rest_w{l}", [P, RS, SLOT], st)
    placed = b.sb(f"rest_placed{l}", [P, 2, E], st)
    hot = b.sb(f"rest_hot{l}", [P, 2, CAP], st)
    hotq = b.sb(f"rest_hotq{l}", [P, 2, CAP], st)
    hg = b.sb(f"rest_hg{l}", [P, KT * CAP], st)
    comb = b.sb(f"rest_comb{l}", [C, T], st)
    act_g = b.sb(f"rest_act{l}", [P, FF], st)
    uT = b.sb(f"rest_uT{l}", [P, 4, CAP], st)
    f = b.sb(f"rest_f{l}", [C, D], st)
    p_x = b.ps(f"rest_p_x{l}", [P, 2, NB], st)
    p_c = b.ps(f"rest_p_c{l}", [P, NB], st)
    p_gu = b.ps(f"rest_p_gu{l}", [P, NB], st)
    p_t = b.ps(f"rest_p_t{l}", [P, 4, P], st)
    p_d = b.ps(f"rest_p_d{l}", [P, 2, NB], st)
    w_full = [S(f"w_full{i}") for i in range(RS)]
    w_used, hot_ready, gathered, g_evac = S("w_used"), S("hot_ready"), S("gathered"), S("gather_evac")
    silu, u_ready, t_ready, t_evac = S("silu"), S("u_ready"), S("ut_ready"), S("ut_evac")
    d_ready, d_act, d_dve = S("down_ready"), S("down_evac_act"), S("down_evac_dve")
    c_ready, c_evac, own_dve, act_clear = S("comb_ready"), S("comb_evac"), S("own_dve"), S("act_clear")

    def if_over(eng):
        n = eng.value_load(r.over_i[0:1, 0:1], min_val=0, max_val=2 * T)
        return eng.If(n > 0)

    with nc.Block() as block:
        @block.sync
        def _(sp):
            with if_over(sp):
                with sp.Fori(0, PASSES) as p:
                    with sp.Fori(0, E) as e:
                        for q in range(12):
                            n = (p * E + e) * 12
                            sp.wait_ge(w_used, n + (max(q - RS + 1, 0) + CREDIT))
                            sp.dma_start(w[:, q % RS, :], d["experts"][l, bass.ds(e, 1), q][0]
                                         ).then_inc(w_full[q % RS], 16)

        @block.tensor
        def _(pe):
            with if_over(pe):
                pe.sem_inc(w_used, CREDIT)
                pe.wait_ge(act_clear, 1)
                with pe.Fori(0, PASSES) as p:
                    with pe.Fori(0, E) as e:
                        n = p * E + e
                        pe.wait_ge(hot_ready, n + 1)
                        pe.wait_ge(c_evac, n * 8 + CREDIT)
                        for k in range(KT):
                            for tt in range(2):
                                mm = pe.matmul(p_x[:, k // 8, (k % 8) * CAP:(k % 8 + 1) * CAP],
                                               htok[:, tt, k * P:(k + 1) * P], hot[:, tt, :],
                                               start=tt == 0, stop=tt == 1)
                        for tt in range(2):
                            mm = pe.matmul(p_c[0:CAP, tt * P:(tt + 1) * P], hotq[:, tt, :], b.ident[:],
                                           start=True, stop=True)
                        mm.then_inc(gathered, 1)
                        pe.wait_ge(g_evac, n + 1)
                        for q in range(8):
                            pe.wait_ge(w_full[q % RS], n * (16 * 12 // RS) + 16 * (q // RS + 1))
                            for kk in range(4):
                                k = 4 * (q // 2) + kk
                                rows = slice((q % 2) * C, (q % 2) * C + C)
                                mm = pe.matmul(p_gu[rows, :], hg[:, k * CAP:(k + 1) * CAP],
                                               w[:, q % RS, kk * NB:(kk + 1) * NB], start=q < 2 and kk == 0,
                                               stop=q >= 6 and kk == 3)
                            mm.then_inc(w_used, 1)
                        pe.wait_ge(u_ready, n + 1)
                        for q in range(4):
                            mm = pe.transpose(p_t[:, q, :], act_g[:, q * P:(q + 1) * P], b.ident[:])
                        mm.then_inc(t_ready, 1)
                        pe.wait_ge(t_evac, n + 1)
                        for q in range(4):
                            pe.wait_ge(w_full[q % RS], n * (16 * 12 // RS) + 16 * ((8 + q) // RS + 1))
                            for cb in (0, 2, 1, 3):
                                rows = slice((cb // 2) * C, (cb // 2) * C + C)
                                mm = pe.matmul(p_d[rows, cb % 2, :], uT[:, q, :], w[:, q % RS, cb * NB:(cb + 1) * NB],
                                               start=q == 0, stop=q == 3)
                            mm.then_inc(w_used, 1)
                        pe.wait_ge(d_act, n + 1)
                        pe.wait_ge(d_dve, n + 1)
                        for rd in range(8):
                            if rd >= 2:
                                pe.wait_ge(c_evac, n * 8 + (rd - 1 + CREDIT))
                            for jj in range(2):
                                k = 2 * rd + jj
                                mm = pe.matmul(p_x[:, rd % 2, jj * T:(jj + 1) * T], f[:, k * P:(k + 1) * P],
                                               comb[:], start=True, stop=True)
                            mm.then_inc(c_ready, 1)

        @block.scalar
        def _(act):
            with if_over(act):
                with act.Fori(0, PASSES) as p:
                    with act.Fori(0, E) as e:
                        n = p * E + e
                        act.wait_ge(gathered, n + 1)
                        act.activation(hg[:], p_x[:].rearrange("p b n -> p (b n)"), ACT.Copy)
                        act.activation(comb[:], p_c[0:CAP, 0:T], ACT.Copy).then_inc(g_evac, 1)
                        act.wait_ge(w_used, n * 12 + (8 + CREDIT))
                        act.activation(act_g[C:P, :], p_gu[0:C, :], ACT.Silu).then_inc(silu, 1)
                        act.wait_ge(t_ready, n + 1)
                        act.activation(uT[:], p_t[:, :, C:P], ACT.Copy).then_inc(t_evac, 1)
                        act.wait_ge(w_used, n * 12 + (12 + CREDIT))
                        act.activation(f[:, 0:D // 2].rearrange("p (b n) -> p b n", n=NB), p_d[0:C, :, :], ACT.Copy
                                       ).then_inc(d_act, 1)

        @block.gpsimd
        def _(pool):
            pool.memset(act_g[0:C], 0.0).then_inc(act_clear, 1)

        @block.vector
        def _(dve):
            with if_over(dve):
                dve.sem_inc(c_evac, CREDIT)
                dve.tensor_copy(placed[:], r.placed[:]).then_inc(own_dve, 1)
                with dve.Fori(0, PASSES) as p:
                    dve.wait_ge(own_dve, p * (1 + E) + 1)
                    dve.tensor_scalar(placed[:], placed[:], -float(CAP), None, ALU.add).then_inc(own_dve, 1)
                    with dve.Fori(0, E) as e:
                        n = p * E + e
                        own = p * (1 + E) + e + 2
                        slot = b.slot_no[:].rearrange("p (o n) -> p o n", o=1).broadcast_to([P, 2, CAP])
                        dve.wait_ge(own_dve, own)
                        dve.tensor_tensor(hot[:], slot, placed[:, :, bass.ds(e, 1)].broadcast_to([P, 2, CAP]),
                                          ALU.is_equal).then_inc(own_dve, 1)
                        dve.wait_ge(own_dve, own + 1)
                        dve.tensor_tensor(hotq[:], hot[:], r.gates[:, :, bass.ds(e, 1)].broadcast_to([P, 2, CAP]),
                                          ALU.mult).then_inc(hot_ready, 1)
                        dve.wait_ge(silu, n + 1)
                        dve.tensor_tensor(act_g[C:P, :], act_g[C:P, :], p_gu[C:P, :], ALU.mult).then_inc(u_ready, 1)
                        dve.wait_ge(w_used, n * 12 + (12 + CREDIT))
                        dve.tensor_copy(f[:, D // 2:D].rearrange("p (b n) -> p b n", n=NB), p_d[C:P, :, :]
                                        ).then_inc(d_dve, 1)
                        for rd in range(8):
                            dve.wait_ge(c_ready, n * 8 + (rd + 1))
                            for jj in range(2):
                                k = 2 * rd + jj
                                ins = dve.scalar_tensor_tensor(x[:, k, :], p_x[:, rd % 2, jj * T:(jj + 1) * T],
                                                               mcol[:, l, 5 * KT + k:5 * KT + k + 1], x[:, k, :],
                                                               ALU.mult, ALU.add)
                            ins.then_inc(c_evac, 1)
    st.close()
    b.end_stage()


def build_fourier(b):
    nc, d = b.nc, b.d
    st = ExitStack()
    S = lambda n: b.stage_sem(f"ft_{n}")
    x, mcol, ring, htok, mixT = b.x, b.mcol, b.ring, b.htok, b.mixT
    hT = b.sb("h_ft", [P, KT, T], st)
    dft_t = b.sb("dft_t", [P, 2, 2 * T], st)
    dft_c = b.sb("dft_c", [P, 2, 2, T], st)
    ab = b.sb("ft_ab", [P, KT, 2 * T], st)
    p_s = b.ps("p_ft_s", [P, 2, NB], st)
    p_f = b.ps("p_ft_f", [P, 2, NB], st)
    p_o = b.ps("p_ft_o", [P, 2, NB], st)
    norm = Norm(b, "ft", hT, htok, p_s[:, 0, 0:T], p_f, mcol[:, 1, KT:2 * KT], mcol[:, 1, 0:KT])
    dft_in, ab_ready, ab_act, ab_dve = S("dft_in"), S("ab_ready"), S("ab_evac_act"), S("ab_evac_dve")
    mix_ready, mix_evac, o_evac = S("mix_ready"), S("mix_evac"), S("o_evac")

    with nc.Block() as block:
        @block.sync
        def _(sp):
            sp.dma_start(dft_t[:], d["dft_t"]).then_inc(dft_in, 16)
            sp.dma_start(dft_c[:], d["dft_c"]).then_inc(dft_in, 16)
            with sp.Fori(0, KT // SLOTS) as i:
                for j in range(SLOTS):
                    ring.load(sp, d["f_out"][bass.ds(i * SLOTS + j, 1)][0], i=i, k=SLOTS, ahead=j)

        @block.tensor
        def _(pe):
            norm.pe_sum(pe)
            norm.pe_flip(pe)
            norm.flips_out(pe)
            pe.wait_ge(dft_in, 32)
            for k in range(KT):
                wait(pe, ab_dve if k % 2 else ab_act, k // 2)
                for tt in range(2):
                    mm = pe.matmul(p_s[:, k % 2, :], htok[:, tt, k * P:(k + 1) * P], dft_t[:, tt, :],
                                   start=tt == 0, stop=tt == 1)
                mm.then_inc(ab_ready, 1)
            pe.wait_ge(ab_act, 8)
            pe.wait_ge(ab_dve, 8)
            for k in range(KT):
                g, half = k // 2, k % 2
                wait(pe, mix_evac, k - 1)
                for kk in range(2):
                    for part in range(2):
                        mm = pe.matmul(p_f[:, k % 2, 0:T], dft_c[:, kk, part, half * P:(half + 1) * P],
                                       ab[:, 2 * g + kk, part * T:(part + 1) * T],
                                       start=kk == 0 and part == 0, stop=kk == 1 and part == 1)
                mm.then_inc(mix_ready, 1)
            pe.wait_ge(mix_evac, KT)
            with pe.Fori(0, KT // SLOTS) as i:
                for j in range(SLOTS):
                    w = ring.use(pe, ahead=j, i=i, k=SLOTS)
                    pe.wait_ge(o_evac, i * SLOTS + (max(j - 1, 0) + CREDIT))
                    for k in range(KT):
                        mm = pe.matmul(p_o[:, j % 2, 0:T], w[:, k * P:(k + 1) * P], mixT[:, k, :],
                                       start=k == 0, stop=k == KT - 1)
                    mm.then_inc(ring.used, 1)

        @block.scalar
        def _(act):
            norm.act(act)
            for k in range(0, KT, 2):
                act.wait_ge(ab_ready, k + 1)
                act.activation(ab[:, k, :], p_s[:, 0, :], ACT.Copy).then_inc(ab_act, 1)
            for k in range(KT):
                act.wait_ge(mix_ready, k + 1)
                act.activation(mixT[:, k, :], p_f[:, k % 2, 0:T], ACT.Copy).then_inc(mix_evac, 1)

        @block.vector
        def _(dve):
            norm.dve(dve)
            for k in range(1, KT, 2):
                dve.wait_ge(ab_ready, k + 1)
                dve.tensor_copy(ab[:, k, :], p_s[:, 1, :]).then_inc(ab_dve, 1)
            base = ring.uses
            dve.sem_inc(o_evac, CREDIT)
            for t in range(KT):
                dve.wait_ge(ring.used, base + t + 1)
                dve.scalar_tensor_tensor(x[:, t, :], p_o[:, t % 2, 0:T], mcol[:, 1, 2 * KT + t:2 * KT + t + 1],
                                         x[:, t, :], ALU.mult, ALU.add).then_inc(o_evac, 1)
    ring.loads += KT
    ring.uses += KT
    st.close()
    b.end_stage()

def build_finish(b):
    nc, d = b.nc, b.d
    stored = b.sem("out_stored")
    with nc.Block() as block:
        @block.sync
        def _(sp):
            sp.dma_start(d["out"], b.x[:]).then_inc(stored, 16)
            sp.wait_ge(stored, 16)


def build(nc, dram, stages=None):
    b = Builder(nc, dram)
    b.ident = b.sb("ident", [P, P])
    b.ones = b.sb("ones", [P, P])
    b.blk = b.sb("blk", [P, P])
    b.eps = b.sb("eps", [P, 4])
    b.gain = b.sb("gain", [P, 4, KT])
    b.par = b.sb("par", [P, N_PAR + 6, HP])
    b.mixT = b.sb("mixT", [P, KT, T])
    early = ExitStack()
    b.cond = b.sb("cond", [P, KT, 2], early)
    b.scol = b.sb("scol", [P, KT, 32], early)
    b.mring = b.sb("mring", [P, M_RING, SLOT], early)
    b.stage = b.sb("mod_stage", [P, 2, NB], early)
    b.hT = b.sb("hT", [P, KT, T2], early)
    b.mod_full = [b.sem(f"mod_full{i}") for i in range(M_RING)]
    b.mod_used, b.mod_evac = b.sem("mod_used"), b.sem("mod_evac")
    b.mod_stored = [b.sem(f"mod_stored{i}") for i in range(2)]
    build_mix_in(b)
    b.ksq = b.sb("ksq", [P, 2, T2], early)
    build_attend(b)
    early.close()
    b.y = b.sb("y", [P, HP, 4, C])
    build_recur(b)
    b.x = b.sb("x", [P, KT, T])
    b.mcol = b.sb("mcol", [P, LAYERS, 96])
    b.ring = Ring(b, b.sb("ring", [P, SLOTS, SLOT]), [b.sem(f"ring_full{i}") for i in range(SLOTS)],
                  b.sem("ring_used"))
    b.htok = b.sb("htok", [P, 2, D])
    b.rms = b.sb("rms", [P, T])
    b.router = b.sb("router", [P, KT, E])
    b.router_b = b.sb("router_b", [P, E])
    b.before = b.sb("before", [P, P])
    b.lower = b.sb("lower", [P, 16])
    b.slot_no = b.sb("slot_no", [P, CAP])
    build_mix_out(b)
    build_moe(b, 0)
    if stages != "moe0":
        build_fourier(b)
        build_moe(b, 1)
    build_finish(b)
    return b


def shape_tables():
    f32 = np.float32
    t = np.arange(T)
    inv = f32(10000.0) ** (-np.arange(0, HD // 2, 2, dtype=f32) / f32(HD // 2))
    ang = np.concatenate([(t // 64).astype(f32)[:, None] * inv, (t % 64).astype(f32)[:, None] * inv], axis=1)
    ang = np.repeat(ang, 2, axis=1).T
    rot = np.zeros((HD, HD), f32)
    even = np.arange(0, HD, 2)
    rot[even + 1, even], rot[even, even + 1] = -1.0, 1.0
    n = np.arange(T)
    turn = 2 * np.pi / T * (np.outer(n, n) % T)
    cos, sin = np.cos(turn) / 16, np.sin(turn) / 16
    dft_t = np.concatenate([cos, sin], axis=1).reshape(2, P, 2 * T).transpose(1, 0, 2).astype(f32)
    dft_c = np.stack([cos, -sin], axis=1).reshape(2, P, 2, T).transpose(1, 0, 2, 3).astype(f32)
    return {"dft_t": dft_t, "dft_c": dft_c, "rope": np.stack([np.cos(ang), np.sin(ang)], axis=1).astype(f32), "rot": rot}


def host_layout(i):
    f = {}
    cols = lambda v: v.reshape(-1, P).T
    f["xT"] = i["x"][0].T.reshape(KT, P, T).transpose(1, 0, 2)
    f["ctxT"] = i["ctx"][0].T.reshape(KT, P, T).transpose(1, 0, 2)
    f["cond"] = np.stack([cols(i["c"][0]), cols(i["c_ctx"])], axis=2)
    f["mod_w"] = (i["mod_w"].reshape(2, 4, 4, P, MOD_BLOCKS, NB).transpose(0, 4, 1, 3, 2, 5)
                  .reshape(2 * MOD_BLOCKS, 4, P, SLOT))
    f["mod_b"] = i["mod_b"].reshape(2, 96, P)
    f["gain"] = np.stack([cols(i["norm_mix"][0]), cols(i["norm_mix"][1]),
                          cols(i["norm_ffn"][0]), cols(i["norm_ffn"][1])], axis=1)
    f["mu"] = np.stack([i["ab_mu_prev"][0].reshape(26, P).T, i["ab_mu_next"][0].reshape(26, P).T], axis=1)[:, :, TILE_ORDER[:26]]
    w = i["ab_w_in"][0].reshape(KT, P, 38, P).transpose(2, 1, 0, 3).reshape(38, P, SLOT)
    f["w_in"] = w[TILE_ORDER]
    f["par"] = np.stack([cols(v) for v in (i["rwkv_w0"][0, 0], i["rwkv_w0"][0, 1], i["rwkv_a0"][0, 0],
                                           i["rwkv_a0"][0, 1], i["rwkv_k_k"][0], i["rwkv_k_a"][0],
                                           i["rwkv_r_k"][0].reshape(-1), i["rwkv_ln_g"][0],
                                           i["rwkv_ln_b"][0])], axis=1)
    low = np.concatenate([i["rwkv_w2"][0], i["rwkv_a2"][0]], axis=1)
    low = np.concatenate([low, i["rwkv_g2"][0][None]], axis=0)
    f["lora_w"] = low.reshape(3, P, HP, P).transpose(2, 1, 0, 3)
    f["w_out"] = i["ab_w_out"][0].reshape(KT, P, KT, P).transpose(2, 1, 0, 3).reshape(KT, P, SLOT)
    f["f_out"] = i["fourier_w_out"][0].reshape(KT, P, KT, P).transpose(2, 1, 0, 3).reshape(KT, P, SLOT)
    f["router_w"] = i["router_w"].reshape(KT, P, E).transpose(1, 0, 2)
    f["router_b"] = i["router_b"][None]
    gu = np.stack([i["exp_w_gate"], i["exp_w_up"]], axis=2).reshape(2, E, 2, 4, 4, P, FF)
    gu = gu.transpose(0, 1, 3, 2, 5, 4, 6).reshape(2, E, 8, P, SLOT)
    f["experts"] = np.concatenate([gu, i["exp_w_down"].reshape(2, E, 4, P, D)], axis=2)
    f["hgain"] = np.stack([i["attn_q_norm"][0], i["attn_k_norm"][0]], axis=1)
    f.update(shape_tables())
    return {k: np.ascontiguousarray(v) for k, v in f.items()}


SCRATCH = {
    "modp": (2, 4, 2 * MOD_BLOCKS * NB),
    "rec": (HP, P, REC_LEN),
    "tri": (2, HP, 2, NCH // 2, 2, C, C),
    "inv": (2, HP, 2, NCH // 2, 2, C, C),
}


def program(nc, arrays, stages=None):
    dram = {k: nc.dram_tensor("in_" + k, a.shape, F32, kind="ExternalInput").ap() for k, a in arrays.items()}
    for k, shape in SCRATCH.items():
        dram[k] = nc.dram_tensor("scratch_" + k, shape, F32, kind="Internal").ap()
    dram["out"] = nc.dram_tensor("out", (P, KT, T), F32, kind="ExternalOutput").ap()
    build(nc, dram, stages)


def kernel(**inputs):
    import concourse.bacc as bacc
    from concourse.bass_utils import run_bass_kernel_spmd
    nc = bacc.Bacc("TRN2", target_bir_lowering=False, num_devices=1)
    arrays = host_layout({k: np.asarray(v) for k, v in inputs.items()})
    program(nc, arrays)
    got = run_bass_kernel_spmd(nc, [{"in_" + k: a for k, a in arrays.items()}], core_ids=[0]).results[0]["out"]
    return np.ascontiguousarray(got.transpose(1, 0, 2).reshape(D, T).T[None])
```

```python
from contextlib import ExitStack

import numpy as np

import concourse.bass as bass
from concourse import mybir

F32 = mybir.dt.float32
ALU = mybir.AluOpType
ACT = mybir.ActivationFunctionType
AX = mybir.AxisListType

P = 128
D = 2048
KT = D // P
T = 256
T2 = 2 * T
NB = 512
MOD_BLOCKS = 6 * D // NB
MOD_FIRST = 2 * D // NB
HP = 1024 // P
C = 64
A_TILES = 26
NH = 8
HD = 128
NCH = T2 // C
SLOT = KT * P
W_RING = 3
SLOTS = 12
LAYERS = 2
E = 16
CAP = 64
FF = 512
M_RING = 4
NORM_EPS = 1e-6
LNX_EPS = 64e-5
MOD_PAIRS = HP - 1
EARLY_TILES = 4
CREDIT = 1
DECAY = float(np.exp(-0.5))

TILE_ORDER = ([24, 25] + [t for hp in range(HP) for t in (hp, 8 + hp, 16 + hp)]
              + [34, 35, 36, 37] + list(range(26, 34)))
W0, A0, K_K, K_A, R_K, LN_G, LN_B = 0, 2, 4, 5, 6, 7, 8
N_PAR = 9

G_LEN = 2 * (4 * C + 4 * 2 * C)
BK_LEN = NCH * P
AR_LEN = NCH * 2 * C
DIR_LEN = G_LEN + BK_LEN + AR_LEN + NCH
V_AT = 2 * DIR_LEN
BONUS_AT = V_AT + 4 * P
GATE_AT = BONUS_AT + T
REC_LEN = GATE_AT + T


def g_at(head, c):
    base = head * (G_LEN // 2)
    return (base + c * C, C) if c < 4 else (base + 4 * C + (c - 4) * 2 * C, 2 * C)


class Count:

    def __init__(self, eng, sem):
        self.eng, self.sem, self.n, self.i, self.k, self.first = eng, sem, 0, None, 0, 0

    def loop(self, i, k, first=0):
        self.i, self.k, self.first, self.start = i, k, first, self.n

    def end(self, iterations):
        assert self.n - self.start == self.k, (self.n - self.start, self.k)
        self.n, self.i = self.start + self.k * iterations, None

    def inc(self, ins):
        ins.then_inc(self.sem, 1)
        self.n += 1

    def wait(self, back=0):
        v = self.n - back
        wait(self.eng, self.sem, v if self.i is None else self.i * self.k + (v - self.first * self.k))


def wait(eng, sem, value):
    if not (isinstance(value, int) and value <= 0):
        eng.wait_ge(sem, value)


class Builder:
    def __init__(self, nc, dram):
        self.nc, self.d = nc, dram
        self.keep = ExitStack()
        self.staged = []

    def sem(self, name):
        return self.nc.alloc_semaphore(name)

    def stage_sem(self, name):
        self.staged.append(self.nc.alloc_semaphore(name))
        return self.staged[-1]

    def end_stage(self):
        self.nc.clear_and_free_semaphores(self.staged)
        self.staged = []
        self.nc.all_engine_barrier()

    def sb(self, name, shape, stack=None):
        return (stack or self.keep).enter_context(self.nc.sbuf_tensor(name, shape, F32))

    def ps(self, name, shape, stack):
        return stack.enter_context(self.nc.psum_tensor(name, shape, F32))


    def attention_tile_out(self, act, n, bank):
        if n < 4:
            ins = act.activation(self.kv[:, n, :], bank, ACT.Copy)
            return act.activation(self.ksq[:, n, :], bank, ACT.Square) if n < 2 else ins
        act.activation(self.q[:, n - 4, :], bank[:, 0:T], ACT.Copy)
        return act.activation(self.qsq[:, n - 4, :], bank[:, 0:T], ACT.Square)


def build_mix_in(b):
    nc, d = b.nc, b.d
    st = ExitStack()
    S = b.stage_sem
    ident, blk, hT, par = b.ident, b.blk, b.hT, b.par
    wring, mring, stage = b.wring, b.mring, b.stage
    sq = b.sb("sq_mix", [P, 2, T2], st)
    mload = b.sb("mload", [32, 2, 5, P], st)
    shc = b.sb("shc", [P, 2, KT], st)
    scc = b.sb("scc", [P, 2, KT], st)
    lora = b.sb("lora", [P, 2, T2], st)
    rkv = b.sb("rkv", [P, 3, T2], st)
    mu = b.sb("mu", [P, 3, 26], st)
    cur = b.sb("cur_cols", [P, 8], st)
    lw = b.sb("lora_w", [P, 3, P], st)
    mask = b.sb("mask", [P, 2, 2 * C], st)
    restart = b.sb("restart", [P, T2], st)
    tw = b.sb("tw", [P, 2, T2], st)
    ta = b.sb("ta", [P, 2, T2], st)
    cum = b.sb("cum", [P, T2], st)
    ep = b.sb("ep", [P, T2], st)
    en = b.sb("en", [P, T2], st)
    ex = b.sb("ex", [P, T2], st)
    kkr = b.sb("kkr", [P, T2], st)
    kk = b.sb("kk", [P, T2], st)
    kd = b.sb("kd", [P, 2, T2], st)
    rkb = b.sb("rkb", [P, T], st)
    both = b.mixT[:].rearrange("p k t -> p (k t)").rearrange("p (w d c n) -> p w d c n", w=2, d=2, n=2 * C)
    kb, kbp = both[:, 0], both[:, 1]
    rec = b.sb("rec", [P, REC_LEN], st)
    p_in = b.ps("p_in", [P, 2, NB], st)
    p_mod = b.ps("p_mod", [P, 2, NB], st)
    p_lo = b.ps("p_lo", [P, 2, NB], st)
    p_g = b.ps("p_g", [P, 2, NB], st)

    cond_in, x_in, small_in = S("cond_in"), S("x_in"), S("small_in")
    consts_ready, silu_ready, par_ready = S("consts_ready"), S("silu_ready"), S("par_ready")
    mod_full, mod_used, mod_evac, mod_stored = b.mod_full, b.mod_used, b.mod_evac, b.mod_stored
    w_full = b.w_full
    sq_ready, sq_used, rms_ready, rstd_ready, hr_ready = (
        S("sq_ready"), S("sq_used"), S("rms_ready"), S("rstd_ready"), S("hr_ready"))
    mload_in, mcol_ready, mcol_evac = S("mload_in"), S("mcol_ready"), S("mcol_evac")
    h_ctx, h_lat = S("h_ctx_ready"), S("h_lat_ready")
    in_ready, in_scaled, in_evac = S("in_ready"), S("in_scaled"), S("in_evac")
    cur_ready, at_evac = S("cur_ready"), S("at_early_evac")
    lora_ready, lw_in = S("lora_ready"), S("lora_w_in")
    z_ready, z_used = S("z_ready"), S("z_used")
    kks_ready, rkb_ready = S("kks_ready"), S("rkb_ready")
    cum_ready, x_ready, e_ready = S("cum_ready"), S("x_ready"), S("e_ready")
    kb_ready, kbp_ready = S("kb_ready"), S("kbp_ready")
    g_ready, g_evac, t_ready, t_evac = S("g_ready"), S("g_evac"), S("t_ready"), S("t_evac")
    pair_read = S("pair_read")
    rec_stored, tri_stored = S("rec_stored"), S("tri_stored")
    own_dve, own_pool = S("own_dve_in"), S("own_pool_in")

    def chunks(ap):
        return ap.rearrange("p (c t) -> p c t", t=C)

    with nc.Block() as block:
        @block.sync
        def _(sp):
            def mod_load(m):
                for q in range(4):
                    wait(sp, mod_used, m * 4 + q - 3)
                    sp.dma_start(mring[:, q, :], d["mod_w"][bass.ds(m, 1), q][0]).then_inc(mod_full[q], 16)

            def w_load(t, slot):
                wait(sp, in_ready, t - 2)
                sp.dma_start(wring[:, slot, :], d["w_in"][bass.ds(t, 1)][0]).then_inc(w_full[slot], 16)

            mod_load(0)
            with sp.Fori(1, MOD_FIRST) as m:
                mod_load(m)
            for t in range(5):
                w_load(t, t % 3)

            def lora_load(hp):
                wait(sp, z_ready, hp * 6)
                sp.dma_start(lw[:], d["lora_w"][bass.ds(hp, 1)][0]).then_inc(lw_in, 16)

            def pair(hp, mods=True, last=False):
                for j in range(3):
                    if mods:
                        mod_load(hp * 4 + (MOD_FIRST + 1 + j))
                        if j == 2:
                            mod_load(hp * 4 + (MOD_FIRST + 4))
                    w_load(hp * 3 + (5 + j), (2 + j) % 3)
                if not last:
                    lora_load(hp + 1)

            lora_load(0)
            mod_load(MOD_FIRST)
            with sp.Fori(0, MOD_PAIRS) as hp:
                pair(hp)
            for hp in range(MOD_PAIRS, HP):
                pair(hp, mods=False, last=hp == HP - 1)
            for t in range(A_TILES + 3, A_TILES + EARLY_TILES + 3):
                w_load(t, t % 3)

        @block.gpsimd
        def _(pool):
            own = Count(pool, own_pool)

            def link(ins):
                own.inc(ins)
                own.wait()

            link(pool.memset(ident[:], 0.0))
            link(pool.memset(blk[:], 0.0))
            link(pool.memset(restart[:], 1.0))
            link(pool.memset(mask[:], 1.0))
            link(pool.memset(b.ones[:], 1.0))
            link(pool.memset(b.eps[:, 0:1], NORM_EPS))
            link(pool.memset(b.eps[:, 1:2], 1e-12))
            link(pool.memset(b.eps[:, 2:3], LNX_EPS))
            link(pool.memset(blk[0:C, 0:C], 1.0))
            link(pool.memset(blk[C:P, C:P], 1.0))
            link(pool.memset(chunks(restart[:])[:, :, 0:1], 0.0))
            for half in range(2):
                rows = slice(half * C, half * C + C)
                for dr in range(2):
                    sign = 1 if dr == 0 else -1
                    for incl in range(2):
                        part = mask[rows, dr, incl * C:incl * C + C]
                        link(pool.affine_select(out=part, in_=part, compare_op=ALU.is_ge, fill=0.0,
                                                   base=incl - 1, pattern=[[sign, C]],
                                                   channel_multiplier=-sign))
            link(pool.affine_select(out=ident[:], in_=ident[:], compare_op=ALU.not_equal, fill=1.0,
                                       base=0, pattern=[[-1, P]], channel_multiplier=1))
            pool.sem_inc(consts_ready, 1)

            def mod_store(m, buf):
                pool.wait_ge(mod_evac, m + 1)
                for row in range(2):
                    pool.dma_start(d["modp"][row, :, bass.ds(m * NB, NB)], stage[row:P:32, buf, :]
                                   ).then_inc(mod_stored[buf], 16)

            with pool.Fori(0, MOD_FIRST, 2) as m:
                mod_store(m, 0)
                mod_store(m + 1, 1)
            for q in range(2):
                pool.wait_ge(mod_stored[q], 16 * MOD_FIRST)
            for row in range(2):
                pool.dma_start(mload[:, row, 0:4, :],
                               d["modp"][row, :, 0:32 * P].rearrange("g (j p) -> j g p", p=P)
                               ).then_inc(mload_in, 16)
                pool.dma_start(mload[:, row, 4, :], d["mod_b"][0, 0:32, :]).then_inc(mload_in, 16)

            def record_out(hp):
                for dr in range(2):
                    pool.wait_ge(g_evac, hp * 5 + (2 * dr + 2))
                    for head in range(2):
                        for lat in range(2):
                            base, n = g_at(head, 4 * lat)
                            for odd in range(2):
                                rows = slice(0, C) if odd else slice(C, P)
                                src = rec[rows, dr * DIR_LEN + base:dr * DIR_LEN + base + 4 * n]
                                src = src.rearrange("p (c e t) -> p e c t", e=2, t=n)[:, odd, :, 0:C]
                                dst = d["tri"][dr, bass.ds(hp, 1), head, 2 * lat:2 * lat + 2, odd]
                                pool.dma_start(dst.rearrange("o c s t -> s (o c) t"), src
                                               ).then_inc(tri_stored, 16)
                pool.wait_ge(g_evac, hp * 5 + 5)
                pool.wait_ge(t_evac, hp * 3 + 3)
                pool.wait_ge(z_used, hp * 6 + 6)
                pool.dma_start(d["rec"][bass.ds(hp, 1)][0], rec[:]).then_inc(rec_stored, 16)

            def pair(hp, first=False, mods=True):
                if mods:
                    for j in range(3):
                        mod_store(hp * 4 + (MOD_FIRST + j), j % 2)
                if not first:
                    record_out(hp - 1)
                if mods:
                    mod_store(hp * 4 + (MOD_FIRST + 3), 1)
                if not first:
                    pool.wait_ge(rec_stored, hp * 16)
                    pool.wait_ge(tri_stored, hp * 256)
                for dr in range(2):
                    pool.wait_ge(kb_ready, hp * 2 + (dr + 1))
                    last = C - 1 if dr == 0 else 0
                    total = chunks(ep[:])[:, :, last:last + 1]
                    pool.tensor_tensor(kbp[:, dr], kb[:, dr], total.broadcast_to([P, NCH, 2 * C]), ALU.mult)
                    pool.tensor_copy(rec[:, dr * DIR_LEN + DIR_LEN - NCH:dr * DIR_LEN + DIR_LEN],
                                     total.rearrange("p c o -> p (c o)")).then_inc(kbp_ready, 1)

            pair(0, True)
            with pool.Fori(1, MOD_PAIRS) as hp:
                pair(hp)
            for hp in range(MOD_PAIRS, HP):
                pair(hp, mods=False)
            record_out(HP - 1)
            pool.wait_ge(rec_stored, 16 * HP)
            pool.wait_ge(tri_stored, 256 * HP)
            for q in range(2):
                pool.wait_ge(mod_stored[q], 16 * (MOD_FIRST + 4 * MOD_PAIRS))

        @block.tensor
        def _(pe):
            def mod_slots(m, bank, qs):
                for q in qs:
                    if q == 0:
                        wait(pe, mod_evac, m - 1)
                    pe.wait_ge(mod_full[q], m * 16 + 16)
                    for g in range(4):
                        mm = pe.matmul(p_mod[32 * g:32 * g + 32, bank, :], b.scol[:, 4 * q + g, :],
                                       mring[:, q, g * NB:(g + 1) * NB], start=q == 0, stop=q == 3)
                    mm.then_inc(mod_used, 1)

            def mod_block(m, bank):
                mod_slots(m, bank, range(4))

            pe.wait_ge(consts_ready, 1)
            pe.wait_ge(silu_ready, 1)
            for half in range(2):
                mod_block(half, half)
                for k in range(half * HP, half * HP + HP):
                    pe.wait_ge(sq_ready, k + 1)
                    pe.matmul(p_in[:, 0, :], b.ones[:], sq[:, k % 2, :], start=k == 0, stop=k == KT - 1
                              ).then_inc(sq_used, 1)
            with pe.Fori(2, MOD_FIRST, 2) as m:
                mod_block(m, 0)
                mod_block(m + 1, 1)
            pe.wait_ge(mload_in, 64)
            for row in range(2):
                for part in range(5):
                    mm = pe.matmul(p_lo[:, 0, row * 32:row * 32 + 32], mload[:, row, part, :],
                                   ident[0:32, 0:32], start=part == 0, stop=part == 4)
            mm.then_inc(mcol_ready, 1)

            def tile(slot, full, bank, first=False, after=lambda quarter: None, cols=slice(0, T2)):
                pe.wait_ge(w_full[slot], full)
                for k in range(KT):
                    if first:
                        pe.wait_ge(h_ctx, k + 1)
                        pe.wait_ge(h_lat, k + 1)
                    mm = pe.matmul(p_in[:, bank, 0:cols.stop - cols.start],
                                   wring[:, slot, k * P:(k + 1) * P], hT[:, k, cols],
                                   start=k == 0, stop=k == KT - 1)
                    if k == KT - 1:
                        mm.then_inc(in_ready, 1)
                    if k % 4 == 3:
                        after(k // 4)

            tile(0, 16, 0, first=True)
            tile(1, 16, 1)

            def low_rank(hp, kind):
                n = 6
                if kind == 0:
                    pe.wait_ge(lw_in, hp * 16 + 16)
                    pe.wait_ge(lora_ready, 2)
                if kind < 2:
                    rows = slice(kind * C, kind * C + C)
                    for dr in range(2):
                        wait(pe, z_used, hp * n + (2 * kind + dr - 1))
                        pe.matmul(p_lo[:, dr, :], lw[rows, dr, :], lora[rows, 0, :], start=True, stop=True
                                  ).then_inc(z_ready, 1)
                elif kind == 2:
                    pe.wait_ge(z_used, hp * n + 3)
                    pe.wait_ge(kks_ready, hp + 1)
                    pe.matmul(p_lo[:, 0, :], blk[:], sq[:, 0, :], start=True, stop=True).then_inc(z_ready, 1)
                else:
                    pe.wait_ge(z_used, hp * n + 4)
                    pe.matmul(p_lo[:, 1, 0:T], lw[:, 2, :], lora[:, 1, T:T2], start=True, stop=True
                              ).then_inc(z_ready, 1)

            def chunk_matrices(hp, between=lambda step: None):
                def flip(dr):
                    pe.wait_ge(kbp_ready, hp * 2 + (dr + 1))
                    for c in range(NCH):
                        mm = pe.transpose(p_g[:, c // 4, (c % 4) * P:(c % 4 + 1) * P], kbp[:, dr, c, :], ident[:])
                    mm.then_inc(t_ready, 1)

                def products(dr, lat):
                    ar = rec[:, dr * DIR_LEN + G_LEN + BK_LEN:dr * DIR_LEN + DIR_LEN - NCH]
                    ar = ar.rearrange("p (c n) -> p c n", n=2 * C)
                    n = 2 * C if lat else C
                    for c in range(4):
                        for head in range(2):
                            rows = slice(head * C, head * C + C)
                            mm = pe.matmul(p_g[:, head, c * n:(c + 1) * n], kb[rows, dr, 4 * lat + c, :],
                                           ar[rows, 4 * lat + c, 0:n], start=True, stop=True)
                    mm.then_inc(g_ready, 1)

                wait(pe, g_evac, hp * 5)
                wait(pe, t_evac, hp * 3)
                for dr in range(2):
                    if dr:
                        pe.wait_ge(g_evac, hp * 5 + 2)
                    flip(dr)
                    between(3 * dr)
                    pe.wait_ge(t_evac, hp * 3 + (dr + 1))
                    products(dr, 0)
                    between(3 * dr + 1)
                    pe.wait_ge(g_evac, hp * 5 + (2 * dr + 1))
                    products(dr, 1)
                    between(3 * dr + 2)
                pe.wait_ge(g_evac, hp * 5 + 4)
                for i in range(4):
                    mm = pe.transpose(p_g[:, 0, i * P:(i + 1) * P], rkv[:, 2, i * P:(i + 1) * P], ident[:])
                mm.then_inc(t_ready, 1)
                pe.wait_ge(rkb_ready, hp + 1)
                pe.matmul(p_g[:, 1, 0:T], blk[:], rkb[:], start=True, stop=True).then_inc(g_ready, 1)

            def pair(hp, first=False, mods=True):
                m = hp * 4 + MOD_FIRST

                def modulate(block, qs):
                    if mods:
                        mod_slots(m + block, block % 2, qs)

                def in_k(quarter):
                    modulate(1, [quarter])
                    if quarter == 2:
                        low_rank(hp, 0)
                    elif quarter == 3:
                        low_rank(hp, 1)

                def in_chunks(step):
                    if step in (0, 1, 3, 4):
                        modulate(2, [step - step // 3])
                    elif step == 5:
                        low_rank(hp, 2)

                pe.wait_ge(in_evac, hp * 3 + 2)
                tile(2, hp * 16 + 16, 0, after=lambda quarter: modulate(0, [quarter]))
                tile(0, hp * 16 + 32, 1, after=in_k)
                if first:
                    for step in range(6):
                        in_chunks(step)
                else:
                    chunk_matrices(hp - 1, in_chunks)
                pe.wait_ge(in_evac, hp * 3 + 3)
                tile(1, hp * 16 + 32, 0, after=lambda quarter: modulate(3, [quarter] if quarter < 2 else []))
                low_rank(hp, 3)
                modulate(3, (2, 3))

            pair(0, True)
            with pe.Fori(1, MOD_PAIRS) as hp:
                pair(hp)
            for hp in range(MOD_PAIRS, HP):
                pair(hp, mods=False)

            def attention_tile(n):
                t = A_TILES + n
                wait(pe, at_evac, n - 1)
                tile(t % 3, 16 * (t // 3 + 1), (n + 1) % 2, cols=slice(0, T2) if n < 4 else slice(T, T2))

            for n in range(2):
                if n == 1:
                    pe.wait_ge(in_evac, 3 * HP + 2)
                attention_tile(n)
            chunk_matrices(HP - 1)
            for n in range(2, EARLY_TILES):
                attention_tile(n)

        @block.scalar
        def _(act):
            act.dma_start(b.cond[:], d["cond"]).then_inc(cond_in, 16)
            for g in range(4):
                kt = slice(4 * g, 4 * g + 4)
                act.dma_start(hT[:, kt, 0:T], d["ctxT"][:, kt, :]).then_inc(x_in, 16)
                act.dma_start(hT[:, kt, T:T2], d["xT"][:, kt, :]).then_inc(x_in, 16)
            act.dma_start(mu[:, 0:2, :], d["mu"]).then_inc(small_in, 16)
            act.dma_start(par[:, 0:N_PAR, :], d["par"]).then_inc(small_in, 16)
            act.dma_start(b.gain[:], d["gain"]).then_inc(small_in, 16)
            act.wait_ge(cond_in, 16)
            act.wait_ge(par_ready, 1)
            act.activation(b.scol[:, :, 0:2], b.cond[:], ACT.Silu).then_inc(silu_ready, 1)
            act.wait_ge(x_in, 16 * 8)
            for k in range(KT):
                wait(act, sq_used, k - 1)
                act.activation(sq[:, k % 2, :], hT[:, k, :], ACT.Square).then_inc(sq_ready, 1)
            act.wait_ge(sq_used, KT)
            act.activation(sq[:, 0, :], p_in[:, 0, :], ACT.Sqrt, scale=1.0 / D, bias=b.eps[:, 0:1]
                           ).then_inc(rms_ready, 1)

            def mod_evacuate(m, buf):
                act.wait_ge(mod_used, m * 4 + 4)
                wait(act, mod_stored[buf], (m - buf) * 16)
                act.activation(stage[:, buf, :], p_mod[:, buf, :], ACT.Copy).then_inc(mod_evac, 1)

            mod_evacuate(0, 0)
            mod_evacuate(1, 1)
            with act.Fori(2, MOD_FIRST, 2) as m:
                mod_evacuate(m, 0)
                mod_evacuate(m + 1, 1)
            act.wait_ge(mcol_evac, 1)
            for k in range(KT):
                act.wait_ge(hr_ready, k + 1)
                act.activation(hT[:, k, 0:T], hT[:, k, 0:T], ACT.Identity, bias=shc[:, 1, k:k + 1],
                               scale=scc[:, 1, k:k + 1]).then_inc(h_ctx, 1)

            def scaled(bank, ready, mu_col, out):
                act.wait_ge(in_ready, ready)
                act.activation(out, p_in[:, bank, :], ACT.Copy, scale=mu_col).then_inc(in_scaled, 1)

            scaled(0, 1, mu[:, 2, 0:1], lora[:, 0, :])
            scaled(1, 2, mu[:, 2, 1:2], lora[:, 1, :])
            act.wait_ge(in_evac, 2)
            act.activation(lora[0:C, 0, :], lora[0:C, 0, :], ACT.Tanh).then_inc(lora_ready, 1)
            act.activation(lora[:, 1, T:T2], lora[:, 1, T:T2], ACT.Sigmoid).then_inc(lora_ready, 1)

            def flipped(hp, dr):
                act.wait_ge(t_ready, hp * 3 + (dr + 1))
                at = dr * DIR_LEN + G_LEN
                act.activation(rec[:, at:at + NB], p_g[:, 0, :], ACT.Copy)
                act.activation(rec[:, at + NB:at + 2 * NB], p_g[:, 1, :], ACT.Copy).then_inc(t_evac, 1)

            def values_flipped(hp):
                act.wait_ge(t_ready, hp * 3 + 3)
                act.activation(rec[:, V_AT:V_AT + 4 * P], p_g[:, 0, :], ACT.Copy).then_inc(t_evac, 1)

            def bends(hp, kind, out):
                for dr in range(2):
                    act.wait_ge(z_ready, hp * 6 + (2 * kind + dr + 1))
                    at = 3 + 2 * kind + dr
                    act.activation(out[:, dr, :], p_lo[:, dr, :], ACT.Tanh, scale=0.5, bias=cur[:, at:at + 1]
                                   ).then_inc(z_used, 1)

            def exponentials(hp, dr):
                act.wait_ge(cum_ready, hp * 2 + (dr + 1))
                wait(act, kbp_ready, hp * 2 + dr)
                act.activation(ep[:], cum[:], ACT.Exp)
                act.activation(en[:], cum[:], ACT.Exp, scale=-1.0)
                act.wait_ge(x_ready, hp * 2 + (dr + 1))
                act.activation(ex[:], ex[:], ACT.Exp).then_inc(e_ready, 1)

            def pair(hp, first=False, mods=True):
                def modulated(block):
                    if mods:
                        mod_evacuate(hp * 4 + (MOD_FIRST + block), block % 2)

                modulated(0)
                act.wait_ge(cur_ready, hp + 1)
                if not first:
                    act.wait_ge(rkb_ready, hp)
                scaled(0, hp * 3 + 3, cur[:, 0:1], rkv[:, 0, :])
                bends(hp, 0, tw)
                scaled(1, hp * 3 + 4, cur[:, 1:2], rkv[:, 1, :])
                modulated(1)
                bends(hp, 1, ta)
                act.wait_ge(in_evac, hp * 3 + 4)
                kcol = cur[:, 7:8]
                act.activation(kkr[:], rkv[:, 1, :], ACT.Copy, scale=kcol)
                wait(act, z_ready, hp * 6)
                act.activation(sq[:, 0, :], rkv[:, 1, :], ACT.Square, scale=kcol).then_inc(kks_ready, 1)
                if not first:
                    flipped(hp - 1, 0)
                    flipped(hp - 1, 1)
                modulated(2)
                if not first:
                    values_flipped(hp - 1)
                act.wait_ge(z_ready, hp * 6 + 5)
                act.activation(ex[:], p_lo[:, 0, :], ACT.Sqrt, bias=b.eps[:, 1:2]).then_inc(z_used, 1)
                if not first:
                    act.wait_ge(pair_read, hp)
                scaled(0, hp * 3 + 5, cur[:, 2:3], rkv[:, 2, :])
                modulated(3)
                exponentials(hp, 0)
                act.wait_ge(z_ready, hp * 6 + 6)
                if not first:
                    act.wait_ge(rec_stored, hp * 16)
                act.activation(rec[:, GATE_AT:GATE_AT + T], p_lo[:, 1, 0:T], ACT.Copy).then_inc(z_used, 1)
                exponentials(hp, 1)

            pair(0, True)
            with act.Fori(1, MOD_PAIRS) as hp:
                pair(hp)
            for hp in range(MOD_PAIRS, HP):
                pair(hp, mods=False)

            def attention_evacuate(n):
                act.wait_ge(in_ready, A_TILES + n + 1)
                b.attention_tile_out(act, n, p_in[:, (n + 1) % 2, :]).then_inc(at_evac, 1)

            for n in range(2):
                attention_evacuate(n)
            flipped(HP - 1, 0)
            flipped(HP - 1, 1)
            values_flipped(HP - 1)
            for n in range(2, EARLY_TILES):
                attention_evacuate(n)

        @block.vector
        def _(dve):
            own = Count(dve, own_dve)

            def link(ins):
                own.inc(ins)
                own.wait()

            link(dve.memset(b.scol[:], 0.0))
            dve.sem_inc(par_ready, 1)
            dve.wait_ge(small_in, 48)
            link(dve.tensor_tensor(mu[:, 2, :], mu[:, 0, :], mu[:, 1, :], ALU.add))
            link(dve.tensor_scalar(mu[:, 2, :], mu[:, 2, :], -1.0, 1.0, ALU.mult, ALU.add))
            link(dve.tensor_scalar(par[:, N_PAR:N_PAR + 4, :], par[:, 0:4, :], 0.5, None, ALU.mult))
            link(dve.tensor_scalar(par[:, N_PAR + 4, :], par[:, K_A, :], 0.5, None, ALU.mult))
            link(dve.tensor_scalar(par[:, N_PAR + 5, :], par[:, K_A, :], -0.5, 1.0, ALU.mult, ALU.add))
            dve.wait_ge(rms_ready, 1)
            dve.reciprocal(sq[:, 1, :], sq[:, 0, :]).then_inc(rstd_ready, 1)
            dve.wait_ge(rstd_ready, 1)
            for k in range(KT):
                dve.tensor_tensor(hT[:, k, :], hT[:, k, :], sq[:, 1, :], ALU.mult).then_inc(hr_ready, 1)
            dve.wait_ge(mcol_ready, 1)
            mod = p_lo[:, 0, 0:64].rearrange("p (r n) -> p r n", n=32)
            dve.tensor_copy(shc[:], mod[:, :, 0:KT])
            for row in range(2):
                own.inc(dve.scalar_tensor_tensor(scc[:, row, :], mod[:, row, KT:2 * KT], 1.0, b.gain[:, 0, :],
                                                 ALU.add, ALU.mult))
            own.wait()
            dve.sem_inc(mcol_evac, 1)
            dve.wait_ge(hr_ready, KT)
            for k in range(KT):
                dve.tensor_scalar(hT[:, k, T:T2], hT[:, k, T:T2], scc[:, 0, k:k + 1], shc[:, 0, k:k + 1],
                                  ALU.mult, ALU.add).then_inc(h_lat, 1)

            def shift(bank, scaled, prev, nxt, out):
                dve.wait_ge(in_scaled, scaled)
                o = out.rearrange("p (s t) -> p s t", t=T)
                p = p_in[:, bank, :].rearrange("p (s t) -> p s t", t=T)
                link(dve.scalar_tensor_tensor(o[:, :, 1:T], p[:, :, 0:T - 1], prev, o[:, :, 1:T],
                                              ALU.mult, ALU.add))
                dve.scalar_tensor_tensor(o[:, :, 0:T - 1], p[:, :, 1:T], nxt, o[:, :, 0:T - 1],
                                         ALU.mult, ALU.add).then_inc(in_evac, 1)

            for j in range(2):
                shift(j, j + 1, mu[:, 0, j:j + 1], mu[:, 1, j:j + 1], lora[:, j, :])

            def tail(hp):
                for dr in range(2):
                    for lat in range(2):
                        dve.wait_ge(g_ready, hp * 5 + (2 * dr + lat + 1))
                        for head in range(2):
                            base, n = g_at(head, 4 * lat)
                            out = rec[:, dr * DIR_LEN + base:dr * DIR_LEN + base + 4 * n]
                            m = mask[:, dr:dr + 1, 0:n].broadcast_to([P, 4, n])
                            ins = dve.tensor_tensor(out.rearrange("p (c n) -> p c n", n=n),
                                                    p_g[:, head, 0:4 * n].rearrange("p (c n) -> p c n", n=n),
                                                    m, ALU.mult)
                        ins.then_inc(g_evac, 1)
                dve.wait_ge(g_ready, hp * 5 + 5)
                ins = dve.tensor_tensor(rec[:, BONUS_AT:BONUS_AT + T], p_g[:, 1, 0:T], rkv[:, 2, T:T2], ALU.mult)
                own.inc(ins)
                own.wait()
                dve.sem_inc(g_evac, 1)
                dve.sem_inc(pair_read, 1)

            def pair(hp, first=False):
                dve.tensor_copy(cur[:, 0:3], mu[:, 2, bass.ds(hp * 3 + 2, 3)])
                dve.tensor_copy(cur[:, 3:7], par[:, N_PAR:N_PAR + 4, bass.ds(hp, 1)].rearrange("p n o -> p (n o)"))
                dve.tensor_copy(cur[:, 7:8], par[:, K_K, bass.ds(hp, 1)]).then_inc(cur_ready, 1)

                def shifted(j):
                    cols = bass.ds(hp * 3 + (2 + j), 1)
                    shift([0, 1, 0][j], hp * 3 + (3 + j), mu[:, 0, cols], mu[:, 1, cols], rkv[:, j, :])

                shifted(0)
                shifted(1)
                if not first:
                    tail(hp - 1)
                dve.wait_ge(in_evac, hp * 3 + 4)
                r, k = rkv[:, 0, :], rkv[:, 1, :]
                for dr in range(2):
                    dve.wait_ge(z_used, hp * 6 + (dr + 3))
                    own.inc(dve.tensor_scalar(tw[:, dr, :], tw[:, dr, :], -DECAY / 2, -DECAY / 2, ALU.mult, ALU.add))
                    own.inc(dve.tensor_scalar(kd[:, dr, :], ta[:, dr, :], par[:, N_PAR + 4, bass.ds(hp, 1)],
                                              par[:, N_PAR + 5, bass.ds(hp, 1)], ALU.mult, ALU.add))
                    own.wait()
                    own.inc(dve.tensor_tensor(kd[:, dr, :], kd[:, dr, :], k, ALU.mult))
                    own.inc(dve.tensor_scalar(ta[:, dr, :], ta[:, dr, :], 0.5, 0.5, ALU.mult, ALU.add))
                dve.wait_ge(z_used, hp * 6 + 5)
                link(dve.reciprocal(ex[:], ex[:]))
                link(dve.tensor_tensor(kk[:], kkr[:], ex[:], ALU.mult))
                shifted(2)
                dve.wait_ge(in_evac, hp * 3 + 5)
                for dr in range(2):
                    fwd = slice(None) if dr == 0 else slice(None, None, -1)
                    if dr:
                        dve.wait_ge(e_ready, hp * 2 + 1)
                    own.inc(dve.tensor_tensor_scan(cum[:, fwd], restart[:], tw[:, dr, fwd], 0.0, ALU.mult, ALU.add))
                    own.wait()
                    dve.sem_inc(cum_ready, 1)
                    own.inc(dve.tensor_tensor(ex[:], cum[:], tw[:, dr, :], ALU.subtract))
                    own.wait()
                    dve.sem_inc(x_ready, 1)
                    link(dve.tensor_tensor(ta[:, dr, :], kk[:], ta[:, dr, :], ALU.mult))
                    dve.wait_ge(e_ready, hp * 2 + (dr + 1))
                    wait(dve, t_ready, hp * 3)
                    quads = kb[:, dr].rearrange("p (c e) (h t) -> p c (e h) t", e=2, h=2)
                    en4 = en[:].rearrange("p (c e t) -> p c e t", e=2, t=C)
                    kd4 = kd[:, dr, :].rearrange("p (c e t) -> p c e t", e=2, t=C)
                    b4 = ta[:, dr, :].rearrange("p (c e t) -> p c e t", e=2, t=C)
                    own.inc(dve.tensor_tensor(quads[:, :, 0:4:3, :], kd4, en4, ALU.mult))
                    own.inc(dve.tensor_tensor(quads[:, :, 1:3, :], b4, en4, ALU.mult))
                    if dr == 0 and not first:
                        dve.wait_ge(rec_stored, hp * 16)
                        dve.wait_ge(tri_stored, hp * 256)
                    ar = rec[:, dr * DIR_LEN + G_LEN + BK_LEN:dr * DIR_LEN + DIR_LEN - NCH]
                    ar = ar.rearrange("p (c n) -> p c n", n=2 * C)
                    own.inc(dve.scalar_tensor_tensor(ar[:, :, 0:C], chunks(kk[:]), -1.0, chunks(ex[:]),
                                                     ALU.mult, ALU.mult))
                    for cs in (slice(0, 4), slice(4, 8)):
                        own.inc(dve.tensor_tensor(ar[:, cs, C:2 * C], chunks(r)[:, cs, :], chunks(ep[:])[:, cs, :],
                                                  ALU.mult))
                    own.wait()
                    dve.sem_inc(kb_ready, 1)
                link(dve.tensor_tensor(rkb[:], kd[:, 0, T:T2], kd[:, 1, T:T2], ALU.add))
                own.inc(dve.scalar_tensor_tensor(rkb[:], rkb[:], par[:, R_K, bass.ds(hp, 1)], r[:, T:T2],
                                                 ALU.mult, ALU.mult))
                own.wait()
                dve.sem_inc(rkb_ready, 1)

            before = own.n
            pair(0, True)
            k_first = own.n - before
            with dve.Fori(1, HP) as hp:
                own.loop(hp, k_first + 1, 1)
                pair(hp)
            own.end(HP - 1)
            tail(HP - 1)
    st.close()
    b.end_stage()


def build_attend(b):
    nc, d = b.nc, b.d
    st = ExitStack()
    S = b.stage_sem
    ident, hT, mring, stage = b.ident, b.hT, b.mring, b.stage
    mixT = b.mixT
    wring, kv, w_full = b.wring, b.kv, b.w_full
    q = b.q = b.sb("q", [P, NH, T], st)
    qsq = b.qsq = b.sb("qsq", [P, NH, T], st)
    rsq = b.sb("rsq", [P, 2, T2], st)
    rope = b.sb("rope", [P, 2, T], st)
    rot = b.sb("rot", [P, P], st)
    hgain = b.sb("hgain", [P, 2], st)
    part = b.sb("rope_part", [P, 2, T], st)
    vt = b.sb("vt", [P, 2, 4, P], st)
    prob = b.sb("prob", [P, 2, T2], st)
    probT = b.sb("probT", [P, 2, 4, T], st)
    smax = b.sb("smax", [P, 16], st)
    ssum = b.sb("ssum", [P, 16], st)
    tri = [b.sb(f"tri{dr}", [P, C, C], st) for dr in range(2)]
    outer = [b.sb(f"outer{dr}", [P, C * C // 4], st) for dr in range(2)]
    p_in = b.ps("p_in_at", [P, 2, NB], st)
    p_mod = b.ps("p_mod_at", [P, 2, NB], st)
    p_pt = b.ps("p_pt", [P, 2, NB], st)
    p_b = b.ps("p_b", [P, 2, NB], st)

    small_in = S("at_small_in")
    tile_ready, tile_evac = S("at_tile_ready"), S("at_tile_evac")
    mod_full, mod_used, mod_evac = b.mod_full, b.mod_used, b.mod_evac
    mod_stored = [S(f"at_mod_stored{i}") for i in range(2)]
    ssq_ready, rms_ready, normed = S("at_ssq_ready"), S("at_rms_ready"), S("at_normed")
    rot_ready, roped = S("rot_ready"), S("roped")
    vt_ready, vt_evac = S("vt_ready"), S("vt_evac")
    sc_ready, max_ready, exp_ready, prob_ready = (
        S("scores_ready"), S("max_ready"), S("exp_ready"), S("prob_ready"))
    pt_ready, pt_evac, av_ready, av_evac = S("pt_ready"), S("pt_evac"), S("av_ready"), S("av_evac")
    tri_in, inv_fwd, inv_bwd, inv_stored = S("tri_in"), S("inv_fwd"), S("inv_bwd"), S("inv_stored")
    own_dve = S("own_dve_at")
    FIRST = MOD_FIRST + 4 * MOD_PAIRS
    LEFT = 2 * MOD_BLOCKS - FIRST
    WITH_TILES = 12 - EARLY_TILES
    assert LEFT == WITH_TILES + 4
    SCALE = float(HD) ** -0.5

    def invert(eng, dr, sem):
        y = tri[dr]
        n = 0
        for s in range(1, C - 1):
            s = s if dr == 0 else C - 1 - s
            js = slice(0, s) if dr == 0 else slice(s + 1, C)
            ts = slice(s + 1, C) if dr == 0 else slice(0, s)
            nj, nt = js.stop - js.start, ts.stop - ts.start
            o = outer[dr][:, 0:nj * nt].rearrange("p (j t) -> p j t", t=nt)
            eng.tensor_tensor(o, y[:, js, s:s + 1].broadcast_to([P, nj, nt]),
                              y[:, s:s + 1, ts].broadcast_to([P, nj, nt]), ALU.mult).then_inc(sem, 1)
            eng.wait_ge(sem, n + 1)
            eng.tensor_tensor(y[:, js, ts], y[:, js, ts], o, ALU.add).then_inc(sem, 1)
            eng.wait_ge(sem, n + 2)
            n += 2
        eng.memset(y[:].rearrange("p s t -> p (s t)")[:, 0:C * C:C + 1], 1.0).then_inc(sem, 1)
        return n + 1

    INV = 2 * (C - 2) + 1

    with nc.Block() as block:
        @block.sync
        def _(sp):
            def w_load(n):
                t = A_TILES + n
                wait(sp, tile_ready, n - EARLY_TILES - 2)
                sp.dma_start(wring[:, t % 3, :], d["w_in"][t]).then_inc(w_full[t % 3], 16)

            for dr in range(2):
                sp.dma_start(tri[dr][:].rearrange("p s t -> p (s t)"),
                             d["tri"][dr].rearrange("hp h k e s t -> (hp h k e) (s t)")).then_inc(tri_in, 16)
            for n in range(LEFT):
                if n:
                    m = FIRST + n
                    for q4 in range(4):
                        sp.wait_ge(mod_used, 4 * m + q4 - 3)
                        sp.dma_start(mring[:, q4, :], d["mod_w"][m, q4]).then_inc(mod_full[q4], 16)
                if EARLY_TILES + 3 + n < 12:
                    w_load(EARLY_TILES + 3 + n)
            for dr, sem in ((0, inv_fwd), (1, inv_bwd)):
                sp.wait_ge(sem, INV)
                sp.dma_start(d["inv"][dr].rearrange("hp h k e s t -> (hp h k e) (s t)"),
                             tri[dr][:].rearrange("p s t -> p (s t)")).then_inc(inv_stored, 16)
            sp.wait_ge(inv_stored, 32)

        @block.gpsimd
        def _(pool):
            pool.dma_start(rope[:], d["rope"]).then_inc(small_in, 16)
            pool.dma_start(rot[:], d["rot"]).then_inc(small_in, 16)
            pool.dma_start(hgain[:], d["hgain"]).then_inc(small_in, 16)
            pool.wait_ge(tri_in, 32)
            y = invert(pool, 1, inv_bwd)
            assert y == INV

        @block.tensor
        def _(pe):
            def mod_slots(n, slots=range(4)):
                m = FIRST + n
                for q4 in slots:
                    if q4 == 0:
                        pe.wait_ge(mod_evac, m - 1)
                    pe.wait_ge(mod_full[q4], 16 * (m + 1))
                    for g in range(4):
                        mm = pe.matmul(p_mod[32 * g:32 * g + 32, n % 2, :], b.scol[:, 4 * q4 + g, :],
                                       mring[:, q4, g * NB:(g + 1) * NB], start=q4 == 0, stop=q4 == 3)
                    mm.then_inc(mod_used, 1)

            for n in range(EARLY_TILES, 12):
                t = A_TILES + n
                pe.wait_ge(w_full[t % 3], 16 * (t // 3 + 1))
                wait(pe, tile_evac, n - EARLY_TILES - 1)
                for k in range(KT):
                    mm = pe.matmul(p_in[:, n % 2, 0:T], wring[:, t % 3, k * P:(k + 1) * P],
                                   hT[:, k, T:T2], start=k == 0, stop=k == KT - 1)
                mm.then_inc(tile_ready, 1)
                mod_slots(n - EARLY_TILES)
                if n in (4, 5):
                    g = n - 4
                    for i in range(4):
                        mm = pe.transpose(p_b[:, g, i * P:(i + 1) * P], kv[:, 2 + g, i * P:(i + 1) * P], ident[:])
                    mm.then_inc(vt_ready, 1)
            for n in range(6):
                if n < 2:
                    pe.wait_ge(vt_evac, n + 1)
                else:
                    pe.wait_ge(rms_ready, n - 1)
                if n == 0:
                    pe.wait_ge(tile_evac, 12 - EARLY_TILES)
                rhs = qsq[:, 2 * n:2 * n + 2, :] if n < 4 else b.ksq[:, n - 4, :]
                pe.matmul(p_b[:, n % 2, :], b.ones[:], rhs, start=True, stop=True).then_inc(ssq_ready, 1)
            pe.wait_ge(small_in, 48)
            for n in range(5):
                pe.wait_ge(rms_ready, 6)
                pe.wait_ge(normed, n + 1 if n < 4 else 6)
                wait(pe, roped, n - 1)
                rhs = q[:, 2 * n:2 * n + 2, :] if n < 4 else kv[:, 0:2, T:T2]
                pe.matmul(p_b[:, n % 2, :], rot[:], rhs, start=True, stop=True).then_inc(rot_ready, 1)
            pe.wait_ge(roped, 5)

            def scores(i):
                head, qt = i // 2, i % 2
                wait(pe, exp_ready, i - 1)
                pe.matmul(p_in[:, i % 2, :], q[:, head, qt * P:(qt + 1) * P], kv[:, head // 4, :],
                          start=True, stop=True).then_inc(sc_ready, 1)

            def attended(head):
                pe.wait_ge(pt_evac, 2 * head + 2)
                wait(pe, av_evac, head - 1)
                for kc in range(4):
                    mm = pe.matmul(p_b[:, head % 2, 0:T], vt[:, head // 4, kc, :], probT[:, head % 2, kc, :],
                                   start=kc == 0, stop=kc == 3)
                mm.then_inc(av_ready, 1)

            scores(0)
            scores(1)
            for i in range(16):
                pe.wait_ge(prob_ready, i + 1)
                wait(pe, pt_evac, i - 1)
                for kc in range(4):
                    keys = slice(kc * P, kc * P + P)
                    mm = pe.transpose(p_pt[:, i % 2, keys], prob[:, i % 2, keys], ident[:])
                mm.then_inc(pt_ready, 1)
                if i + 2 < 16:
                    scores(i + 2)
                if i >= 2 and i % 2 == 0:
                    attended(i // 2 - 1)
                mod_slots(WITH_TILES + i // 4, [i % 4])
            attended(7)

        @block.scalar
        def _(act):
            def mod_out(j):
                m = FIRST + j
                act.wait_ge(mod_used, 4 * m + 4)
                wait(act, mod_stored[j % 2], 32 * (j // 2))
                act.activation(stage[:, j % 2, :], p_mod[:, j % 2, :], ACT.Copy).then_inc(mod_evac, 1)
                act.wait_ge(mod_evac, m + 1)
                for row in range(2):
                    act.dma_start(d["modp"][row, :, m * NB:(m + 1) * NB], stage[row:P:32, j % 2, :]
                                  ).then_inc(mod_stored[j % 2], 16)

            for n in range(EARLY_TILES, 12):
                act.wait_ge(tile_ready, n - EARLY_TILES + 1)
                b.attention_tile_out(act, n, p_in[:, n % 2, :]).then_inc(tile_evac, 1)
                mod_out(n - EARLY_TILES)
                if n in (5, 6):
                    g = n - 5
                    act.wait_ge(vt_ready, g + 1)
                    act.activation(vt[:, g, :, :].rearrange("p k n -> p (k n)"), p_b[:, g, :], ACT.Copy
                                   ).then_inc(vt_evac, 1)
            for n in range(6):
                act.wait_ge(ssq_ready, n + 1)
                wait(act, normed, n - 1)
                act.activation(rsq[:, n % 2, :], p_b[:, n % 2, :], ACT.Sqrt, scale=1.0 / HD, bias=b.eps[:, 0:1]
                               ).then_inc(rms_ready, 1)
            for i in range(18):
                if i < 16:
                    act.wait_ge(max_ready, i + 1)
                    wait(act, pt_ready, i - 1)
                    act.activation(prob[:, i % 2, :], p_in[:, i % 2, :], ACT.Exp, scale=SCALE, bias=smax[:, i:i + 1],
                                   accum_out=ssum[:, i:i + 1]).then_inc(exp_ready, 1)
                if i >= 3 and i % 2:
                    head = (i - 3) // 2
                    act.wait_ge(av_ready, head + 1)
                    act.activation(mixT[:, HP + head, :], p_b[:, head % 2, 0:T], ACT.Copy).then_inc(av_evac, 1)
                if i >= 2 and i % 2 == 0:
                    head = i // 2 - 1
                    for j in (i - 2, i - 1):
                        act.wait_ge(pt_ready, j + 1)
                        wait(act, av_ready, head - 1)
                        act.activation(probT[:, head % 2, :, (j % 2) * P:(j % 2 + 1) * P],
                                       p_pt[:, j % 2, :].rearrange("p (k t) -> p k t", t=P), ACT.Copy
                                       ).then_inc(pt_evac, 1)
                if i >= 4 and i % 4 == 0:
                    mod_out(WITH_TILES + i // 4 - 1)
            for q2 in range(2):
                act.wait_ge(mod_stored[q2], 16 * LEFT)

        @block.vector
        def _(dve):
            own = Count(dve, own_dve)

            def link(ins):
                own.inc(ins)
                own.wait()

            dve.wait_ge(tri_in, 32)
            invert(dve, 0, inv_fwd)
            dve.wait_ge(small_in, 48)
            for n in range(6):
                dve.wait_ge(rms_ready, n + 1)
                link(dve.reciprocal(rsq[:, n % 2, :], rsq[:, n % 2, :]))
                x = q[:, 2 * n:2 * n + 2, :].rearrange("p h t -> p (h t)") if n < 4 else kv[:, n - 4, :]
                dve.scalar_tensor_tensor(x, x, hgain[:, n // 4:n // 4 + 1], rsq[:, n % 2, :],
                                         ALU.mult, ALU.mult).then_inc(normed, 1)
            dve.wait_ge(normed, 6)
            cos = rope[:, 0:1, :].broadcast_to([P, 2, T])
            sin = rope[:, 1:2, :].broadcast_to([P, 2, T])
            for n in range(5):
                x = q[:, 2 * n:2 * n + 2, :] if n < 4 else kv[:, 0:2, T:T2]
                dve.wait_ge(rot_ready, n + 1)
                own.inc(dve.tensor_tensor(part[:], p_b[:, n % 2, :].rearrange("p (h t) -> p h t", t=T), sin, ALU.mult))
                own.inc(dve.tensor_tensor(x, x, cos, ALU.mult))
                own.wait()
                own.inc(dve.tensor_tensor(x, x, part[:], ALU.add))
                own.wait()
                dve.sem_inc(roped, 1)
            for i in range(16 + 2):
                if i >= 2:
                    j = i - 2
                    dve.wait_ge(exp_ready, j + 1)
                    link(dve.reciprocal(ssum[:, j:j + 1], ssum[:, j:j + 1]))
                    dve.tensor_scalar(prob[:, j % 2, :], prob[:, j % 2, :], ssum[:, j:j + 1], None, ALU.mult
                                      ).then_inc(prob_ready, 1)
                if i < 16:
                    dve.wait_ge(sc_ready, i + 1)
                    link(dve.tensor_reduce(smax[:, i:i + 1], p_in[:, i % 2, :], AX.X, ALU.max))
                    own.inc(dve.tensor_scalar(smax[:, i:i + 1], smax[:, i:i + 1], -SCALE, None, ALU.mult))
                    own.wait()
                    dve.sem_inc(max_ready, 1)
    st.close()
    b.end_stage()


def build_recur(b):
    nc, d = b.nc, b.d
    st = ExitStack()
    S = b.stage_sem
    y = b.y
    CUT = BONUS_AT
    rec = b.sb("rec_rc", [P, 2, 2, CUT], st)
    inv = b.sb("inv_rc", [P, 2, 2, 2, 2, 4, C], st)
    akv = b.sb("akv", [P, 2, 2, 2, 4, C], st)
    H = b.sb("state", [P, 2, 2, 2, C], st)
    W = b.sb("w_rc", [P, 2, 2, C], st)
    UV = b.sb("uv", [P, 2, 2, 2, 2 * C], st)
    p_c = [b.ps(f"p_chain{g}", [P, 2, NB], st) for g in range(2)]
    p_y = [b.ps(f"p_y{g}", [P, 2, NB], st) for g in range(2)]

    rec_in = [[S(f"rec_in{s}{g}") for g in range(2)] for s in range(2)]
    ak_ready, ak_evac = ([S(f"{n}{g}") for g in range(2)] for n in ("ak_ready", "ak_evac"))
    w_ready, w_evac = ([S(f"{n}{g}") for g in range(2)] for n in ("rc_w_ready", "rc_w_evac"))
    u_ready, u_evac = ([S(f"{n}{g}") for g in range(2)] for n in ("rc_u_ready", "rc_u_evac"))
    v_placed = [S(f"v_placed{g}") for g in range(2)]
    hy_ready = [S(f"hy_ready{g}") for g in range(2)]
    h_done = [S(f"h_done{g}") for g in range(2)]
    y_evac = [S(f"y_evac{g}") for g in range(2)]

    def chunk(i, dr):
        return i if dr == 0 else (3 - i if i < 4 else 11 - i)

    def half(c, u=True):
        return slice(C, P) if (c % 2 == 0) == u else slice(0, C)

    def g_cols(s, g, dr, head, c, lat_part):
        base = g_at(head, c)[0]
        base += dr * DIR_LEN + (C if lat_part else 0)
        return rec[:, s, g, base:base + C]

    def ar_cols(s, g, dr, c, lat_part):
        base = dr * DIR_LEN + G_LEN + BK_LEN + c * 2 * C + (C if lat_part else 0)
        return rec[:, s, g, base:base + C]

    with nc.Block() as block:
        @block.sync
        def _(sp):
            def load(n, s, g):
                hp = n * 4 + (2 * s + g)
                wait(sp, h_done[g], (n * 2 + s - 1) * 9)
                wait(sp, hy_ready[g], (n * 2 + s - 1) * 8)
                sp.dma_start(rec[:, s, g, :], d["rec"][bass.ds(hp, 1)][0][:, 0:CUT]).then_inc(rec_in[s][g], 16)
                for dr in range(2):
                    for odd in range(2):
                        rows = half(odd)
                        sp.dma_start(inv[rows, s, g, dr].rearrange("s h k t -> s (h k) t"),
                                     d["inv"][dr, bass.ds(hp, 1), :, :, odd].rearrange("o h k s t -> s (o h k) t")
                                     ).then_inc(rec_in[s][g], 16)

            for s in range(2):
                for g in range(2):
                    load(0, s, g)
            for s in range(2):
                for g in range(2):
                    sp.wait_ge(h_done[g], (s + 1) * 9)
                    load(1, s, g)

        @block.gpsimd
        def _(pool):
            def place(n, s, i, g):
                cnt = n * 16 + (8 * s + i)
                pool.wait_ge(rec_in[s][g], n * 80 + 80)
                wait(pool, hy_ready[g], cnt - 1)
                for dr in range(2):
                    c = chunk(i, dr)
                    rows = half(c, u=False)
                    v = rec[rows, s, g, V_AT + (c // 2) * P:V_AT + (c // 2 + 1) * P]
                    ins = pool.tensor_copy(UV[rows, g, i % 2, dr, :], v)
                ins.then_inc(v_placed[g], 1)

            def steps(n):
                for s in range(2):
                    for i in range(8):
                        for g in range(2):
                            place(n, s, i, g)

            for n in range(2):
                steps(n)

        @block.tensor
        def _(pe):
            def outer_values(n, s, g):
                pe.wait_ge(rec_in[s][g], n * 80 + 80)
                for dr in range(2):
                    wait(pe, y_evac[g], (n * 2 + s) * 4)
                    wait(pe, ak_evac[g], (n * 2 + s) * 2 + dr)
                    for head in range(2):
                        for k in range(4):
                            for odd in range(2):
                                c = 2 * k + odd
                                vr, ur = half(c, False), half(c)
                                mm = pe.matmul(p_y[g][ur, odd, (head * 4 + k) * C:(head * 4 + k + 1) * C],
                                               g_cols(s, g, dr, head, c, False)[vr],
                                               rec[vr, s, g, V_AT + k * P + head * C:V_AT + k * P + (head + 1) * C],
                                               start=True, stop=True)
                    mm.then_inc(ak_ready[g], 1)

            def form_w(n, s, i, g):
                pe.wait_ge(h_done[g], (n * 2 + s) * 9 + (i + 1))
                for dr in range(2):
                    c = chunk(i, dr)
                    for head in range(2):
                        rows = slice(head * C, head * C + C)
                        mm = pe.matmul(p_c[g][half(c), head, 0:C], ar_cols(s, g, dr, c, False)[rows],
                                       H[rows, g, i % 2, dr, :], start=True, stop=True)
                mm.then_inc(w_ready[g], 1)

            def form_u(n, s, i, g):
                pe.wait_ge(w_evac[g], n * 16 + (8 * s + i + 1))
                for dr in range(2):
                    c = chunk(i, dr)
                    rows = half(c)
                    for head in range(2):
                        mm = pe.matmul(p_c[g][rows, rows.start // C, head * C:(head + 1) * C],
                                       inv[rows, s, g, dr, head, c // 2, :], W[rows, g, head, :],
                                       start=True, stop=True)
                mm.then_inc(u_ready[g], 1)

            def form_state(n, s, i, g):
                pe.wait_ge(u_evac[g], n * 16 + (8 * s + i + 1))
                pe.wait_ge(v_placed[g], n * 16 + (8 * s + i + 1))
                if i > 4:
                    pe.wait_ge(y_evac[g], (n * 2 + s) * 4 + (i - 4))
                for dr in range(2):
                    c = chunk(i, dr)
                    for head in range(2):
                        rows = slice(head * C, head * C + C)
                        bk = dr * DIR_LEN + G_LEN + c * P + head * C
                        mm = pe.matmul(p_c[g][rows, 0, dr * C:(dr + 1) * C], rec[:, s, g, bk:bk + C],
                                       UV[:, g, i % 2, dr, rows], start=True, stop=True)
                if i >= 4:
                    for dr in range(2):
                        c = chunk(i, dr)
                        for head in range(2):
                            rows = slice(head * C, head * C + C)
                            out = p_y[g][rows, head, dr * C:(dr + 1) * C]
                            pe.matmul(out, UV[:, g, i % 2, dr, rows], g_cols(s, g, dr, head, c, True),
                                      start=True, stop=False)
                            mm = pe.matmul(out, H[rows, g, i % 2, dr, :], ar_cols(s, g, dr, c, True)[rows],
                                           start=False, stop=True)
                mm.then_inc(hy_ready[g], 1)

            for n in range(2):
                for s in range(2):
                    for g in range(2):
                        outer_values(n, s, g)
                    for i in range(8):
                        for f in (form_w, form_u, form_state):
                            for g in range(2):
                                f(n, s, i, g)

        @block.scalar
        def _(act):
            for n in range(2):
                for s in range(2):
                    for g in range(2):
                        for dr in range(2):
                            act.wait_ge(ak_ready[g], (n * 2 + s) * 2 + dr + 1)
                            for odd in range(2):
                                rows = half(odd)
                                ins = act.activation(akv[rows, g, dr].rearrange("p h k t -> p (h k t)"),
                                                     p_y[g][rows, odd, :], ACT.Copy)
                            ins.then_inc(ak_evac[g], 1)
                    for i in range(8):
                        for g in range(2):
                            act.wait_ge(u_ready[g], n * 16 + (8 * s + i + 1))
                            for dr in range(2):
                                rows = half(chunk(i, dr))
                                ins = act.activation(UV[rows, g, i % 2, dr, :],
                                                     p_c[g][rows, rows.start // C, 0:2 * C], ACT.Copy)
                            ins.then_inc(u_evac[g], 1)

        @block.vector
        def _(dve):
            for n in range(2):
                for s in range(2):
                    for g in range(2):
                        wait(dve, h_done[g], (n * 2 + s) * 9)
                        dve.memset(H[:, g, 0], 0.0).then_inc(h_done[g], 1)
                        dve.wait_ge(ak_evac[g], (n * 2 + s) * 2 + 2)
                    for i in range(8):
                        cnt = n * 16 + (8 * s + i)
                        for g in range(2):
                            dve.wait_ge(w_ready[g], cnt + 1)
                            for dr in range(2):
                                c = chunk(i, dr)
                                rows = half(c)
                                ins = dve.tensor_tensor(W[rows, g], p_c[g][rows, :, 0:C],
                                                        akv[rows, g, dr, :, c // 2, :], ALU.add)
                            ins.then_inc(w_evac[g], 1)
                        for g in range(2):
                            dve.wait_ge(hy_ready[g], cnt + 1)
                            dve.wait_ge(h_done[g], (n * 2 + s) * 9 + (i + 1))
                            for dr in range(2):
                                tot = dr * DIR_LEN + DIR_LEN - NCH + chunk(i, dr)
                                ins = dve.scalar_tensor_tensor(
                                    H[:, g, (i + 1) % 2, dr, :], H[:, g, i % 2, dr, :], rec[:, s, g, tot:tot + 1],
                                    p_c[g][:, 0, dr * C:(dr + 1) * C], ALU.mult, ALU.add)
                            ins.then_inc(h_done[g], 1)
                            if i >= 4:
                                hp = n * 4 + 2 * s + g
                                if i > 5:
                                    dve.wait_ge(y_evac[g], (n * 2 + s) * 4 + 2)
                                for head in range(2):
                                    rows = slice(head * C, head * C + C)
                                    cf, cb = chunk(i, 0) - 4, chunk(i, 1) - 4
                                    lo, hi = min(cf, cb), max(cf, cb)
                                    out = y[rows, hp, lo:hi + 1:hi - lo, :]
                                    new = p_y[g][rows, head, 0:2 * C].rearrange("p (d t) -> p d t", t=C)
                                    if cf > cb:
                                        new = new[:, ::-1, :]
                                    if i < 6:
                                        ins = dve.tensor_copy(out, new)
                                    else:
                                        ins = dve.tensor_tensor(out, new, out, ALU.add)
                                ins.then_inc(y_evac[g], 1)
    st.close()
    b.end_stage()


class Ring:

    def __init__(self, b, tile, full, used):
        self.tile, self.full, self.used = tile, full, used
        self.loads = self.uses = 0

    def load(self, sp, src, i=0, k=0, ahead=0):
        n = self.loads + ahead
        slot = n % SLOTS
        if isinstance(i, int):
            wait(sp, self.used, n + i * k - (SLOTS - 1))
        else:
            sp.wait_ge(self.used, i * k + (n - (SLOTS - 1)))
        sp.dma_start(self.tile[:, slot, :], src).then_inc(self.full[slot], 16)

    def use(self, pe, ahead=0, i=0, k=0):
        n = self.uses + ahead
        slot = n % SLOTS
        pe.wait_ge(self.full[slot], i * (k // SLOTS * 16) + 16 * (n // SLOTS + 1))
        return self.tile[:, slot, :]


EX_SLOTS = 12


def project(pe, b, p_o, o_evac, first=0):
    for j in range(first, KT):
        w = b.ring.use(pe, ahead=j)
        wait(pe, o_evac, j - 1)
        for k in range(KT):
            mm = pe.matmul(p_o[:, j % 2, 0:T], w[:, k * P:(k + 1) * P], b.mixT[:, k, :],
                           start=k == 0, stop=k == KT - 1)
        mm.then_inc(b.ring.used, 1)


def load_experts(sp, b, l, e, first, count, ahead, i=0, k=0):
    for r in range(count):
        q = first + r
        ex = bass.ds(e + q // EX_SLOTS, 1)
        b.ring.load(sp, b.d["experts"][l, ex, q % EX_SLOTS][0], i=i, k=k, ahead=ahead + r)


def build_mix_out(b):
    nc, d = b.nc, b.d
    st = ExitStack()
    S = b.stage_sem
    y, x, mixT, mcol, ring = b.y, b.x, b.mixT, b.mcol, b.ring
    ml = b.sb("mload2", [96, 2, 5, P], st)
    bg = b.sb("bonus_gate", [P, HP, 2, T], st)
    sd = b.sb("sd_gn", [P, HP, T], st)
    p_n = b.ps("p_n", [P, 4, NB], st)
    p_m = b.ps("p_mcol", [P, 2, NB], st)
    p_o = b.ps("p_out", [P, 2, NB], st)
    ml_in, bg_in, x_in = S("mload2_in"), S("bonus_gate_in"), S("x_again_in")
    mc_ready = S("mcol2_ready")
    mean_ready, cent, sq_ready, var_ready, sd_ready, mix_ready = (
        S("gn_mean_ready"), S("gn_centred"), S("gn_sq_ready"), S("gn_var_ready"), S("gn_sd_ready"), S("mix_ready"))
    o_evac = S("wout_evac")
    own_dve, own_pool, router_in = S("own_dve_mo"), S("own_pool_mo"), S("router_in")
    slot_i = st.enter_context(nc.sbuf_tensor("slot_i", [P, CAP], mybir.dt.int32))
    y2 = y[:].rearrange("p h c t -> p (h c t)")
    sd2 = sd[:].rearrange("p h t -> p (h t)")

    def quarter(flat, q):
        return flat[:, q * NB:(q + 1) * NB]


    with nc.Block() as block:
        @block.sync
        def _(sp):
            for l in range(LAYERS):
                sp.dma_start(ml[:, l, 0:4, :], d["modp"][0, :, l * 96 * P:(l + 1) * 96 * P]
                             .rearrange("g (j p) -> j g p", p=P)).then_inc(ml_in, 16)
                sp.dma_start(ml[:, l, 4, :], d["mod_b"][l]).then_inc(ml_in, 16)
            for ot in range(SLOTS):
                ring.load(sp, d["w_out"][ot], ahead=ot)
            sp.dma_start(x[:], d["xT"]).then_inc(x_in, 16)
            for ot in range(SLOTS, KT):
                ring.load(sp, d["w_out"][ot], ahead=ot)
            load_experts(sp, b, 0, 0, 0, SLOTS, ahead=KT)


        @block.gpsimd
        def _(pool):
            own = Count(pool, own_pool)

            def link(ins):
                own.inc(ins)
                own.wait()

            link(pool.memset(b.before[:], 1.0))
            link(pool.affine_select(out=b.before[:], in_=b.before[:], compare_op=ALU.is_ge, fill=0.0, base=-1,
                                    pattern=[[1, P]], channel_multiplier=-1))
            link(pool.memset(b.lower[:], 0.0))
            for mine in range(1, 4):
                link(pool.memset(b.lower[:, 4 * mine:4 * mine + mine], 1.0))
            link(pool.iota(slot_i[:], pattern=[[1, CAP]], base=0, channel_multiplier=0))
            link(pool.tensor_copy(b.slot_no[:], slot_i[:]))
            pool.dma_start(b.router[:], d["router_w"]).then_inc(router_in, 16)
            pool.dma_start(b.router_b[:], d["router_b"].broadcast_to([P, E])).then_inc(router_in, 16)
            pool.wait_ge(router_in, 32)

        @block.scalar
        def _(act):
            act.dma_start(bg[:].rearrange("p h two t -> p h (two t)"),
                          d["rec"][:, :, BONUS_AT:REC_LEN].rearrange("h p n -> p h n")).then_inc(bg_in, 16)
            for q in range(4):
                act.wait_ge(cent, q + 1)
                act.activation(quarter(sd2, q), quarter(y2, q), ACT.Square).then_inc(sq_ready, 1)
            for q in range(4):
                act.wait_ge(var_ready, q + 1)
                act.activation(quarter(sd2, q), p_n[:, q, :], ACT.Sqrt, scale=1.0 / C, bias=b.eps[:, 2:3]
                               ).then_inc(sd_ready, 1)

        @block.tensor
        def _(pe):
            for q in range(4):
                pe.matmul(p_n[:, q, :], b.blk[:], quarter(y2, q), start=True, stop=True).then_inc(mean_ready, 1)
            for q in range(4):
                pe.wait_ge(sq_ready, q + 1)
                pe.matmul(p_n[:, q, :], b.blk[:], quarter(sd2, q), start=True, stop=True).then_inc(var_ready, 1)
            pe.wait_ge(ml_in, 64)
            for l in range(LAYERS):
                for part in range(5):
                    mm = pe.matmul(p_m[:, l, 0:96], ml[:, l, part, :], b.ident[0:96, 0:96],
                                   start=part == 0, stop=part == 4)
            mm.then_inc(mc_ready, 1)
            early = [ring.use(pe, ahead=j) for j in range(2)]
            for j in range(2):
                for k in range(HP, KT):
                    pe.matmul(p_o[:, j, 0:T], early[j][:, k * P:(k + 1) * P], mixT[:, k, :], start=k == HP, stop=False)
            for j in range(2):
                for k in range(HP):
                    pe.wait_ge(mix_ready, k + 1)
                    mm = pe.matmul(p_o[:, j, 0:T], early[j][:, k * P:(k + 1) * P], mixT[:, k, :],
                                   start=False, stop=k == HP - 1)
                mm.then_inc(ring.used, 1)
            project(pe, b, p_o, o_evac, first=2)

        @block.vector
        def _(dve):
            own = Count(dve, own_dve)

            def link(ins):
                own.inc(ins)
                own.wait()

            for q in range(4):
                dve.wait_ge(mean_ready, q + 1)
                dve.scalar_tensor_tensor(quarter(y2, q), p_n[:, q, :], -1.0 / C, quarter(y2, q), ALU.mult, ALU.add
                                         ).then_inc(cent, 1)
            dve.wait_ge(bg_in, 16)
            dve.wait_ge(cent, 4)
            for q in range(4):
                dve.wait_ge(sd_ready, q + 1)
                link(dve.reciprocal(quarter(sd2, q), quarter(sd2, q)))
                for h in (2 * q, 2 * q + 1):
                    own.inc(dve.scalar_tensor_tensor(sd[:, h, :], sd[:, h, :], b.par[:, LN_G, h:h + 1],
                                                     y2[:, h * T:(h + 1) * T], ALU.mult, ALU.mult))
                for h in (2 * q, 2 * q + 1):
                    own.wait(1)
                    own.inc(dve.scalar_tensor_tensor(sd[:, h, :], sd[:, h, :], b.par[:, LN_B, h:h + 1],
                                                     bg[:, h, 0, :], ALU.add, ALU.add))
                for h in (2 * q, 2 * q + 1):
                    own.wait(2 * q + 1 - h)
                    dve.tensor_tensor(mixT[:, h, :], sd[:, h, :], bg[:, h, 1, :], ALU.mult).then_inc(mix_ready, 1)
            dve.wait_ge(mc_ready, 1)
            link(dve.tensor_copy(mcol[:], p_m[:, :, 0:96]))
            for l in range(LAYERS):
                own.inc(dve.scalar_tensor_tensor(mcol[:, l, 4 * KT:5 * KT], mcol[:, l, 4 * KT:5 * KT], 1.0,
                                                 b.gain[:, 2 + l, :], ALU.add, ALU.mult))
            own.inc(dve.scalar_tensor_tensor(mcol[:, 1, KT:2 * KT], mcol[:, 1, KT:2 * KT], 1.0,
                                             b.gain[:, 1, :], ALU.add, ALU.mult))
            dve.wait_ge(x_in, 16)
            base = ring.uses
            for t in range(KT):
                dve.wait_ge(ring.used, base + t + 1)
                dve.scalar_tensor_tensor(x[:, t, :], p_o[:, t % 2, 0:T], mcol[:, 0, 2 * KT + t:2 * KT + t + 1],
                                         x[:, t, :], ALU.mult, ALU.add).then_inc(o_evac, 1)
    ring.loads += KT
    ring.uses += KT
    st.close()
    b.end_stage()


class Norm:

    def __init__(self, b, name, hT, htok, p_sum, p_flip, gain, shift):
        self.b, self.hT, self.htok, self.p_sum, self.p_flip = b, hT, htok, p_sum, p_flip
        self.gain, self.shift = gain, shift
        S = lambda n: b.stage_sem(f"{name}_{n}")
        self.squared, self.summed, self.rooted = S("squared"), S("summed"), S("rooted")
        self.inverted, self.scaled = S("inverted"), S("scaled")
        self.done_act, self.done_dve = S("normed_act"), S("normed_dve")
        self.flipped, self.flip_out = S("flipped"), S("flip_out")

    def ready(self, eng, k):
        eng.wait_ge(self.done_dve if k % 2 else self.done_act, k // 2 + 1)

    def act(self, act):
        x, h = self.b.x, self.hT
        for q in range(4):
            act.activation(h[:, 4 * q:4 * q + 4, :], x[:, 4 * q:4 * q + 4, :], ACT.Square).then_inc(self.squared, 1)
        act.wait_ge(self.summed, 1)
        act.activation(self.b.rms[:], self.p_sum, ACT.Sqrt, scale=1.0 / D, bias=self.b.eps[:, 0:1]
                       ).then_inc(self.rooted, 1)
        for k in range(0, KT, 2):
            act.wait_ge(self.scaled, k // 4 + 1)
            act.activation(h[:, k, :], h[:, k, :], ACT.Identity, bias=self.shift[:, k:k + 1],
                           scale=self.gain[:, k:k + 1]).then_inc(self.done_act, 1)

    def act_flips(self, act):
        for r in range(8):
            act.wait_ge(self.flipped, r + 1)
            act.activation(self.htok[:, r % 2, (r // 2) * NB:(r // 2 + 1) * NB], self.p_flip[:, r % 2, :], ACT.Copy
                           ).then_inc(self.flip_out, 1)

    def dve(self, dve):
        x, h, rms = self.b.x, self.hT, self.b.rms
        dve.wait_ge(self.rooted, 1)
        dve.reciprocal(rms[:], rms[:]).then_inc(self.inverted, 1)
        dve.wait_ge(self.inverted, 1)
        r4 = rms[:].rearrange("p (o t) -> p o t", o=1).broadcast_to([P, 4, T])
        for q in range(4):
            dve.tensor_tensor(h[:, 4 * q:4 * q + 4, :], x[:, 4 * q:4 * q + 4, :], r4, ALU.mult).then_inc(self.scaled, 1)
        for k in range(1, KT, 2):
            dve.wait_ge(self.scaled, k // 4 + 1)
            dve.tensor_scalar(h[:, k, :], h[:, k, :], self.gain[:, k:k + 1], self.shift[:, k:k + 1],
                              ALU.mult, ALU.add).then_inc(self.done_dve, 1)

    def pe_sum(self, pe):
        for k in range(KT):
            pe.wait_ge(self.squared, k // 4 + 1)
            mm = pe.matmul(self.p_sum, self.b.ones[:], self.hT[:, k, :], start=k == 0, stop=k == KT - 1)
        mm.then_inc(self.summed, 1)

    def pe_flip(self, pe):
        for r in range(8):
            wait(pe, self.flip_out, r - 1)
            for j in range(4):
                k = 4 * (r // 2) + j
                self.ready(pe, k)
                mm = pe.transpose(self.p_flip[:, r % 2, j * P:(j + 1) * P],
                                  self.hT[:, k, (r % 2) * P:(r % 2 + 1) * P], self.b.ident[:])
            mm.then_inc(self.flipped, 1)

    def flips_out(self, eng):
        eng.wait_ge(self.flip_out, 8)


class Route:

    def __init__(self, placed, gates, over_i):
        self.placed, self.gates, self.over_i = placed, gates, over_i


def build_moe(b, l):
    nc, d = b.nc, b.d
    st = ExitStack()
    S = lambda n: b.stage_sem(f"moe{l}_{n}")
    x, mcol, ring, htok = b.x, b.mcol, b.ring, b.htok
    chosen = b.sb(f"chosen{l}", [P, 2, E], st)
    placed = b.sb(f"placed{l}", [P, 2, E], st)
    gates = b.sb(f"gates{l}", [P, 2, E], st)
    over = b.sb(f"over{l}", [P, 2, E], st)
    over_n = b.sb(f"over_n{l}", [P, 1], st)
    over_i = st.enter_context(nc.sbuf_tensor(f"over_i{l}", [P, 1], mybir.dt.int32))
    inner = ExitStack()
    hot = b.mixT[:, HP:KT, :].rearrange("p k t -> p (k t)").rearrange("p (a e n) -> p a e n", a=2, e=E)
    hotq = b.sb(f"hotq{l}", [P, 2, 4, CAP], inner)
    s = b.sb(f"score{l}", [P, 2, E], inner)
    sT = b.sb(f"score_t{l}", [E, T], inner)
    sel = b.sb(f"sel{l}", [P, 2, E], inner)
    beat = b.sb(f"beat{l}", [P, 8, 4, 4], inner)
    beat2 = b.sb(f"beat2{l}", [P, 8, 4, 4], inner)
    gsum = b.sb(f"gsum{l}", [P, 2, 4], inner)
    gwin = b.sb(f"gwin{l}", [P, 2, 4], inner)
    tot = b.sb(f"tot{l}", [P, 2], inner)
    hg = b.sb(f"hg{l}", [P, 2, KT, 4 * CAP], inner)
    hT = hg[:, 1]
    comb = b.sb(f"comb{l}", [P, 2, 2, T], inner)
    act_g = b.sb(f"act_g{l}", [P, 2, FF], inner)
    uT = b.sb(f"uT{l}", [P, 2, 4, CAP], inner)
    f = b.mixT[:, 0:HP, :].rearrange("p k t -> p (k t)")
    p_x = b.ps(f"p_x{l}", [P, 2, NB], inner)
    p_gu = b.ps(f"p_gu{l}", [P, 2, NB], inner)
    p_t = b.ps(f"p_t{l}", [P, 4, P], inner)
    p_d = b.ps(f"p_d{l}", [P, 2, NB], inner)
    norm = Norm(b, f"moe{l}", hT, htok, p_x[:, 0, 0:T], p_gu, mcol[:, l, 4 * KT:5 * KT], mcol[:, l, 3 * KT:4 * KT])
    score_turned = S("score_turned")
    logits, scored, chosen_ready, counted, hot_ready = (
        S("logits"), S("scored"), S("chosen"), S("counted"), S("hot_ready"))
    over_summed, over_counted, over_done = S("over_summed"), S("over_counted"), S("over_done")
    b.route = Route(placed, gates, over_i)
    hotq_ready, g_ready, g_evac, c_ready, c_evac = (
        S("hotq_ready"), S("gather_ready"), S("gather_evac"), S("comb_ready"), S("comb_evac"))
    silu, u_ready, t_ready, t_evac = S("silu"), S("u_ready"), S("ut_ready"), S("ut_evac")
    d_act, d_dve = S("down_evac_act"), S("down_evac_dve")
    own_dve, act_clear = S("own_dve"), S("act_clear")
    N_EX = 8
    HALVES = E // N_EX
    base_use = ring.uses

    with nc.Block() as block:
        @block.sync
        def _(sp):
            with sp.Fori(0, E // 2 - 1) as i:
                load_experts(sp, b, l, i * 2, SLOTS, 2 * EX_SLOTS, ahead=SLOTS, i=i, k=2 * EX_SLOTS)
            rest = E * EX_SLOTS - SLOTS - (E - 2) * EX_SLOTS
            load_experts(sp, b, l, E - 2, SLOTS, rest, ahead=(E - 2) * EX_SLOTS + SLOTS)
            if l == 0:
                for ot in range(SLOTS):
                    ring.load(sp, d["f_out"][ot], ahead=E * EX_SLOTS + ot)

        @block.tensor
        def _(pe):
            norm.pe_sum(pe)
            for k in range(KT):
                norm.ready(pe, k)
                mm = pe.matmul(p_x[0:E, 1, 0:T], b.router[:, k, :], hT[:, k, :], start=k == 0, stop=k == KT - 1)
            mm.then_inc(logits, 1)
            pe.wait_ge(scored, 1)
            for tt in range(2):
                mm = pe.matmul(p_t[:, 1, tt * E:(tt + 1) * E], sT[:, tt * P:(tt + 1) * P], b.ident[0:E, 0:E],
                               start=True, stop=True)
            mm.then_inc(score_turned, 1)
            norm.pe_flip(pe)
            pe.wait_ge(chosen_ready, 1)
            pe.matmul(p_t[:, 0, 0:E], b.before[:], chosen[:, 0, :], start=True, stop=True)
            pe.matmul(p_t[:, 0, E:2 * E], b.before[:], chosen[:, 1, :], start=True, stop=False)
            pe.matmul(p_t[:, 0, E:2 * E], b.ones[:], chosen[:, 0, :], start=False, stop=True).then_inc(counted, 1)
            pe.wait_ge(hot_ready, 1)
            pe.wait_ge(act_clear, 1)
            norm.flips_out(pe)

            def gather(i, quad, r0, r1):
                base = i * 18 + 9 * quad
                if r0 == 0:
                    pe.wait_ge(c_evac, i * 32 + CREDIT)
                pe.wait_ge(g_evac, base + r0 + CREDIT)
                for r in range(r0, r1):
                    if r >= r0 + 2:
                        pe.wait_ge(g_evac, base + (r - 1 + CREDIT))
                    if r < 8:
                        for j in range(2):
                            k = 2 * r + j
                            for tt in range(2):
                                mm = pe.matmul(p_x[:, r % 2, j * 4 * CAP:(j + 1) * 4 * CAP],
                                               htok[:, tt, k * P:(k + 1) * P],
                                               hot[:, tt, bass.ds(i * N_EX + 4 * quad, 4), :],
                                               start=tt == 0, stop=tt == 1)
                    else:
                        pe.wait_ge(hotq_ready, i * 2 + (quad + 1))
                        for pair in range(2):
                            for tt in range(2):
                                mm = pe.matmul(p_x[:, 0, (pair * 2 + tt) * P:(pair * 2 + tt + 1) * P],
                                               hotq[:, tt, 2 * pair:2 * pair + 2, :], b.ident[:], start=True, stop=True)
                    mm.then_inc(g_ready, 1)

            def gate_up(i, j):
                pe.wait_ge(u_ready, i * N_EX + (max(j - 1, 0) + CREDIT))
                pe.wait_ge(g_evac, i * 18 + (9 * (j // 4 + 1) + CREDIT))
                for q in range(8):
                    w = ring.use(pe, ahead=12 * j + q, i=i, k=12 * N_EX)
                    for kk in range(4):
                        k = 4 * (q // 2) + kk
                        rows = slice((q % 2) * C, (q % 2) * C + C)
                        mm = pe.matmul(p_gu[rows, j % 2, :], hg[:, j // 4, k, (j % 4) * CAP:(j % 4 + 1) * CAP],
                                       w[:, kk * NB:(kk + 1) * NB], start=q < 2 and kk == 0,
                                       stop=q >= 6 and kk == 3)
                    mm.then_inc(ring.used, 1)

            def down(i, j):
                n = i * N_EX + j
                pe.wait_ge(u_ready, n + (1 + CREDIT))
                pe.wait_ge(t_evac, n + CREDIT)
                for q in range(4):
                    mm = pe.transpose(p_t[:, q, :], act_g[:, j % 2, q * P:(q + 1) * P], b.ident[:])
                mm.then_inc(t_ready, 1)
                pe.wait_ge(t_evac, n + (1 + CREDIT))
                pe.wait_ge(d_act, n + CREDIT)
                pe.wait_ge(d_dve, n + CREDIT)
                for q in range(4):
                    w = ring.use(pe, ahead=12 * j + 8 + q, i=i, k=12 * N_EX)
                    for cb in (0, 2, 1, 3):
                        rows = slice((cb // 2) * C, (cb // 2) * C + C)
                        mm = pe.matmul(p_d[rows, cb % 2, :], uT[:, j % 2, q, :], w[:, cb * NB:(cb + 1) * NB],
                                       start=q == 0, stop=q == 3)
                    mm.then_inc(ring.used, 1)

            def combine(i, pair):
                pe.wait_ge(d_act, i * N_EX + (2 * pair + 2 + CREDIT))
                pe.wait_ge(d_dve, i * N_EX + (2 * pair + 2 + CREDIT))
                pe.wait_ge(g_evac, i * 18 + (18 + CREDIT))
                pe.wait_ge(c_evac, (i * 4 + pair) * 8 + CREDIT)
                for r in range(8):
                    if r >= 2:
                        pe.wait_ge(c_evac, (i * 4 + pair) * 8 + (r - 1 + CREDIT))
                    for jj in range(2):
                        k = 2 * r + jj
                        mm = pe.matmul(p_x[:, r % 2, jj * T:(jj + 1) * T], f[:, k * P:(k + 1) * P],
                                       comb[:, pair // 2, pair % 2, :], start=True, stop=True)
                    mm.then_inc(c_ready, 1)

            pe.sem_inc(g_ready, CREDIT)
            with pe.Fori(0, HALVES) as i:
                gather(i, 0, 0, 9)
                for j in range(N_EX):
                    gate_up(i, j)
                    if j == 0:
                        gather(i, 1, 0, 5)
                    elif j == 1:
                        gather(i, 1, 5, 9)
                    elif j % 2 == 0:
                        combine(i, j // 2 - 1)
                    down(i, j)
                combine(i, 3)
            pe.wait_ge(over_summed, 1)
            pe.matmul(p_t[:, 0, 0:1], b.ones[:], over_n[:], start=True, stop=True).then_inc(over_counted, 1)

        @block.scalar
        def _(act):
            norm.act(act)
            act.wait_ge(logits, 1)
            act.activation(sT[:], p_x[0:E, 1, 0:T], ACT.Sigmoid).then_inc(scored, 1)
            norm.act_flips(act)

            def gathered(i, quad, r0, r1):
                for r in range(r0, r1):
                    act.wait_ge(g_ready, i * 18 + (9 * quad + r + 1 + CREDIT))
                    if r < 8:
                        out = hg[:, quad, 2 * r:2 * r + 2, :].rearrange("p k n -> p (k n)")
                    else:
                        out = comb[:, quad].rearrange("p a t -> p (a t)")
                    act.activation(out, p_x[:, r % 2, :], ACT.Copy).then_inc(g_evac, 1)

            for sem in (g_evac, t_evac, d_act):
                act.sem_inc(sem, CREDIT)
            with act.Fori(0, HALVES) as i:
                gathered(i, 0, 0, 9)
                for j in range(N_EX):
                    n = i * N_EX + j
                    act.wait_ge(ring.used, (n * 12) + (base_use + 8))
                    act.activation(act_g[C:P, j % 2, :], p_gu[0:C, j % 2, :], ACT.Silu).then_inc(silu, 1)
                    if j == 0:
                        gathered(i, 1, 0, 5)
                    elif j == 1:
                        gathered(i, 1, 5, 9)
                    act.wait_ge(t_ready, n + 1)
                    act.activation(uT[:, j % 2], p_t[:, :, C:P], ACT.Copy).then_inc(t_evac, 1)
                    act.wait_ge(ring.used, (n * 12) + (base_use + 12))
                    rows = slice((j % 2) * C, (j % 2) * C + C)
                    act.activation(f[rows, 0:D // 2].rearrange("p (b n) -> p b n", n=NB), p_d[0:C, :, :], ACT.Copy
                                   ).then_inc(d_act, 1)

        @block.gpsimd
        def _(pool):
            pool.memset(act_g[0:C], 0.0).then_inc(act_clear, 1)
            pool.wait_ge(hot_ready, 1)

            def gated(i, quad):
                e4 = bass.ds(i * N_EX + 4 * quad, 4)
                pool.wait_ge(g_ready, i * 18 + (9 * quad + CREDIT))
                for tt in range(2):
                    g = gates[:, tt, e4].rearrange("p (e o) -> p e o", o=1).broadcast_to([P, 4, CAP])
                    ins = pool.tensor_tensor(hotq[:, tt], hot[:, tt, e4, :], g, ALU.mult)
                ins.then_inc(hotq_ready, 1)

            with pool.Fori(0, HALVES) as i:
                gated(i, 0)
                gated(i, 1)

        @block.vector
        def _(dve):
            own = Count(dve, own_dve)

            def link(ins):
                own.inc(ins)
                own.wait()

            norm.dve(dve)
            dve.wait_ge(score_turned, 1)
            link(dve.tensor_copy(s[:], p_t[:, 1, 0:2 * E].rearrange("p (a e) -> p a e", e=E)))
            rb = b.router_b[:].rearrange("p (o e) -> p o e", o=1).broadcast_to([P, 2, E])
            link(dve.tensor_tensor(sel[:], s[:], rb, ALU.add))
            low = b.lower[:].rearrange("p (o a c) -> p o a c", o=1, a=4)

            def ranks(values, n):
                v = values.rearrange("p (g e) -> p g e", e=4)
                mine = v.rearrange("p g (e o) -> p g e o", o=1).broadcast_to([P, n, 4, 4])
                other = v.rearrange("p g (o e) -> p g o e", o=1).broadcast_to([P, n, 4, 4])
                own.inc(dve.tensor_tensor(beat[:, 0:n], other, mine, ALU.is_ge))
                own.inc(dve.tensor_tensor(beat2[:, 0:n], other, mine, ALU.is_gt))
                own.wait()
                link(dve.tensor_tensor(beat[:, 0:n], beat[:, 0:n], low.broadcast_to([P, n, 4, 4]), ALU.mult))
                link(dve.tensor_tensor(beat[:, 0:n], beat[:, 0:n], beat2[:, 0:n], ALU.max))

            flat = lambda t: t.rearrange("p a e -> p (a e)")
            ranks(flat(sel[:]), 8)
            link(dve.tensor_reduce(flat(chosen[:]).rearrange("p (g e) -> p g e", e=4), beat[:], AX.X, ALU.add))
            link(dve.tensor_scalar(chosen[:], chosen[:], 2.0, None, ALU.is_lt))
            link(dve.tensor_tensor(placed[:], chosen[:], sel[:], ALU.mult))
            link(dve.tensor_reduce(flat(gsum[:]), flat(placed[:]).rearrange("p (g e) -> p g e", e=4), AX.X, ALU.add))
            ranks(flat(gsum[:]), 2)
            link(dve.tensor_reduce(gwin[:], beat[:, 0:2], AX.X, ALU.add))
            link(dve.tensor_scalar(gwin[:], gwin[:], 1.0, None, ALU.is_lt))
            c4 = flat(chosen[:]).rearrange("p (g e) -> p g e", e=4)
            won = flat(gwin[:]).rearrange("p (g o) -> p g o", o=1).broadcast_to([P, 8, 4])
            own.inc(dve.tensor_tensor(c4, c4, won, ALU.mult))
            own.wait()
            dve.sem_inc(chosen_ready, 1)
            link(dve.tensor_tensor(gates[:], s[:], chosen[:], ALU.mult))
            link(dve.tensor_reduce(tot[:], gates[:], AX.X, ALU.add))
            link(dve.reciprocal(tot[:], tot[:]))
            inv_tot = tot[:].rearrange("p (a o) -> p a o", o=1).broadcast_to([P, 2, E])
            link(dve.tensor_tensor(gates[:], gates[:], inv_tot, ALU.mult))
            dve.wait_ge(counted, 1)
            link(dve.scalar_tensor_tensor(flat(placed[:]), p_t[:, 0, 0:2 * E], 1.0, flat(chosen[:]), ALU.add, ALU.mult))
            link(dve.tensor_scalar(placed[:], placed[:], -1.0, None, ALU.add))
            iota = b.slot_no[:].rearrange("p (o n) -> p o n", o=1).broadcast_to([P, 2 * E, CAP])
            at = flat(placed[:]).rearrange("p (n o) -> p n o", o=1).broadcast_to([P, 2 * E, CAP])
            dve.tensor_tensor(hot[:].rearrange("p a e n -> p (a e) n"), iota, at, ALU.is_equal).then_inc(hot_ready, 1)
            link(dve.tensor_scalar(over[:], placed[:], float(CAP), None, ALU.is_ge))
            dve.tensor_reduce(over_n[:], flat(over[:]), AX.X, ALU.add).then_inc(over_summed, 1)

            def combined(i, pair):
                for r in range(8):
                    dve.wait_ge(c_ready, (i * 4 + pair) * 8 + (r + 1))
                    for jj in range(2):
                        k = 2 * r + jj
                        ins = dve.scalar_tensor_tensor(x[:, k, :], p_x[:, r % 2, jj * T:(jj + 1) * T],
                                                       mcol[:, l, 5 * KT + k:5 * KT + k + 1], x[:, k, :],
                                                       ALU.mult, ALU.add)
                    ins.then_inc(c_evac, 1)

            for sem in (u_ready, c_evac, d_dve):
                dve.sem_inc(sem, CREDIT)
            with dve.Fori(0, HALVES) as i:
                for j in range(N_EX):
                    n = i * N_EX + j
                    dve.wait_ge(silu, n + 1)
                    dve.tensor_tensor(act_g[C:P, j % 2, :], act_g[C:P, j % 2, :], p_gu[C:P, j % 2, :], ALU.mult
                                      ).then_inc(u_ready, 1)
                    if j and j % 2 == 0:
                        combined(i, j // 2 - 1)
                    dve.wait_ge(ring.used, (n * 12) + (base_use + 12))
                    rows = slice((j % 2) * C, (j % 2) * C + C)
                    dve.tensor_copy(f[rows, D // 2:D].rearrange("p (b n) -> p b n", n=NB), p_d[C:P, :, :]
                                    ).then_inc(d_dve, 1)
                combined(i, 3)
            dve.wait_ge(over_counted, 1)
            dve.tensor_copy(over_i[:], p_t[:, 0, 0:1]).then_inc(over_done, 1)
            dve.wait_ge(over_done, 1)
    ring.loads += 12 * E
    ring.uses += 12 * E
    inner.close()
    b.end_stage()
    build_moe_rest(b, l, b.route)
    st.close()


def build_moe_rest(b, l, r):
    nc, d = b.nc, b.d
    st = ExitStack()
    S = lambda n: b.stage_sem(f"rest{l}_{n}")
    x, mcol, htok = b.x, b.mcol, b.htok
    PASSES = T // CAP - 1
    RS = 4
    w = b.sb(f"rest_w{l}", [P, RS, SLOT], st)
    placed = b.sb(f"rest_placed{l}", [P, 2, E], st)
    hot = b.sb(f"rest_hot{l}", [P, 2, CAP], st)
    hotq = b.sb(f"rest_hotq{l}", [P, 2, CAP], st)
    hg = b.sb(f"rest_hg{l}", [P, KT * CAP], st)
    comb = b.sb(f"rest_comb{l}", [C, T], st)
    act_g = b.sb(f"rest_act{l}", [P, FF], st)
    uT = b.sb(f"rest_uT{l}", [P, 4, CAP], st)
    f = b.sb(f"rest_f{l}", [C, D], st)
    p_x = b.ps(f"rest_p_x{l}", [P, 2, NB], st)
    p_c = b.ps(f"rest_p_c{l}", [P, NB], st)
    p_gu = b.ps(f"rest_p_gu{l}", [P, NB], st)
    p_t = b.ps(f"rest_p_t{l}", [P, 4, P], st)
    p_d = b.ps(f"rest_p_d{l}", [P, 2, NB], st)
    w_full = [S(f"w_full{i}") for i in range(RS)]
    w_used, hot_ready, gathered, g_evac = S("w_used"), S("hot_ready"), S("gathered"), S("gather_evac")
    silu, u_ready, t_ready, t_evac = S("silu"), S("u_ready"), S("ut_ready"), S("ut_evac")
    d_act, d_dve = S("down_evac_act"), S("down_evac_dve")
    c_ready, c_evac, own_dve, act_clear = S("comb_ready"), S("comb_evac"), S("own_dve"), S("act_clear")

    def if_over(eng):
        n = eng.value_load(r.over_i[0:1, 0:1], min_val=0, max_val=2 * T)
        return eng.If(n > 0)

    with nc.Block() as block:
        @block.sync
        def _(sp):
            with if_over(sp):
                with sp.Fori(0, PASSES) as p:
                    with sp.Fori(0, E) as e:
                        for q in range(12):
                            n = (p * E + e) * 12
                            sp.wait_ge(w_used, n + (max(q - RS + 1, 0) + CREDIT))
                            sp.dma_start(w[:, q % RS, :], d["experts"][l, bass.ds(e, 1), q][0]
                                         ).then_inc(w_full[q % RS], 16)

        @block.tensor
        def _(pe):
            with if_over(pe):
                pe.sem_inc(w_used, CREDIT)
                pe.wait_ge(act_clear, 1)
                with pe.Fori(0, PASSES) as p:
                    with pe.Fori(0, E) as e:
                        n = p * E + e
                        pe.wait_ge(hot_ready, n + 1)
                        pe.wait_ge(c_evac, n * 8 + CREDIT)
                        for k in range(KT):
                            for tt in range(2):
                                mm = pe.matmul(p_x[:, k // 8, (k % 8) * CAP:(k % 8 + 1) * CAP],
                                               htok[:, tt, k * P:(k + 1) * P], hot[:, tt, :],
                                               start=tt == 0, stop=tt == 1)
                        for tt in range(2):
                            mm = pe.matmul(p_c[0:CAP, tt * P:(tt + 1) * P], hotq[:, tt, :], b.ident[:],
                                           start=True, stop=True)
                        mm.then_inc(gathered, 1)
                        pe.wait_ge(g_evac, n + 1)
                        for q in range(8):
                            pe.wait_ge(w_full[q % RS], n * (16 * 12 // RS) + 16 * (q // RS + 1))
                            for kk in range(4):
                                k = 4 * (q // 2) + kk
                                rows = slice((q % 2) * C, (q % 2) * C + C)
                                mm = pe.matmul(p_gu[rows, :], hg[:, k * CAP:(k + 1) * CAP],
                                               w[:, q % RS, kk * NB:(kk + 1) * NB], start=q < 2 and kk == 0,
                                               stop=q >= 6 and kk == 3)
                            mm.then_inc(w_used, 1)
                        pe.wait_ge(u_ready, n + 1)
                        for q in range(4):
                            mm = pe.transpose(p_t[:, q, :], act_g[:, q * P:(q + 1) * P], b.ident[:])
                        mm.then_inc(t_ready, 1)
                        pe.wait_ge(t_evac, n + 1)
                        for q in range(4):
                            pe.wait_ge(w_full[q % RS], n * (16 * 12 // RS) + 16 * ((8 + q) // RS + 1))
                            for cb in (0, 2, 1, 3):
                                rows = slice((cb // 2) * C, (cb // 2) * C + C)
                                mm = pe.matmul(p_d[rows, cb % 2, :], uT[:, q, :], w[:, q % RS, cb * NB:(cb + 1) * NB],
                                               start=q == 0, stop=q == 3)
                            mm.then_inc(w_used, 1)
                        pe.wait_ge(d_act, n + 1)
                        pe.wait_ge(d_dve, n + 1)
                        for rd in range(8):
                            if rd >= 2:
                                pe.wait_ge(c_evac, n * 8 + (rd - 1 + CREDIT))
                            for jj in range(2):
                                k = 2 * rd + jj
                                mm = pe.matmul(p_x[:, rd % 2, jj * T:(jj + 1) * T], f[:, k * P:(k + 1) * P],
                                               comb[:], start=True, stop=True)
                            mm.then_inc(c_ready, 1)

        @block.scalar
        def _(act):
            with if_over(act):
                with act.Fori(0, PASSES) as p:
                    with act.Fori(0, E) as e:
                        n = p * E + e
                        act.wait_ge(gathered, n + 1)
                        act.activation(hg[:], p_x[:].rearrange("p b n -> p (b n)"), ACT.Copy)
                        act.activation(comb[:], p_c[0:CAP, 0:T], ACT.Copy).then_inc(g_evac, 1)
                        act.wait_ge(w_used, n * 12 + (8 + CREDIT))
                        act.activation(act_g[C:P, :], p_gu[0:C, :], ACT.Silu).then_inc(silu, 1)
                        act.wait_ge(t_ready, n + 1)
                        act.activation(uT[:], p_t[:, :, C:P], ACT.Copy).then_inc(t_evac, 1)
                        act.wait_ge(w_used, n * 12 + (12 + CREDIT))
                        act.activation(f[:, 0:D // 2].rearrange("p (b n) -> p b n", n=NB), p_d[0:C, :, :], ACT.Copy
                                       ).then_inc(d_act, 1)

        @block.gpsimd
        def _(pool):
            pool.memset(act_g[0:C], 0.0).then_inc(act_clear, 1)

        @block.vector
        def _(dve):
            with if_over(dve):
                dve.sem_inc(c_evac, CREDIT)
                dve.tensor_copy(placed[:], r.placed[:]).then_inc(own_dve, 1)
                with dve.Fori(0, PASSES) as p:
                    dve.wait_ge(own_dve, p * (1 + E) + 1)
                    dve.tensor_scalar(placed[:], placed[:], -float(CAP), None, ALU.add).then_inc(own_dve, 1)
                    with dve.Fori(0, E) as e:
                        n = p * E + e
                        own = p * (1 + E) + e + 2
                        slot = b.slot_no[:].rearrange("p (o n) -> p o n", o=1).broadcast_to([P, 2, CAP])
                        dve.wait_ge(own_dve, own)
                        dve.tensor_tensor(hot[:], slot, placed[:, :, bass.ds(e, 1)].broadcast_to([P, 2, CAP]),
                                          ALU.is_equal).then_inc(own_dve, 1)
                        dve.wait_ge(own_dve, own + 1)
                        dve.tensor_tensor(hotq[:], hot[:], r.gates[:, :, bass.ds(e, 1)].broadcast_to([P, 2, CAP]),
                                          ALU.mult).then_inc(hot_ready, 1)
                        dve.wait_ge(silu, n + 1)
                        dve.tensor_tensor(act_g[C:P, :], act_g[C:P, :], p_gu[C:P, :], ALU.mult).then_inc(u_ready, 1)
                        dve.wait_ge(w_used, n * 12 + (12 + CREDIT))
                        dve.tensor_copy(f[:, D // 2:D].rearrange("p (b n) -> p b n", n=NB), p_d[C:P, :, :]
                                        ).then_inc(d_dve, 1)
                        for rd in range(8):
                            dve.wait_ge(c_ready, n * 8 + (rd + 1))
                            for jj in range(2):
                                k = 2 * rd + jj
                                ins = dve.scalar_tensor_tensor(x[:, k, :], p_x[:, rd % 2, jj * T:(jj + 1) * T],
                                                               mcol[:, l, 5 * KT + k:5 * KT + k + 1], x[:, k, :],
                                                               ALU.mult, ALU.add)
                            ins.then_inc(c_evac, 1)
    st.close()
    b.end_stage()


def build_fourier(b):
    nc, d = b.nc, b.d
    st = ExitStack()
    S = lambda n: b.stage_sem(f"ft_{n}")
    x, mcol, ring, htok, mixT = b.x, b.mcol, b.ring, b.htok, b.mixT
    dft_t = b.sb("dft_t", [P, 2, T], st)
    dft_c = b.sb("dft_c", [P, 2, 2, T], st)
    ab = b.sb("ft_ab", [P, KT, T], st)
    COS, SIN = slice(0, T // 2 + 1), slice(T // 2 + 1, T)
    N_COS, N_SIN = T // 2 + 1, T // 2 - 1
    hT = b.sb("h_ft", [P, KT, T], st)
    p_s = b.ps("p_ft_s", [P, 2, NB], st)
    p_f = b.ps("p_ft_f", [P, 2, NB], st)
    p_q = b.ps("p_ft_q", [P, 2, NB], st)
    p_o = b.ps("p_ft_o", [P, 2, NB], st)
    norm = Norm(b, "ft", hT, htok, p_s[:, 0, 0:T], p_f, mcol[:, 1, KT:2 * KT], mcol[:, 1, 0:KT])
    dft_in, ab_ready, ab_act, ab_dve = S("dft_in"), S("ab_ready"), S("ab_evac_act"), S("ab_evac_dve")
    mix_ready, odd_ready, mix_evac, o_evac = S("mix_ready"), S("odd_ready"), S("mix_evac"), S("o_evac")
    odds = b.sb("ft_odds", [P, 2, 2, N_SIN], st)

    with nc.Block() as block:
        @block.sync
        def _(sp):
            sp.dma_start(dft_t[:], d["dft_t"]).then_inc(dft_in, 16)
            sp.dma_start(dft_c[:], d["dft_c"]).then_inc(dft_in, 16)
            for ot in range(SLOTS, KT):
                ring.load(sp, d["f_out"][ot], ahead=ot)
            load_experts(sp, b, 1, 0, 0, SLOTS, ahead=KT)

        @block.tensor
        def _(pe):
            norm.pe_sum(pe)
            norm.pe_flip(pe)
            norm.flips_out(pe)
            pe.wait_ge(dft_in, 32)
            for k in range(KT):
                wait(pe, ab_dve if k % 2 else ab_act, k // 2)
                for tt in range(2):
                    mm = pe.matmul(p_s[:, k % 2, 0:T], htok[:, tt, k * P:(k + 1) * P], dft_t[:, tt, :],
                                   start=tt == 0, stop=tt == 1)
                mm.then_inc(ab_ready, 1)
            pe.wait_ge(ab_act, 8)
            pe.wait_ge(ab_dve, 8)
            for n in range(HP):
                g, half = 2 * (n // 2), n % 2
                wait(pe, mix_evac, n - 1)
                wait(pe, odd_ready, n - 1)
                for part, bank, cols in ((0, p_f, COS), (1, p_q, SIN)):
                    size = cols.stop - cols.start
                    for kk in range(2):
                        mm = pe.matmul(bank[:, n % 2, 0:2 * size], dft_c[:, kk, part, half * P:(half + 1) * P],
                                       ab[:, 2 * g + kk:2 * g + kk + 3:2, cols], start=kk == 0, stop=kk == 1)
                mm.then_inc(mix_ready, 1)
            pe.wait_ge(mix_evac, HP)
            project(pe, b, p_o, o_evac)

        @block.scalar
        def _(act):
            norm.act(act)
            norm.act_flips(act)
            for k in range(0, KT, 2):
                act.wait_ge(ab_ready, k + 1)
                act.activation(ab[:, k, :], p_s[:, 0, 0:T], ACT.Copy).then_inc(ab_act, 1)
            for n in range(HP):
                act.wait_ge(mix_ready, n + 1)
                wait(act, mix_evac, n - 1)
                act.activation(odds[:, n % 2].rearrange("p g n -> p (g n)"), p_q[:, n % 2, 0:2 * N_SIN], ACT.Copy
                               ).then_inc(odd_ready, 1)

        @block.vector
        def _(dve):
            norm.dve(dve)
            for k in range(1, KT, 2):
                dve.wait_ge(ab_ready, k + 1)
                dve.tensor_copy(ab[:, k, :], p_s[:, 1, 0:T]).then_inc(ab_dve, 1)
            for n in range(HP):
                dve.wait_ge(mix_ready, n + 1)
                k = 4 * (n // 2) + n % 2
                even = p_f[:, n % 2, 0:2 * N_COS].rearrange("p (g n) -> p g n", g=2)[:, :, 1:T // 2]
                half = odds[:, n % 2, :, :]
                edges = p_f[:, n % 2, 0:2 * N_COS].rearrange("p (g n) -> p g n", g=2)[:, :, 0:N_COS:T // 2]
                dve.tensor_copy(mixT[:, k:k + 3:2, 0:T:T // 2], edges)
                dve.wait_ge(odd_ready, n + 1)
                dve.tensor_tensor(mixT[:, k:k + 3:2, 1:T // 2], even, half, ALU.add)
                dve.tensor_tensor(mixT[:, k:k + 3:2, T - 1:T // 2:-1], even, half, ALU.subtract).then_inc(mix_evac, 1)
            base = ring.uses
            for t in range(KT):
                dve.wait_ge(ring.used, base + t + 1)
                dve.scalar_tensor_tensor(x[:, t, :], p_o[:, t % 2, 0:T], mcol[:, 1, 2 * KT + t:2 * KT + t + 1],
                                         x[:, t, :], ALU.mult, ALU.add).then_inc(o_evac, 1)
    ring.loads += KT
    ring.uses += KT
    st.close()
    b.end_stage()

def build_finish(b):
    nc, d = b.nc, b.d
    stored = b.sem("out_stored")
    with nc.Block() as block:
        @block.sync
        def _(sp):
            sp.dma_start(d["out"], b.x[:]).then_inc(stored, 16)
            sp.wait_ge(stored, 16)


def build(nc, dram):
    b = Builder(nc, dram)
    b.ident = b.sb("ident", [P, P])
    b.ones = b.sb("ones", [P, P])
    b.blk = b.sb("blk", [P, P])
    b.eps = b.sb("eps", [P, 4])
    b.gain = b.sb("gain", [P, 4, KT])
    b.par = b.sb("par", [P, N_PAR + 6, HP])
    b.mixT = b.sb("mixT", [P, KT, T])
    early = ExitStack()
    b.cond = b.sb("cond", [P, KT, 2], early)
    b.scol = b.sb("scol", [P, KT, 32], early)
    b.mring = b.sb("mring", [P, M_RING, SLOT], early)
    b.stage = b.sb("mod_stage", [P, 2, NB], early)
    b.hT = b.sb("hT", [P, KT, T2], early)
    b.mod_full = [b.sem(f"mod_full{i}") for i in range(M_RING)]
    b.mod_used, b.mod_evac = b.sem("mod_used"), b.sem("mod_evac")
    b.mod_stored = [b.sem(f"mod_stored{i}") for i in range(2)]
    b.wring = b.sb("wring", [P, W_RING, SLOT], early)
    b.w_full = [b.sem(f"w_full{i}") for i in range(W_RING)]
    b.kv = b.sb("kv", [P, 4, T2], early)
    b.ksq = b.sb("ksq", [P, 2, T2], early)
    build_mix_in(b)
    build_attend(b)
    early.close()
    b.htok = b.sb("htok", [P, 2, D])
    b.y = b.htok[:, 0, :].rearrange("p (h c t) -> p h c t", c=4, t=C)
    build_recur(b)
    b.x = b.sb("x", [P, KT, T])
    b.mcol = b.sb("mcol", [P, LAYERS, 96])
    b.ring = Ring(b, b.sb("ring", [P, SLOTS, SLOT]), [b.sem(f"ring_full{i}") for i in range(SLOTS)],
                  b.sem("ring_used"))
    b.rms = b.sb("rms", [P, T])
    b.router = b.sb("router", [P, KT, E])
    b.router_b = b.sb("router_b", [P, E])
    b.before = b.sb("before", [P, P])
    b.lower = b.sb("lower", [P, 16])
    b.slot_no = b.sb("slot_no", [P, CAP])
    build_mix_out(b)
    build_moe(b, 0)
    build_fourier(b)
    build_moe(b, 1)
    build_finish(b)
    return b


def shape_tables():
    f32 = np.float32
    t = np.arange(T)
    inv = f32(10000.0) ** (-np.arange(0, HD // 2, 2, dtype=f32) / f32(HD // 2))
    ang = np.concatenate([(t // 64).astype(f32)[:, None] * inv, (t % 64).astype(f32)[:, None] * inv], axis=1)
    ang = np.repeat(ang, 2, axis=1).T
    rot = np.zeros((HD, HD), f32)
    even = np.arange(0, HD, 2)
    rot[even + 1, even], rot[even, even + 1] = -1.0, 1.0
    n = np.arange(T)
    turn = 2 * np.pi / T * (np.outer(n, n) % T)
    cos, sin = np.cos(turn) / 16, np.sin(turn) / 16
    dft_t = np.concatenate([cos[:, :T // 2 + 1], sin[:, 1:T // 2]], axis=1)
    dft_t = dft_t.reshape(2, P, T).transpose(1, 0, 2).astype(f32)
    dft_c = np.stack([cos, -sin], axis=1).reshape(2, P, 2, T).transpose(1, 0, 2, 3).astype(f32)
    rope = np.stack([np.cos(ang), np.sin(ang)], axis=1).astype(f32)
    return {"dft_t": dft_t, "dft_c": dft_c, "rope": rope, "rot": rot}


def host_layout(i):
    f = {}
    cols = lambda v: v.reshape(-1, P).T
    f["xT"] = i["x"][0].T.reshape(KT, P, T).transpose(1, 0, 2)
    f["ctxT"] = i["ctx"][0].T.reshape(KT, P, T).transpose(1, 0, 2)
    f["cond"] = np.stack([cols(i["c"][0]), cols(i["c_ctx"])], axis=2)
    f["mod_w"] = (i["mod_w"].reshape(2, 4, 4, P, MOD_BLOCKS, NB).transpose(0, 4, 1, 3, 2, 5)
                  .reshape(2 * MOD_BLOCKS, 4, P, SLOT))
    f["mod_b"] = i["mod_b"].reshape(2, 96, P)
    f["gain"] = np.stack([cols(i["norm_mix"][0]), cols(i["norm_mix"][1]),
                          cols(i["norm_ffn"][0]), cols(i["norm_ffn"][1])], axis=1)
    mu = np.stack([cols(i["ab_mu_prev"][0]), cols(i["ab_mu_next"][0])], axis=1)
    f["mu"] = mu[:, :, TILE_ORDER[:26]]
    w = i["ab_w_in"][0].reshape(KT, P, 38, P).transpose(2, 1, 0, 3).reshape(38, P, SLOT)
    f["w_in"] = w[TILE_ORDER]
    f["par"] = np.stack([cols(v) for v in (i["rwkv_w0"][0, 0], i["rwkv_w0"][0, 1], i["rwkv_a0"][0, 0],
                                           i["rwkv_a0"][0, 1], i["rwkv_k_k"][0], i["rwkv_k_a"][0],
                                           i["rwkv_r_k"][0].reshape(-1), i["rwkv_ln_g"][0],
                                           i["rwkv_ln_b"][0])], axis=1)
    low = np.concatenate([i["rwkv_w2"][0], i["rwkv_a2"][0]], axis=1)
    low = np.concatenate([low, i["rwkv_g2"][0][None]], axis=0)
    f["lora_w"] = low.reshape(3, P, HP, P).transpose(2, 1, 0, 3)
    f["w_out"] = i["ab_w_out"][0].reshape(KT, P, KT, P).transpose(2, 1, 0, 3).reshape(KT, P, SLOT)
    f["f_out"] = i["fourier_w_out"][0].reshape(KT, P, KT, P).transpose(2, 1, 0, 3).reshape(KT, P, SLOT)
    f["router_w"] = i["router_w"].reshape(KT, P, E).transpose(1, 0, 2)
    f["router_b"] = i["router_b"][None]
    gu = np.stack([i["exp_w_gate"], i["exp_w_up"]], axis=2).reshape(2, E, 2, 4, 4, P, FF)
    gu = gu.transpose(0, 1, 3, 2, 5, 4, 6).reshape(2, E, 8, P, SLOT)
    f["experts"] = np.concatenate([gu, i["exp_w_down"].reshape(2, E, 4, P, D)], axis=2)
    f["hgain"] = np.stack([i["attn_q_norm"][0], i["attn_k_norm"][0]], axis=1)
    f.update(shape_tables())
    return {k: np.ascontiguousarray(v) for k, v in f.items()}


SCRATCH = {
    "modp": (2, 4, 2 * MOD_BLOCKS * NB),
    "rec": (HP, P, REC_LEN),
    "tri": (2, HP, 2, NCH // 2, 2, C, C),
    "inv": (2, HP, 2, NCH // 2, 2, C, C),
}


def program(nc, arrays):
    dram = {k: nc.dram_tensor("in_" + k, a.shape, F32, kind="ExternalInput").ap() for k, a in arrays.items()}
    for k, shape in SCRATCH.items():
        dram[k] = nc.dram_tensor("scratch_" + k, shape, F32, kind="Internal").ap()
    dram["out"] = nc.dram_tensor("out", (P, KT, T), F32, kind="ExternalOutput").ap()
    build(nc, dram)


def kernel(**inputs):
    import concourse.bacc as bacc
    from concourse.bass_utils import run_bass_kernel_spmd
    nc = bacc.Bacc("TRN2", target_bir_lowering=False, num_devices=1)
    arrays = host_layout({k: np.asarray(v) for k, v in inputs.items()})
    program(nc, arrays)
    got = run_bass_kernel_spmd(nc, [{"in_" + k: a for k, a in arrays.items()}], core_ids=[0]).results[0]["out"]
    return np.ascontiguousarray(got.transpose(1, 0, 2).reshape(D, T).T[None])
```
